# Optimizing a Trainium2 kernel written in Bass

```python
import math
import jax
import jax.numpy as jnp
from jax import lax
import numpy as np

D_MODEL = 1024
BATCH = 1
SEQ = 1024
DEPTH = 2

GRID_W = 64
CTX_LEN = 256
N_MIXERS = 3
EPS = 1e-6
F32 = jnp.float32

M_EXPAND = 2
M_DI = M_EXPAND * D_MODEL
M_HEADDIM = 64
M_NH = M_DI // M_HEADDIM
M_NG = 8
M_HPG = M_NH // M_NG
M_NS = 128
M_CONV_W = 5
M_CHUNK = 128
M_CONV_CH = M_DI + 2 * M_NG * M_NS
M_IN = M_DI + M_CONV_CH + 2 * M_NH

A_HEADDIM = 64
A_NH = D_MODEL // A_HEADDIM
A_NKV = 4
A_REP = A_NH // A_NKV
A_W = A_NH * A_HEADDIM
A_KW = A_NKV * A_HEADDIM
A_IN = 2 * A_W + 2 * A_KW
A_QBLOCK = 128
ROPE_BASE = 10000.0

S_DI = D_MODEL
S_GROUP = 16
S_NG = S_DI // S_GROUP
S_P = 64

N_A = (DEPTH + N_MIXERS - 1) // N_MIXERS
N_B = (DEPTH + N_MIXERS - 2) // N_MIXERS
N_C = DEPTH // N_MIXERS


def rmsnorm(x, w):
    xf = x.astype(F32)
    y = xf * lax.rsqrt(jnp.mean(xf * xf, axis=-1, keepdims=True) + EPS)
    return (y * w.astype(F32)).astype(x.dtype)

def dwconv_centred(u, w, b):
    pad = w.shape[0] // 2
    out = lax.conv_general_dilated(u, w[:, None, :], window_strides=(1,), padding=[(pad, pad)],
                                   dimension_numbers=('NWC', 'WIO', 'NWC'),
                                   feature_group_count=u.shape[-1])
    return out + b

def ssd_scan(xs, dt, a, bm, cm, init_state, need_y=True):
    bsz, L = xs.shape[:2]
    nc = L // M_CHUNK

    def chunks(t):
        return t.astype(F32).reshape((bsz, nc, M_CHUNK) + t.shape[2:])

    xc, dtc, bc, cc = chunks(xs), chunks(dt), chunks(bm), chunks(cm)
    la_cum = jnp.cumsum(dtc * a, axis=2)
    to_end = jnp.exp(la_cum[:, :, -1:] - la_cum) * dtc
    states = jnp.einsum('bcsgn,bcsgr,bcsgrp->bcgrpn', bc, to_end, xc)
    chunk_decay = jnp.exp(la_cum[:, :, -1])

    def step(carry, inp):
        st, dec = inp
        return carry * dec[..., None, None] + st, carry

    final, prev = lax.scan(step, init_state.astype(F32),
                           (jnp.moveaxis(states, 1, 0), jnp.moveaxis(chunk_decay, 1, 0)))
    if not need_y:
        return None, final
    prev = jnp.moveaxis(prev, 0, 1)
    causal = jnp.tril(jnp.ones((M_CHUNK, M_CHUNK), dtype=bool))[:, :, None, None]
    seg = la_cum[:, :, :, None] - la_cum[:, :, None, :]
    decay = jnp.exp(jnp.where(causal, seg, -jnp.inf))
    cb = jnp.einsum('bclgn,bcsgn->bclsg', cc, bc)
    w = cb[..., None] * decay * dtc[:, :, None]
    y_diag = jnp.einsum('bclsgr,bcsgrp->bclgrp', w, xc)
    y_off = jnp.einsum('bclgn,bcgrpn,bclgr->bclgrp', cc, prev, jnp.exp(la_cum))
    return (y_diag + y_off).reshape(xs.shape), final

def mamba_mixer(h_ctx, h_lat, in_w, conv_w, conv_b, a_log, dt_bias, d_skip, norm_w, out_w, ctx_out):
    a = -jnp.exp(a_log.astype(F32)).reshape(2, M_NG, M_HPG)
    dtb = dt_bias.astype(F32).reshape(2, M_NG, M_HPG)

    def project(h):
        bsz, L, _ = h.shape
        z, xbc, dt = jnp.split(h @ in_w, [M_DI, M_DI + M_CONV_CH], axis=-1)
        xbc = jax.nn.silu(dwconv_centred(xbc, conv_w, conv_b))
        xs, bm, cm = jnp.split(xbc, [M_DI, M_DI + M_NG * M_NS], axis=-1)
        xs = xs.reshape(bsz, L, M_NG, M_HPG, M_HEADDIM)
        bm = bm.reshape(bsz, L, M_NG, M_NS)
        cm = cm.reshape(bsz, L, M_NG, M_NS)
        dt = jax.nn.softplus(dt.astype(F32).reshape(bsz, L, 2, M_NG, M_HPG) + dtb)
        return z, xs, bm, cm, dt

    zc, xc, bc, cc, dtc = project(h_ctx)
    zl, xl, bl, cl, dtl = project(h_lat)
    bsz = h_lat.shape[0]
    zero = jnp.zeros((bsz, M_NG, M_HPG, M_HEADDIM, M_NS), F32)
    rev = lambda t: jnp.flip(t, axis=1)
    yc_f, st_f = ssd_scan(xc, dtc[:, :, 0], a[0], bc, cc, zero, ctx_out)
    yl_f, _ = ssd_scan(xl, dtl[:, :, 0], a[0], bl, cl, st_f)
    yc_b, st_b = ssd_scan(rev(xc), rev(dtc[:, :, 1]), a[1], rev(bc), rev(cc), zero, ctx_out)
    yl_b, _ = ssd_scan(rev(xl), rev(dtl[:, :, 1]), a[1], rev(bl), rev(cl), st_b)
    dsk = d_skip.astype(F32).reshape(M_NG, M_HPG, 1)

    def finish(y, xs, z):
        b_, L = xs.shape[:2]
        y = (y + dsk * xs.astype(F32)).reshape(b_, L, M_DI).astype(z.dtype)
        return rmsnorm(y * jax.nn.silu(z), norm_w) @ out_w

    o_lat = finish(yl_f + rev(yl_b), xl, zl)
    o_ctx = finish(yc_f + rev(yc_b), xc, zc) if ctx_out else None
    return o_ctx, o_lat

def axial_rope_tables(L):
    rows = L // GRID_W
    r_idx, c_idx = jnp.meshgrid(jnp.arange(rows), jnp.arange(GRID_W), indexing='ij')
    r_idx = r_idx.reshape(-1).astype(F32)
    c_idx = c_idx.reshape(-1).astype(F32)
    half = A_HEADDIM // 2
    inv = ROPE_BASE ** (-jnp.arange(0, half, 2, dtype=F32) / half)
    ang = jnp.concatenate([r_idx[:, None] * inv, c_idx[:, None] * inv], axis=-1)
    return jnp.cos(ang), jnp.sin(ang)

def apply_rope(t, cos, sin):
    b_, L, h, d = t.shape
    q = d // 4
    tf = t.astype(F32).reshape(b_, L, h, 2, 2, q)
    t1, t2 = tf[..., 0, :], tf[..., 1, :]
    cs = cos.reshape(1, L, 1, 2, q)
    sn = sin.reshape(1, L, 1, 2, q)
    out = jnp.stack([t1 * cs - t2 * sn, t1 * sn + t2 * cs], axis=-2)
    return out.reshape(b_, L, h, d).astype(t.dtype)

def attend(q, k, v):
    bsz, lq = q.shape[:2]
    q = q.reshape(bsz, lq, A_NKV, A_REP, A_HEADDIM)
    s = jnp.einsum('bqgrd,bkgd->bgrqk', q, k).astype(F32) * (A_HEADDIM ** -0.5)
    p = jax.nn.softmax(s, axis=-1).astype(v.dtype)
    o = jnp.einsum('bgrqk,bkgd->bqgrd', p, v)
    return o.reshape(bsz, lq, A_W)

def attn_mixer(h_ctx, h_lat, in_w, q_norm, k_norm, out_w, ctx_out):
    def project(h):
        bsz, L, _ = h.shape
        q, k, v, g = jnp.split(h @ in_w, [A_W, A_W + A_KW, A_W + 2 * A_KW], axis=-1)
        q = rmsnorm(q.reshape(bsz, L, A_NH, A_HEADDIM), q_norm)
        k = rmsnorm(k.reshape(bsz, L, A_NKV, A_HEADDIM), k_norm)
        v = v.reshape(bsz, L, A_NKV, A_HEADDIM)
        return q, k, v, g

    qc, kc, vc, gc = project(h_ctx)
    ql, kl, vl, gl = project(h_lat)
    bsz, L = h_lat.shape[:2]
    cos, sin = axial_rope_tables(L)
    ql = apply_rope(ql, cos, sin)
    kl = apply_rope(kl, cos, sin)
    k_all = jnp.concatenate([kc, kl], axis=1)
    v_all = jnp.concatenate([vc, vl], axis=1)
    nblk = L // A_QBLOCK
    q_blocks = jnp.moveaxis(ql.reshape(bsz, nblk, A_QBLOCK, A_NH, A_HEADDIM), 1, 0)
    ol = lax.map(lambda qb: attend(qb, k_all, v_all), q_blocks)
    ol = jnp.moveaxis(ol, 0, 1).reshape(bsz, L, A_W)
    o_lat = (ol * jax.nn.silu(gl)) @ out_w
    o_ctx = (attend(qc, kc, vc) * jax.nn.silu(gc)) @ out_w if ctx_out else None
    return o_ctx, o_lat

def s5_discretize(lam_re, lam_im, log_step, b_re, b_im):
    lr, li = lam_re.astype(F32), lam_im.astype(F32)
    step = jnp.exp(log_step.astype(F32))[:, None]
    mag = jnp.exp(lr * step)
    abar_re, abar_im = mag * jnp.cos(li * step), mag * jnp.sin(li * step)
    den = lr * lr + li * li
    nr, ni = abar_re - 1.0, abar_im
    coef_re = ((nr * lr + ni * li) / den)[..., None]
    coef_im = ((ni * lr - nr * li) / den)[..., None]
    br, bi = b_re.astype(F32), b_im.astype(F32)
    return abar_re, abar_im, coef_re * br - coef_im * bi, coef_re * bi + coef_im * br

def complex_affine_combine(e1, e2):
    a1r, a1i, b1r, b1i = e1
    a2r, a2i, b2r, b2i = e2
    return (a1r * a2r - a1i * a2i, a1r * a2i + a1i * a2r,
            a2r * b1r - a2i * b1i + b2r, a2r * b1i + a2i * b1r + b2i)

def s5_scan(u, abar_re, abar_im, bbar_re, bbar_im, init_re, init_im):
    L = u.shape[1]
    bu_re = jnp.einsum('blgh,gph->lbgp', u, bbar_re)
    bu_im = jnp.einsum('blgh,gph->lbgp', u, bbar_im)
    bu_re = bu_re.at[0].add(abar_re * init_re - abar_im * init_im)
    bu_im = bu_im.at[0].add(abar_re * init_im + abar_im * init_re)
    a_re = jnp.broadcast_to(abar_re, (L, 1) + abar_re.shape)
    a_im = jnp.broadcast_to(abar_im, (L, 1) + abar_im.shape)
    _, _, x_re, x_im = lax.associative_scan(complex_affine_combine, (a_re, a_im, bu_re, bu_im), axis=0)
    return x_re, x_im

def s5_mixer(h_ctx, h_lat, in_w, lam_re, lam_im, log_step, b_re, b_im, c_re, c_im,
             d_skip, glu_w, glu_b, out_w, ctx_out):
    bsz = h_lat.shape[0]
    disc = [s5_discretize(lam_re[k], lam_im[k], log_step[k], b_re[k], b_im[k]) for k in range(2)]
    cr, ci = c_re.astype(F32), c_im.astype(F32)

    def readout(x_re, x_im, k):
        return jnp.einsum('lbgp,ghp->blgh', x_re, cr[k]) - jnp.einsum('lbgp,ghp->blgh', x_im, ci[k])

    uc, zc = jnp.split(h_ctx @ in_w, 2, axis=-1)
    ul, zl = jnp.split(h_lat @ in_w, 2, axis=-1)
    grp = lambda u: u.astype(F32).reshape(u.shape[0], u.shape[1], S_NG, S_GROUP)
    rev = lambda t: jnp.flip(t, axis=1)
    ucg, ulg = grp(uc), grp(ul)
    zero = jnp.zeros((bsz, S_NG, S_P), F32)
    xr, xi = s5_scan(ucg, *disc[0], zero, zero)
    yc = readout(xr, xi, 0) if ctx_out else None
    xr, xi = s5_scan(ulg, *disc[0], xr[-1], xi[-1])
    yl = readout(xr, xi, 0)
    xr, xi = s5_scan(rev(ucg), *disc[1], zero, zero)
    if ctx_out:
        yc = yc + rev(readout(xr, xi, 1))
    xr, xi = s5_scan(rev(ulg), *disc[1], xr[-1], xi[-1])
    yl = yl + rev(readout(xr, xi, 1))
    dsk = d_skip.astype(F32)

    def finish(y, u, z):
        b_, L = u.shape[:2]
        y = (y.reshape(b_, L, S_DI) + dsk * u.astype(F32)).astype(z.dtype)
        y = jax.nn.gelu(y)
        y = y * jax.nn.sigmoid(y @ glu_w + glu_b)
        return (y * jax.nn.silu(z)) @ out_w

    o_lat = finish(yl, ul, zl)
    o_ctx = finish(yc, uc, zc) if ctx_out else None
    return o_ctx, o_lat

def first_inputs(seed: int = 0) -> dict:
    key = jax.random.key(seed)
    ks = iter(jax.random.split(key, 48))
    nrm = lambda shape, scale: jax.random.normal(next(ks), shape, F32) * scale
    gain = lambda shape: 1.0 + nrm(shape, 0.02)
    inp = {}
    inp['x'] = nrm((BATCH, SEQ, D_MODEL), 1.0)
    inp['c'] = nrm((BATCH, D_MODEL), 1.0)
    inp['ctx'] = nrm((BATCH, CTX_LEN, D_MODEL), 1.0)
    inp['c_ctx'] = nrm((D_MODEL,), 1.0)
    inp['norm_w'] = gain((DEPTH, D_MODEL))
    inp['mod_w'] = nrm((DEPTH, D_MODEL, 3 * D_MODEL), 0.5 * D_MODEL ** -0.5)
    inp['mod_b'] = nrm((DEPTH, 3 * D_MODEL), 0.02)
    inp['final_norm_w'] = gain((D_MODEL,))
    inp['m_in_w'] = nrm((N_A, D_MODEL, M_IN), D_MODEL ** -0.5)
    inp['m_conv_w'] = nrm((N_A, M_CONV_W, M_CONV_CH), M_CONV_W ** -0.5)
    inp['m_conv_b'] = nrm((N_A, M_CONV_CH), 0.02)
    inp['m_a_log'] = jnp.log(jax.random.uniform(next(ks), (N_A, 2, M_NH), F32, 1.0, 16.0))
    dt0 = jnp.exp(jax.random.uniform(next(ks), (N_A, 2, M_NH), F32, math.log(1e-3), math.log(1e-1)))
    inp['m_dt_bias'] = dt0 + jnp.log(-jnp.expm1(-dt0))
    inp['m_d'] = 1.0 + nrm((N_A, M_NH), 0.1)
    inp['m_norm_w'] = gain((N_A, M_DI))
    inp['m_out_w'] = nrm((N_A, M_DI, D_MODEL), M_DI ** -0.5)
    inp['a_in_w'] = nrm((N_B, D_MODEL, A_IN), D_MODEL ** -0.5)
    inp['a_q_norm'] = gain((N_B, A_HEADDIM))
    inp['a_k_norm'] = gain((N_B, A_HEADDIM))
    inp['a_out_w'] = nrm((N_B, A_W, D_MODEL), A_W ** -0.5)
    inp['s_in_w'] = nrm((N_C, D_MODEL, 2 * S_DI), D_MODEL ** -0.5)
    inp['s_lambda_re'] = -0.5 + nrm((N_C, 2, S_NG, S_P), 0.01)
    inp['s_lambda_im'] = math.pi * jnp.arange(S_P, dtype=F32) + nrm((N_C, 2, S_NG, S_P), 0.01)
    inp['s_log_step'] = jax.random.uniform(next(ks), (N_C, 2, S_NG), F32, math.log(1e-3), math.log(1e-1))
    inp['s_b_re'] = nrm((N_C, 2, S_NG, S_P, S_GROUP), (2 * S_GROUP) ** -0.5)
    inp['s_b_im'] = nrm((N_C, 2, S_NG, S_P, S_GROUP), (2 * S_GROUP) ** -0.5)
    inp['s_c_re'] = nrm((N_C, 2, S_NG, S_GROUP, S_P), S_P ** -0.5)
    inp['s_c_im'] = nrm((N_C, 2, S_NG, S_GROUP, S_P), S_P ** -0.5)
    inp['s_d'] = nrm((N_C, S_DI), 1.0)
    inp['s_glu_w'] = nrm((N_C, S_DI, S_DI), S_DI ** -0.5)
    inp['s_glu_b'] = nrm((N_C, S_DI), 0.02)
    inp['s_out_w'] = nrm((N_C, S_DI, D_MODEL), S_DI ** -0.5)
    return inp

def first_block(x, c, ctx, c_ctx, norm_w, mod_w, mod_b, final_norm_w,
              m_in_w, m_conv_w, m_conv_b, m_a_log, m_dt_bias, m_d, m_norm_w, m_out_w,
              a_in_w, a_q_norm, a_k_norm, a_out_w,
              s_in_w, s_lambda_re, s_lambda_im, s_log_step, s_b_re, s_b_im, s_c_re, s_c_im,
              s_d, s_glu_w, s_glu_b, s_out_w):
    h_lat, h_ctx = x, ctx
    sc, scc = jax.nn.silu(c), jax.nn.silu(c_ctx)
    for i in range(DEPTH):
        kind, j = i % N_MIXERS, i // N_MIXERS
        ctx_out = i < DEPTH - 1
        sh, scl, gt = jnp.split(sc @ mod_w[i] + mod_b[i], 3, axis=-1)
        shc, sclc, gtc = jnp.split(scc @ mod_w[i] + mod_b[i], 3, axis=-1)
        in_lat = rmsnorm(h_lat, norm_w[i]) * (1.0 + scl[:, None]) + sh[:, None]
        in_ctx = rmsnorm(h_ctx, norm_w[i]) * (1.0 + sclc) + shc
        if kind == 0:
            o_ctx, o_lat = mamba_mixer(in_ctx, in_lat, m_in_w[j], m_conv_w[j], m_conv_b[j], m_a_log[j],
                                       m_dt_bias[j], m_d[j], m_norm_w[j], m_out_w[j], ctx_out)
        elif kind == 1:
            o_ctx, o_lat = attn_mixer(in_ctx, in_lat, a_in_w[j], a_q_norm[j], a_k_norm[j], a_out_w[j], ctx_out)
        else:
            o_ctx, o_lat = s5_mixer(in_ctx, in_lat, s_in_w[j], s_lambda_re[j], s_lambda_im[j], s_log_step[j],
                                    s_b_re[j], s_b_im[j], s_c_re[j], s_c_im[j], s_d[j], s_glu_w[j],
                                    s_glu_b[j], s_out_w[j], ctx_out)
        h_lat = h_lat + gt[:, None] * o_lat
        if ctx_out:
            h_ctx = h_ctx + gtc * o_ctx
    return rmsnorm(h_lat, final_norm_w)


DEPTH_2 = 1

MEM_LEN = 256
NORM_EPS = 1e-6

MLA_HEADS = 8
MLA_NOPE_DIM = 64
MLA_ROPE_DIM = 32
MLA_QK_DIM = MLA_NOPE_DIM + MLA_ROPE_DIM
MLA_V_DIM = 64
MLA_Q_RANK = 192
MLA_KV_RANK = 128
Q_BLOCK = 128

HG_HEADS = 4
HG_KEY_DIM = 128
HG_VAL_DIM = 128
HG_CHUNK = 64

MLA_WIDTH = MLA_HEADS * MLA_V_DIM
HG_FWIDTH = HG_HEADS * HG_KEY_DIM
HG_WIDTH = HG_HEADS * HG_VAL_DIM
MIX_WIDTH = MLA_WIDTH + HG_WIDTH
IN_SIZES = (MLA_Q_RANK, MLA_KV_RANK, MLA_ROPE_DIM, HG_FWIDTH, HG_FWIDTH, HG_FWIDTH, HG_WIDTH, HG_WIDTH)
IN_WIDTH = sum(IN_SIZES)

X_HEADS = 4
X_HEAD_DIM = D_MODEL // X_HEADS

MOE_GROUPS = 8
MOE_PER_GROUP = 8
MOE_EXPERTS = MOE_GROUPS * MOE_PER_GROUP
MOE_TOP_K = 2
MOE_HIDDEN = 256
MOE_BLOCK = 128


def rms_norm(x, w):
    xf = x.astype(jnp.float32)
    y = xf * lax.rsqrt(jnp.mean(xf * xf, axis=-1, keepdims=True) + NORM_EPS)
    return (y * w.astype(jnp.float32)).astype(x.dtype)

def split_columns(p):
    out, start = [], 0
    for size in IN_SIZES:
        out.append(p[..., start:start + size])
        start += size
    return out

def rope_tables(positions):
    half = MLA_ROPE_DIM // 2
    inv_freq = 1.0 / (ROPE_BASE ** (jnp.arange(half, dtype=jnp.float32) / half))
    ang = positions.astype(jnp.float32)[..., None] * inv_freq
    return jnp.cos(ang)[:, :, None, :], jnp.sin(ang)[:, :, None, :]

def apply_rope_2(x, cos, sin):
    x1, x2 = jnp.split(x.astype(jnp.float32), 2, axis=-1)
    return jnp.concatenate([x1 * cos - x2 * sin, x2 * cos + x1 * sin], axis=-1).astype(x.dtype)

def blocked_attention(q, k, v, scale):
    B, S, H, Dq = q.shape
    nb = S // Q_BLOCK
    qb = q.reshape(B, nb, Q_BLOCK, H, Dq).transpose(1, 0, 2, 3, 4)

    def one_block(qblk):
        s = jnp.einsum('bqhd,bkhd->bhqk', qblk, k).astype(jnp.float32) * scale
        p = jax.nn.softmax(s, axis=-1).astype(v.dtype)
        return jnp.einsum('bhqk,bkhd->bqhd', p, v)

    o = lax.map(one_block, qb)
    return o.transpose(1, 0, 2, 3, 4).reshape(B, S, H, v.shape[-1])

def mla_mixer(c_q, c_kv, k_rope, cos, sin, q_a_norm, w_q_up, kv_a_norm, w_kv_up, q_norm, k_norm):
    B, S, _ = c_q.shape
    q = (rms_norm(c_q, q_a_norm) @ w_q_up).reshape(B, S, MLA_HEADS, MLA_QK_DIM)
    kv = (rms_norm(c_kv, kv_a_norm) @ w_kv_up).reshape(B, S, MLA_HEADS, MLA_NOPE_DIM + MLA_V_DIM)
    k_nope, v = kv[..., :MLA_NOPE_DIM], kv[..., MLA_NOPE_DIM:]
    k_r = jnp.broadcast_to(k_rope[:, :, None, :], (B, S, MLA_HEADS, MLA_ROPE_DIM))
    k = jnp.concatenate([k_nope, k_r], axis=-1)
    q = rms_norm(q, q_norm)
    k = rms_norm(k, k_norm)
    q = jnp.concatenate([q[..., :MLA_NOPE_DIM], apply_rope_2(q[..., MLA_NOPE_DIM:], cos, sin)], axis=-1)
    k = jnp.concatenate([k[..., :MLA_NOPE_DIM], apply_rope_2(k[..., MLA_NOPE_DIM:], cos, sin)], axis=-1)
    o = blocked_attention(q, k, v, MLA_QK_DIM ** -0.5)
    return o.reshape(B, S, MLA_WIDTH)

def gla_chunk_scan(q, k, g, v):
    B, S, H, DK = q.shape
    DV = v.shape[-1]
    n = S // HG_CHUNK

    def to_chunks(t):
        return t.astype(jnp.float32).reshape(B, n, HG_CHUNK, H, t.shape[-1]).transpose(1, 0, 3, 2, 4)

    qc, kc, gc, vc = to_chunks(q), to_chunks(k), to_chunks(g), to_chunks(v)
    mask = jnp.tril(jnp.ones((HG_CHUNK, HG_CHUNK), dtype=bool))

    def step(state, inp):
        qi, ki, gi, vi = inp
        b = jnp.cumsum(gi, axis=2)
        o_inter = jnp.einsum('bhtd,bhdv->bhtv', qi * jnp.exp(b), state)
        diff = b[:, :, :, None, :] - b[:, :, None, :, :]
        decay = jnp.exp(jnp.where(mask[:, :, None], diff, -jnp.inf))
        attn = jnp.einsum('bhtd,bhsd,bhtsd->bhts', qi, ki, decay)
        o_intra = jnp.einsum('bhts,bhsv->bhtv', attn, vi)
        b_last = b[:, :, -1:, :]
        new_state = jnp.exp(b_last[:, :, 0, :])[..., None] * state + jnp.einsum(
            'bhsd,bhsv->bhdv', ki * jnp.exp(b_last - b), vi)
        return new_state, o_inter + o_intra

    s0 = jnp.zeros((B, H, DK, DV), jnp.float32)
    _, o = lax.scan(step, s0, (qc, kc, gc, vc))
    return o.transpose(1, 0, 3, 2, 4).reshape(B, S, H, DV)

def hgrn2_mixer(hq, hf_fwd, hf_bwd, hi, hg, lb, o_norm):
    B, S, _ = hq.shape
    q = jax.nn.silu(hq).reshape(B, S, HG_HEADS, HG_KEY_DIM)
    i = hi.reshape(B, S, HG_HEADS, HG_VAL_DIM)

    def direction(f_pre, lb_dir, reverse):
        z = f_pre.astype(jnp.float32)
        log_f = jnp.logaddexp(jnp.log(lb_dir), jnp.log1p(-lb_dir) + jax.nn.log_sigmoid(z))
        log_f = log_f.reshape(B, S, HG_HEADS, HG_KEY_DIM)
        k = -jnp.expm1(log_f)
        args = (q, k, log_f, i)
        if reverse:
            args = tuple(jnp.flip(a, axis=1) for a in args)
        o = gla_chunk_scan(*args)
        return jnp.flip(o, axis=1) if reverse else o

    o = direction(hf_fwd, lb[0], False) + direction(hf_bwd, lb[1], True)
    o = rms_norm(o, o_norm).astype(hq.dtype) * jax.nn.silu(hg.reshape(B, S, HG_HEADS, HG_VAL_DIM))
    return o.reshape(B, S, HG_WIDTH)

def cross_attention(h, m, w_q, w_kv, q_norm, k_norm, w_o):
    B, S, D = h.shape
    M = m.shape[1]
    q = rms_norm((h @ w_q).reshape(B, S, X_HEADS, X_HEAD_DIM), q_norm)
    kv = (m @ w_kv).reshape(B, M, 2, X_HEADS, X_HEAD_DIM)
    k = rms_norm(kv[:, :, 0], k_norm)
    v = kv[:, :, 1]
    s = jnp.einsum('bqhd,bkhd->bhqk', q, k).astype(jnp.float32) * (X_HEAD_DIM ** -0.5)
    p = jax.nn.softmax(s, axis=-1).astype(v.dtype)
    o = jnp.einsum('bhqk,bkhd->bqhd', p, v).reshape(B, S, X_HEADS * X_HEAD_DIM)
    return o @ w_o

def dropless_experts(t, expert_id, weight, w_gate, w_up, w_down):
    T, D = t.shape
    A = T * MOE_TOP_K
    e_flat = expert_id.reshape(A)
    w_flat = weight.reshape(A)
    tok_flat = jnp.arange(A, dtype=jnp.int32) // MOE_TOP_K
    order = jnp.argsort(e_flat)
    e_sorted, tok_sorted, w_sorted = e_flat[order], tok_flat[order], w_flat[order]
    counts = jnp.bincount(e_flat, length=MOE_EXPERTS)
    padded = (counts + MOE_BLOCK - 1) // MOE_BLOCK * MOE_BLOCK
    start = jnp.cumsum(counts) - counts
    pend = jnp.cumsum(padded)
    pstart = pend - padded
    dest = pstart[e_sorted] + jnp.arange(A, dtype=jnp.int32) - start[e_sorted]
    n_blocks = -(-A // MOE_BLOCK) + MOE_EXPERTS
    rows = jnp.zeros((n_blocks * MOE_BLOCK, D), t.dtype).at[dest].set(t[tok_sorted])
    block_e = jnp.searchsorted(pend, jnp.arange(n_blocks, dtype=jnp.int32) * MOE_BLOCK, side='right')
    block_e = jnp.minimum(block_e, MOE_EXPERTS - 1)

    def expert_block(args):
        xb, e = args
        hb = jax.nn.silu(xb @ w_gate[e]) * (xb @ w_up[e])
        return hb @ w_down[e]

    out = lax.map(expert_block, (rows.reshape(n_blocks, MOE_BLOCK, D), block_e)).reshape(-1, D)
    contrib = out[dest] * w_sorted[:, None].astype(out.dtype)
    return jnp.zeros((T, D), out.dtype).at[tok_sorted].add(contrib)

def hier_moe(h, w_group, b_group, w_expert, b_expert, w_gate, w_up, w_down):
    B, S, D = h.shape
    t = h.reshape(B * S, D)
    g_logits = (t @ w_group).astype(jnp.float32) + b_group.astype(jnp.float32)
    g_prob = jax.nn.softmax(g_logits, axis=-1)
    g_sel = jnp.argmax(g_logits, axis=-1).astype(jnp.int32)
    g_weight = jnp.take_along_axis(g_prob, g_sel[:, None], axis=-1)
    e_logits = ((t @ w_expert).astype(jnp.float32) + b_expert.astype(jnp.float32)).reshape(
        -1, MOE_GROUPS, MOE_PER_GROUP)
    e_logits = jnp.take_along_axis(e_logits, g_sel[:, None, None], axis=1)[:, 0]
    top_logit, top_local = lax.top_k(e_logits, MOE_TOP_K)
    top_w = jax.nn.softmax(top_logit, axis=-1) * g_weight
    expert_id = g_sel[:, None] * MOE_PER_GROUP + top_local.astype(jnp.int32)
    y = dropless_experts(t, expert_id, top_w, w_gate, w_up, w_down)
    return y.reshape(B, S, D)

def second_inputs(seed: int = 0) -> dict:
    key = jax.random.key(seed)
    keys = jax.random.split(key, 40)
    counter = [0]

    def nk():
        k = keys[counter[0]]
        counter[0] += 1
        return k

    def nrm(shape, fan_in):
        return jax.random.normal(nk(), shape, jnp.float32) * (fan_in ** -0.5)

    def gain(shape):
        return 1.0 + 0.02 * jax.random.normal(nk(), shape, jnp.float32)

    L = DEPTH_2
    x = jax.random.normal(nk(), (BATCH, SEQ, D_MODEL), jnp.float32)
    mem = jax.random.normal(nk(), (BATCH, MEM_LEN, D_MODEL), jnp.float32)
    positions = jnp.arange(SEQ, dtype=jnp.int32)[None, :] + jax.random.randint(
        nk(), (BATCH, 1), 0, SEQ, dtype=jnp.int32)
    return {
        'x': x,
        'mem': mem,
        'positions': positions,
        'norm_mix': gain((L, D_MODEL)),
        'w_in': nrm((L, D_MODEL, IN_WIDTH), D_MODEL),
        'mla_q_a_norm': gain((L, MLA_Q_RANK)),
        'mla_w_q_up': nrm((L, MLA_Q_RANK, MLA_HEADS * MLA_QK_DIM), MLA_Q_RANK),
        'mla_kv_a_norm': gain((L, MLA_KV_RANK)),
        'mla_w_kv_up': nrm((L, MLA_KV_RANK, MLA_HEADS * (MLA_NOPE_DIM + MLA_V_DIM)), MLA_KV_RANK),
        'mla_q_norm': gain((L, MLA_QK_DIM)),
        'mla_k_norm': gain((L, MLA_QK_DIM)),
        'hg_lb_logits': 0.1 * jax.random.normal(nk(), (L + 1, 2, HG_FWIDTH), jnp.float32),
        'hg_o_norm': gain((L, HG_VAL_DIM)),
        'w_out': nrm((L, MIX_WIDTH, D_MODEL), MIX_WIDTH),
        'norm_cross': gain((L, D_MODEL)),
        'norm_mem': gain((L, D_MODEL)),
        'x_w_q': nrm((L, D_MODEL, X_HEADS * X_HEAD_DIM), D_MODEL),
        'x_w_kv': nrm((L, D_MODEL, 2 * X_HEADS * X_HEAD_DIM), D_MODEL),
        'x_q_norm': gain((L, X_HEAD_DIM)),
        'x_k_norm': gain((L, X_HEAD_DIM)),
        'x_w_o': nrm((L, X_HEADS * X_HEAD_DIM, D_MODEL), X_HEADS * X_HEAD_DIM),
        'norm_ffn': gain((L, D_MODEL)),
        'moe_w_group': nrm((L, D_MODEL, MOE_GROUPS), D_MODEL),
        'moe_b_group': 0.01 * jax.random.normal(nk(), (L, MOE_GROUPS), jnp.float32),
        'moe_w_expert': nrm((L, D_MODEL, MOE_EXPERTS), D_MODEL),
        'moe_b_expert': 0.01 * jax.random.normal(nk(), (L, MOE_EXPERTS), jnp.float32),
        'moe_w_gate': nrm((L, MOE_EXPERTS, D_MODEL, MOE_HIDDEN), D_MODEL),
        'moe_w_up': nrm((L, MOE_EXPERTS, D_MODEL, MOE_HIDDEN), D_MODEL),
        'moe_w_down': nrm((L, MOE_EXPERTS, MOE_HIDDEN, D_MODEL), MOE_HIDDEN),
    }

def second_block(x, mem, positions, norm_mix, w_in, mla_q_a_norm, mla_w_q_up, mla_kv_a_norm, mla_w_kv_up,
              mla_q_norm, mla_k_norm, hg_lb_logits, hg_o_norm, w_out, norm_cross, norm_mem, x_w_q, x_w_kv,
              x_q_norm, x_k_norm, x_w_o, norm_ffn, moe_w_group, moe_b_group, moe_w_expert, moe_b_expert,
              moe_w_gate, moe_w_up, moe_w_down):
    cos, sin = rope_tables(positions)
    lb_table = jnp.cumsum(jax.nn.softmax(hg_lb_logits.astype(jnp.float32), axis=0), axis=0)
    for l in range(DEPTH_2):
        h = rms_norm(x, norm_mix[l])
        c_q, c_kv, k_rope, hq, hf_fwd, hf_bwd, hi, hg = split_columns(h @ w_in[l])
        a = mla_mixer(c_q, c_kv, k_rope, cos, sin, mla_q_a_norm[l], mla_w_q_up[l], mla_kv_a_norm[l],
                      mla_w_kv_up[l], mla_q_norm[l], mla_k_norm[l])
        r = hgrn2_mixer(hq, hf_fwd, hf_bwd, hi, hg, lb_table[l], hg_o_norm[l])
        x = x + jnp.concatenate([a, r], axis=-1) @ w_out[l]
        x = x + cross_attention(rms_norm(x, norm_cross[l]), rms_norm(mem, norm_mem[l]), x_w_q[l], x_w_kv[l],
                                x_q_norm[l], x_k_norm[l], x_w_o[l])
        x = x + hier_moe(rms_norm(x, norm_ffn[l]), moe_w_group[l], moe_b_group[l], moe_w_expert[l],
                         moe_b_expert[l], moe_w_gate[l], moe_w_up[l], moe_w_down[l])
    return x


_first_inputs = second_inputs


def second_inputs(seed=0):
    import zlib

    import numpy as np

    out = dict(_first_inputs(seed))
    spreads = {}
    factors = {'norm_mix': 2.963,
     'mla_q_a_norm': 8.0,
     'mla_kv_a_norm': 8.0,
     'mla_q_norm': 8.0,
     'mla_k_norm': 8.0,
     'hg_lb_logits': 5.734,
     'hg_o_norm': 3.587,
     'norm_cross': 8.0,
     'norm_mem': 8.0,
     'x_q_norm': 8.0,
     'x_k_norm': 8.0,
     'moe_b_group': 5.14,
     'moe_b_expert': 5.75}
    for name, (base, spread) in spreads.items():
        noise = np.random.default_rng([zlib.crc32(name.encode()), seed]).standard_normal(out[name].shape)
        drawn = base * np.exp(spread * noise) if base else spread * noise
        out[name] = jnp.asarray(drawn.astype(out[name].dtype))
    for name, factor in factors.items():
        out[name] = (out[name] * factor).astype(out[name].dtype)
    return out


def setup_inputs(seed=0):
    out = dict(first_inputs(seed))
    for name, value in second_inputs(seed + 1).items():
        if name != "x":
            out[name + "_2"] = value
    return out


def reference(
    x, c, ctx, c_ctx, norm_w, mod_w, mod_b, final_norm_w, m_in_w, m_conv_w, m_conv_b, m_a_log,
    m_dt_bias, m_d, m_norm_w, m_out_w, a_in_w, a_q_norm, a_k_norm, a_out_w, s_in_w, s_lambda_re,
    s_lambda_im, s_log_step, s_b_re, s_b_im, s_c_re, s_c_im, s_d, s_glu_w, s_glu_b, s_out_w,
    mem_2, positions_2, norm_mix_2, w_in_2, mla_q_a_norm_2, mla_w_q_up_2, mla_kv_a_norm_2,
    mla_w_kv_up_2, mla_q_norm_2, mla_k_norm_2, hg_lb_logits_2, hg_o_norm_2, w_out_2,
    norm_cross_2, norm_mem_2, x_w_q_2, x_w_kv_2, x_q_norm_2, x_k_norm_2, x_w_o_2, norm_ffn_2,
    moe_w_group_2, moe_b_group_2, moe_w_expert_2, moe_b_expert_2, moe_w_gate_2, moe_w_up_2,
    moe_w_down_2,
):
    x = first_block(
        x, c, ctx, c_ctx, norm_w, mod_w, mod_b, final_norm_w, m_in_w, m_conv_w, m_conv_b,
        m_a_log, m_dt_bias, m_d, m_norm_w, m_out_w, a_in_w, a_q_norm, a_k_norm, a_out_w, s_in_w,
        s_lambda_re, s_lambda_im, s_log_step, s_b_re, s_b_im, s_c_re, s_c_im, s_d, s_glu_w,
        s_glu_b, s_out_w,
    )
    return second_block(
        x, mem_2, positions_2, norm_mix_2, w_in_2, mla_q_a_norm_2, mla_w_q_up_2,
        mla_kv_a_norm_2, mla_w_kv_up_2, mla_q_norm_2, mla_k_norm_2, hg_lb_logits_2, hg_o_norm_2,
        w_out_2, norm_cross_2, norm_mem_2, x_w_q_2, x_w_kv_2, x_q_norm_2, x_k_norm_2, x_w_o_2,
        norm_ffn_2, moe_w_group_2, moe_b_group_2, moe_w_expert_2, moe_b_expert_2, moe_w_gate_2,
        moe_w_up_2, moe_w_down_2,
    )


_drawn_inputs = setup_inputs


def setup_inputs(seed=0):
    import zlib

    import numpy as np

    out = dict(_drawn_inputs(seed))
    spreads = {}
    factors = {'a_q_norm': 5.925,
     'a_k_norm': 4.976,
     'norm_ffn_2': 8.0,
     'moe_w_group_2': 3.889,
     'moe_b_group_2': 8.0,
     'moe_w_expert_2': 4.124,
     'moe_b_expert_2': 8.0,
     'moe_w_gate_2': 3.975,
     'moe_w_up_2': 3.7,
     'moe_w_down_2': 3.703}
    for name, (base, spread) in spreads.items():
        noise = np.random.default_rng([zlib.crc32(name.encode()), seed]).standard_normal(out[name].shape)
        drawn = base * np.exp(spread * noise) if base else spread * noise
        out[name] = jnp.asarray(drawn.astype(out[name].dtype))
    for name, factor in factors.items():
        out[name] = (out[name] * factor).astype(out[name].dtype)
    return out
```

```python
from contextlib import ExitStack

import numpy as np
import concourse.bass as bass
from concourse import mybir

F32 = mybir.dt.float32
I32 = mybir.dt.int32
U32 = mybir.dt.uint32
F32R = mybir.dt.float32r
ALU = mybir.AluOpType
ACT = mybir.ActivationFunctionType
AX = mybir.AxisListType

P = 128
D = 1024
KD = D // P
CTX, LAT = 256, 1024
T = CTX + LAT
CT, LT, TT = CTX // P, LAT // P, T // P
EPS = 1e-6
HALF = 512


class Chain:

    def __init__(self, eng, sem, turn=0, per=0):
        self.eng, self.sem, self.turn, self.per, self.n = eng, sem, turn, per, 0

    def done(self, ins):
        ins.then_inc(self.sem, 1)
        self.n += 1
        self.eng.wait_ge(self.sem, self.turn * self.per + self.n)

    def close(self):
        assert self.n == self.per, (self.n, self.per)


class Phase:

    def __init__(self, nc, name):
        self.nc, self.name, self.ctx = nc, name, ExitStack()
        self.sems = []

    def __enter__(self):
        self.ctx.__enter__()
        return self

    def __exit__(self, *a):
        r = self.ctx.__exit__(*a)
        if a[0] is None and self.sems:
            self.nc.clear_and_free_semaphores(self.sems)
            self.nc.all_engine_barrier()
        return r

    def sb(self, name, shape, dt=F32):
        return self.ctx.enter_context(self.nc.sbuf_tensor(f"{self.name}_{name}", shape, dt))

    def ps(self, name, shape, dt=F32):
        return self.ctx.enter_context(self.nc.psum_tensor(f"{self.name}_{name}", shape, dt))

    def sem(self, name):
        s = self.nc.alloc_semaphore(f"{self.name}_{name}")
        self.sems.append(s)
        return s

    def sem2(self, name, n=2):
        return [self.sem(f"{name}{i}") for i in range(n)]


def shape_constants():
    p = np.arange(P)[:, None]
    f = np.arange(P)[None, :]
    parts = {
        "ident": p == f,
        "ones": np.ones((P, P)),
        "le": p <= f,
        "ge": p >= f,
        "gt": p > f,
        "lt": p < f,
    }
    levels = []
    for lo, hi in ((0, 1), (1, 0)):
        m = [p == f]
        for l in range(7):
            same = (p >> (l + 1)) == (f >> (l + 1))
            m.append(same & (((p >> l) & 1) == lo) & (((f >> l) & 1) == hi))
        levels += m
    parts["iota64"] = np.tile(np.arange(64)[None, :], (P, 1))
    parts["pidx"] = p
    parts["neghalf"] = np.full((P, 64), -0.5)
    inv = 10000.0 ** (-np.arange(0, 32, 2, dtype=np.float32) / np.float32(32))
    t = np.arange(LAT)
    ang = np.concatenate([(t // 64)[:, None] * inv, (t % 64)[:, None] * inv], 1).astype(np.float32)
    parts["ropec"] = np.cos(ang).reshape(LT, P, 32).transpose(1, 0, 2).reshape(P, LT * 32)
    parts["ropes"] = np.sin(ang).reshape(LT, P, 32).transpose(1, 0, 2).reshape(P, LT * 32)
    inv2 = 1.0 / (10000.0 ** (np.arange(16, dtype=np.float32) / np.float32(16)))
    parts["inv2"] = np.tile(inv2[None, :], (P, 1))
    at, off = 0, {}
    for k, v in parts.items():
        off[k] = (at, at + v.shape[1])
        at += v.shape[1]
    return np.concatenate([v.astype(np.float32) for v in parts.values()], 1), np.concatenate(levels, 1).astype(np.float32), off


def col_view(row, n):
    return row.rearrange("(k p) -> p k", p=P)


def row_bcast(row):
    return row.rearrange("(a n) -> a n", a=1).to_broadcast([P, row.shape[0]])


def modulation(nc, A, S):
    NCH = 3 * D // HALF
    with Phase(nc, "mod") as f:
        cT = f.sb("cT", [P, 2, KD])
        th = f.sb("th", [P, 2, KD])
        sT = f.sb("sT", [P, KD, 2])
        w = f.sb("w", [P, 2, KD, HALF])
        bias = f.sb("bias", [2, 2, 3 * D])
        rows = f.sb("rows", [2, 2, 3 * D])
        acc = f.ps("acc", [2, 2, HALF])
        c_in, c_th, v_chain, s_ready = f.sem("c_in"), f.sem("c_th"), f.sem("v_chain"), f.sem("s_ready")
        w_in, mm_done, row_done, out_done = f.sem2("w_in"), f.sem("mm_done"), f.sem("row_done"), f.sem("out_done")
        steps = [(l, n) for l in range(2) for n in range(NCH)]
        with nc.Block() as block:
            @block.sync
            def _(sp):
                with nc.allow_non_contiguous_dma(reason="two short vectors"):
                    sp.dma_start(cT[:, 0, :], col_view(A["c"][0], KD)).then_inc(c_in, 16)
                    sp.dma_start(cT[:, 1, :], col_view(A["c_ctx"], KD)).then_inc(c_in, 16)
                for a in range(2):
                    sp.dma_start(bias[a:a + 1, :, :], A["mod_b"][:, :].rearrange("(a l) n -> a l n", a=1)).then_inc(c_in, 16)
                for i, (l, n) in enumerate(steps):
                    if i >= 2:
                        sp.wait_ge(mm_done, i - 1)
                    sp.dma_start(w[:, i % 2], A["mod_w"][l, :, n * HALF:(n + 1) * HALF].rearrange("(k p) n -> p k n", p=P)).then_inc(w_in[i % 2], 16)
                sp.wait_ge(row_done, len(steps))
                sp.dma_start(S["mod"], rows[:, :, :]).then_inc(out_done, 16)
                sp.wait_ge(out_done, 16)

            @block.scalar
            def _(act):
                act.wait_ge(c_in, 64)
                act.activation(th[:, :, :], cT[:, :, :], ACT.Tanh, scale=0.5).then_inc(c_th, 1)

            @block.vector
            def _(v):
                ch = Chain(v, v_chain)
                v.wait_ge(c_th, 1)
                ch.done(v.scalar_tensor_tensor(out=th[:, :, :], in0=th[:, :, :], scalar=1.0, in1=cT[:, :, :], op0=ALU.add, op1=ALU.mult))
                v.tensor_scalar(sT[:, :, :].rearrange("p k a -> p a k"), th[:, :, :], 0.5, None, ALU.mult).then_inc(s_ready, 1)
                for i, (l, n) in enumerate(steps):
                    v.wait_ge(mm_done, i + 1)
                    at = slice(n * HALF, (n + 1) * HALF)
                    v.tensor_tensor(rows[:, l, at], acc[:, i % 2], bias[:, l, at], ALU.add).then_inc(row_done, 1)

            @block.tensor
            def _(pe):
                pe.wait_ge(s_ready, 1)
                for i in range(len(steps)):
                    pe.wait_ge(w_in[i % 2], 16 * (i // 2 + 1))
                    if i >= 2:
                        pe.wait_ge(row_done, i - 1)
                    for k in range(KD):
                        mm = pe.matmul(acc[:, i % 2], sT[:, k, :], w[:, i % 2, k], start=(k == 0), stop=(k == KD - 1))
                    mm.then_inc(mm_done, 1)


def norm_turn(nc, name, C, tiles, sets, hT, keep=None, first=None):
    n = len(tiles)
    ns = len(sets)
    with Phase(nc, name) as f:
        x = f.sb("x", [P, 2, D])
        x2 = f.sb("x2", [P, 2, D]) if first else x
        sq = f.sb("sq", [P, D])
        xn = f.sb("xn", [P, 2, D])
        ss, ms, rs = f.sb("ss", [P, 2 * n]), f.sb("ms", [P, 2 * n]), f.sb("rs", [P, 2 * n])
        cols = f.sb("cols", [P, ns, 3, KD])
        gain = f.sb("gain", [P, ns, KD])
        wrow = f.sb("wrow", [P, D]) if first else None
        pt = f.ps("pt", [P, 2, KD, P])
        c_in, x_in, v_chain, ss_done = f.sem("c_in"), f.sem2("x_in"), f.sem("v_chain"), f.sem("ss_done")
        rs_done, p_chain, xn_done, turned = f.sem("rs_done"), f.sem("p_chain"), f.sem("xn_done"), f.sem("turned")
        ev_a, ev_v, kept, resid = f.sem("ev_a"), f.sem("ev_v"), f.sem2("kept"), f.sem2("resid")
        ncol = sum(1 for s in sets for r in s if r is not None)
        R = 2 if first else 1
        with nc.Block() as block:
            @block.sync
            def _(sp):
                with nc.allow_non_contiguous_dma(reason="vectors by channel"):
                    for i, s in enumerate(sets):
                        for j, r in enumerate(s):
                            if r is not None:
                                sp.dma_start(cols[:, i, j], col_view(r, KD)).then_inc(c_in, 16)
                if first:
                    sp.dma_start(wrow[:, :], row_bcast(first[0])).then_inc(c_in, 16)
                for i, (src, s, col) in enumerate(tiles):
                    if i >= 2:
                        sp.wait_ge(xn_done, R * (i - 1))
                        sp.wait_ge(ss_done, R * (i - 2) + 1)
                    sp.dma_start(x[:, i % 2], src).then_inc(x_in[i % 2], 16)

            @block.gpsimd
            def _(g):
                ch = Chain(g, p_chain)
                for j in range(R * n):
                    g.wait_ge(ss_done, j + 1)
                    ch.done(g.tensor_scalar(ms[:, j:j + 1], ss[:, j:j + 1], 1.0 / D, EPS, ALU.mult, ALU.add))
                    g.tensor_tensor(rs[:, j:j + 1], ms[:, j:j + 1], C["neghalf"][:, 0:1], ALU.pow).then_inc(rs_done, 1)
                    i = j // R
                    if first and j % 2 == 0:
                        g.wait_ge(xn_done, j + 1)
                        g.dma_start(first[1][i * P:(i + 1) * P, :], x2[:, i % 2]).then_inc(resid[i % 2], 16)
                    if keep is not None and j % R == R - 1:
                        g.wait_ge(xn_done, j + 1)
                        g.dma_start(keep[i * P:(i + 1) * P, :], xn[:, i % 2]).then_inc(kept[i % 2], 16)
                for b in range(2):
                    if keep is not None:
                        g.wait_ge(kept[b], 16 * ((n - b + 1) // 2))
                    if first:
                        g.wait_ge(resid[b], 16 * ((n - b + 1) // 2))

            @block.scalar
            def _(act):
                def evict(i):
                    src, s, col = tiles[i]
                    act.wait_ge(turned, i + 1)
                    act.wait_ge(v_chain, ns)
                    for k in range(KD // 2):
                        if sets[s][2] is None:
                            e = act.activation(hT[:, k, col:col + P], pt[:, i % 2, k], ACT.Copy, scale=gain[:, s, k:k + 1])
                        else:
                            e = act.activation(hT[:, k, col:col + P], pt[:, i % 2, k], ACT.Identity, scale=gain[:, s, k:k + 1], bias=cols[:, s, 2, k:k + 1])
                    e.then_inc(ev_a, 1)

                for i in range(n):
                    act.wait_ge(x_in[i % 2], 16 * (i // 2 + 1))
                    if i >= 1:
                        act.wait_ge(ss_done, R * i)
                    act.activation(sq[:, :], x[:, i % 2], ACT.Square, accum_out=ss[:, R * i:R * i + 1]).then_inc(ss_done, 1)
                    if first:
                        act.wait_ge(xn_done, R * i + 1)
                        act.wait_ge(ss_done, R * i + 1)
                        act.activation(sq[:, :], x2[:, i % 2], ACT.Square, accum_out=ss[:, 2 * i + 1:2 * i + 2]).then_inc(ss_done, 1)
                    if i >= 1:
                        evict(i - 1)
                evict(n - 1)

            @block.vector
            def _(v):
                ch = Chain(v, v_chain)
                v.wait_ge(c_in, 16 * (ncol + (1 if first else 0)))
                for i, s in enumerate(sets):
                    if s[1] is None:
                        e = v.tensor_copy(gain[:, i], cols[:, i, 0])
                    else:
                        e = v.scalar_tensor_tensor(out=gain[:, i], in0=cols[:, i, 1], scalar=1.0, in1=cols[:, i, 0], op0=ALU.add, op1=ALU.mult)
                    ch.done(e)

                def evict(i):
                    src, s, col = tiles[i]
                    v.wait_ge(turned, i + 1)
                    for k in range(KD // 2, KD):
                        if sets[s][2] is None:
                            e = v.tensor_scalar(hT[:, k, col:col + P], pt[:, i % 2, k], gain[:, s, k:k + 1], None, ALU.mult)
                        else:
                            e = v.tensor_scalar(hT[:, k, col:col + P], pt[:, i % 2, k], gain[:, s, k:k + 1], cols[:, s, 2, k:k + 1], ALU.mult, ALU.add)
                    e.then_inc(ev_v, 1)

                for i in range(n):
                    j = R * i
                    if i >= 2 and keep is not None:
                        v.wait_ge(kept[i % 2], 16 * (i // 2))
                    if i >= 2 and first:
                        v.wait_ge(resid[i % 2], 16 * (i // 2))
                    if first:
                        v.wait_ge(rs_done, j + 1)
                        if i >= 2:
                            v.wait_ge(ss_done, j - 2)
                        v.scalar_tensor_tensor(out=x2[:, i % 2], in0=x[:, i % 2], scalar=rs[:, j:j + 1], in1=wrow[:, :], op0=ALU.mult, op1=ALU.mult).then_inc(xn_done, 1)
                        v.wait_ge(xn_done, j + 1)
                        j += 1
                    v.wait_ge(rs_done, j + 1)
                    if i >= 2:
                        v.wait_ge(turned, i - 1)
                    v.tensor_scalar(xn[:, i % 2], x2[:, i % 2], rs[:, j:j + 1], None, ALU.mult).then_inc(xn_done, 1)
                    if i >= 1:
                        evict(i - 1)
                evict(n - 1)

            @block.tensor
            def _(pe):
                for i in range(n):
                    pe.wait_ge(xn_done, R * (i + 1))
                    if i >= 2:
                        pe.wait_ge(ev_a, i - 1)
                        pe.wait_ge(ev_v, i - 1)
                    for k in range(KD):
                        e = pe.transpose(pt[:, i % 2, k], xn[:, i % 2, k * P:(k + 1) * P], C["ident"])
                    e.then_inc(turned, 1)


def project(nc, name, hT, cols, w, out=None, chunk=HALF, put=None):
    K, N = w.shape
    kt = -(-K // P)
    kp = [min(P, K - k * P) for k in range(kt)]
    chunks = [(a, min(a + chunk, N)) for a in range(0, N, chunk)]
    m = len(cols)
    with Phase(nc, name) as f:
        wb = f.sb("w", [P, 2, kt, HALF])
        NS = 4
        st = f.sb("st", [P, NS, HALF])
        acc = f.ps("acc", [P, NS, HALF])
        w_in, mm_done, copied, stored = f.sem2("w_in"), f.sem("mm_done"), f.sem2("copied"), f.sem2("stored", NS)
        steps = [(c, j) for c in range(len(chunks)) for j in range(m)]
        with nc.Block() as block:
            @block.sync
            def _(sp):
                for c, (a, b) in enumerate(chunks):
                    if c >= 2:
                        sp.wait_ge(mm_done, (c - 1) * m)
                    full = K // P
                    sp.dma_start(wb[:, c % 2, 0:full, 0:b - a], w[0:full * P, a:b].rearrange("(k p) n -> p k n", p=P)).then_inc(w_in[c % 2], 16)
                    if full < kt:
                        sp.dma_start(wb[0:kp[-1], c % 2, full, 0:b - a], w[full * P:, a:b]).then_inc(w_in[c % 2], 16)

            @block.tensor
            def _(pe):
                for i, (c, j) in enumerate(steps):
                    a, b = chunks[c]
                    pe.wait_ge(w_in[c % 2], (16 if K % P == 0 else 32) * (c // 2 + 1))
                    if i >= NS:
                        pe.wait_ge(copied[i % 2], (i - NS) // 2 + 1)
                    for k in range(kt):
                        mm = pe.matmul(acc[:, i % NS, 0:b - a], hT[0:kp[k], k, cols[j]:cols[j] + P], wb[0:kp[k], c % 2, k, 0:b - a], start=(k == 0), stop=(k == kt - 1))
                    mm.then_inc(mm_done, 1)

            def copy(eng, par):
                for i, (c, j) in enumerate(steps):
                    if i % 2 != par:
                        continue
                    a, b = chunks[c]
                    eng.wait_ge(mm_done, i + 1)
                    if i >= NS and put is None:
                        eng.wait_ge(stored[i % NS], 16 * (i // NS))
                    fn = eng.copy if par == 0 else eng.tensor_copy
                    fn(st[:, i % NS, 0:b - a] if put is None else put(j, a, b), acc[:, i % NS, 0:b - a]).then_inc(copied[par], 1)

            @block.scalar
            def _(act):
                copy(act, 0)

            @block.vector
            def _(v):
                copy(v, 1)

            @block.gpsimd
            def _(g):
                if put is not None:
                    return
                for i, (c, j) in enumerate(steps):
                    a, b = chunks[c]
                    g.wait_ge(copied[i % 2], i // 2 + 1)
                    g.dma_start(out[j * P:(j + 1) * P, a:b], st[:, i % NS, 0:b - a]).then_inc(stored[i % NS], 16)
                for s in range(NS):
                    g.wait_ge(stored[s], 16 * len(range(s, len(steps), NS)))


def out_project(nc, name, C, act_rows, w, tiles, dst, norm_w=None):
    K = w.shape[0]
    kt = K // P
    gates = []
    for _, _, g in tiles:
        if g is not None and g not in [x for x in gates]:
            gates.append(g)
    n = len(tiles)
    with Phase(nc, name) as f:
        wb = f.sb("w", [P, kt, D])
        a = f.sb("a", [P, 2, K])
        aT = f.sb("aT", [P, 2, kt, P])
        r = f.sb("r", [P, 2, D])
        y = f.sb("y", [P, 2, D])
        gb = f.sb("gb", [P, max(1, len(gates)), D])
        sq = f.sb("sq", [P, K]) if norm_w is not None else None
        ss, ms, rs = f.sb("ss", [P, n]), f.sb("ms", [P, n]), f.sb("rs", [P, n])
        nw = f.sb("nw", [P, kt])
        pt = f.ps("pt", [P, 2, 4, P])
        acc = f.ps("acc", [P, 2, 2, HALF])
        w_in, c_in, a_in, r_in = f.sem("w_in"), f.sem("c_in"), f.sem2("a_in"), f.sem2("r_in")
        turned, at_done, mm_done, v_chain = f.sem("turned"), f.sem("at_done"), f.sem("mm_done"), f.sem("v_chain")
        y_done, stored, ss_done, ms_done, rs_done = f.sem("y_done"), f.sem2("stored"), f.sem("ss_done"), f.sem("ms_done"), f.sem("rs_done")
        G = kt // 4
        nc_in = len(gates) + (1 if norm_w is not None else 0)
        with nc.Block() as block:
            @block.sync
            def _(sp):
                for i, g in enumerate(gates):
                    sp.dma_start(gb[:, i], row_bcast(g)).then_inc(c_in, 16)
                if norm_w is not None:
                    with nc.allow_non_contiguous_dma(reason="a vector by channel"):
                        sp.dma_start(nw[:, :], col_view(norm_w, kt)).then_inc(c_in, 16)
                sp.dma_start(a[:, 0], act_rows[tiles[0][0]]).then_inc(a_in[0], 16)
                sp.dma_start(r[:, 0], tiles[0][1]).then_inc(r_in[0], 16)
                sp.dma_start(wb[:, :, :], w.rearrange("(k p) n -> p k n", p=P)).then_inc(w_in, 16)
                for i in range(1, n):
                    if i >= 2:
                        sp.wait_ge(turned, G * (i - 1))
                        if norm_w is not None:
                            sp.wait_ge(ss_done, i - 1)
                        sp.wait_ge(y_done, i - 1)
                    sp.dma_start(a[:, i % 2], act_rows[tiles[i][0]]).then_inc(a_in[i % 2], 16)
                    sp.dma_start(r[:, i % 2], tiles[i][1]).then_inc(r_in[i % 2], 16)

            @block.tensor
            def _(pe):
                def turn(i):
                    pe.wait_ge(a_in[i % 2], 16 * (i // 2 + 1))
                    for q in range(G):
                        j = i * G + q
                        if j >= 2:
                            pe.wait_ge(at_done, j - 1)
                        for u in range(4):
                            k = 4 * q + u
                            e = pe.transpose(pt[:, j % 2, u], a[:, i % 2, k * P:(k + 1) * P], C["ident"])
                        e.then_inc(turned, 1)

                turn(0)
                pe.wait_ge(w_in, 16)
                for i in range(n):
                    if i + 1 < n:
                        turn(i + 1)
                    pe.wait_ge(at_done, G * (i + 1))
                    if i >= 2:
                        pe.wait_ge(y_done, i - 1)
                    for h in range(2):
                        for k in range(kt):
                            mm = pe.matmul(acc[:, i % 2, h], aT[:, i % 2, k], wb[:, k, h * HALF:(h + 1) * HALF], start=(k == 0), stop=(k == kt - 1))
                    mm.then_inc(mm_done, 1)

            @block.scalar
            def _(act):
                if norm_w is not None:
                    act.wait_ge(c_in, 16 * nc_in)
                for i in range(n):
                    if norm_w is not None:
                        act.wait_ge(a_in[i % 2], 16 * (i // 2 + 1))
                        if i:
                            act.wait_ge(ss_done, i)
                        act.activation(sq[:, :], a[:, i % 2], ACT.Square, accum_out=ss[:, i:i + 1]).then_inc(ss_done, 1)
                    for q in range(G):
                        j = i * G + q
                        act.wait_ge(turned, j + 1)
                        if i >= 2:
                            act.wait_ge(mm_done, i - 1)
                        if norm_w is None:
                            act.copy(aT[:, i % 2, 4 * q:4 * q + 4], pt[:, j % 2]).then_inc(at_done, 1)
                        else:
                            for u in range(4):
                                k = 4 * q + u
                                e = act.activation(aT[:, i % 2, k], pt[:, j % 2, u], ACT.Copy, scale=nw[:, k:k + 1])
                            e.then_inc(at_done, 1)

            @block.vector
            def _(v):
                ch = Chain(v, v_chain)
                if nc_in:
                    v.wait_ge(c_in, 16 * nc_in)
                for i, (_, _, g) in enumerate(tiles):
                    v.wait_ge(mm_done, i + 1)
                    v.wait_ge(r_in[i % 2], 16 * (i // 2 + 1))
                    if i >= 2:
                        v.wait_ge(stored[i % 2], 16 * (i // 2))
                    z = acc[:, i % 2].rearrange("p h n -> p (h n)")
                    if g is not None:
                        if norm_w is not None:
                            v.wait_ge(rs_done, i + 1)
                            e = v.scalar_tensor_tensor(out=y[:, i % 2], in0=z, scalar=rs[:, i:i + 1], in1=gb[:, gates.index(g)], op0=ALU.mult, op1=ALU.mult)
                        else:
                            e = v.tensor_tensor(y[:, i % 2], z, gb[:, gates.index(g)], ALU.mult)
                        ch.done(e)
                        z = y[:, i % 2]
                    v.tensor_tensor(y[:, i % 2], z, r[:, i % 2], ALU.add).then_inc(y_done, 1)

            @block.gpsimd
            def _(g):
                for i in range(n):
                    if norm_w is not None:
                        g.wait_ge(ss_done, i + 1)
                        g.tensor_scalar(ms[:, i:i + 1], ss[:, i:i + 1], 1.0 / K, EPS, ALU.mult, ALU.add).then_inc(ms_done, 1)
                        g.wait_ge(ms_done, i + 1)
                        g.tensor_tensor(rs[:, i:i + 1], ms[:, i:i + 1], C["neghalf"][:, 0:1], ALU.pow).then_inc(rs_done, 1)
                    g.wait_ge(y_done, i + 1)
                    g.dma_start(dst[i * P:(i + 1) * P, :], y[:, i % 2]).then_inc(stored[i % 2], 16)
                for b in range(2):
                    g.wait_ge(stored[b], 16 * len(range(b, n, 2)))


def load_constants(nc, ctx, A, off):
    n = max(b for _, b in off.values())
    buf = ctx.enter_context(nc.sbuf_tensor("constants", [P, n], F32))
    with Phase(nc, "const") as f:
        got = f.sem("got")
        with nc.Block() as block:
            @block.sync
            def _(sp):
                sp.dma_start(buf[:, :], A["constants"]).then_inc(got, 16)
                sp.wait_ge(got, 16)
    return {k: buf[:, a:b] for k, (a, b) in off.items()}


def turn_heads(nc, name, C, n, H, d, loads, weight, blocks, rope=None, gate=None):
    npiece = len(loads(0))
    na = rope[1] if rope else 0
    with Phase(nc, name) as f:
        x = f.sb("x", [P, 2, H, d])
        sq = f.sb("sq", [P, 2, H, d])
        ss, ms, rs = f.sb("ss", [P, n, H]), f.sb("ms", [P, n, H]), f.sb("rs", [P, n, H])
        y = f.sb("y", [P, 2, H, d])
        z = f.sb("z", [P, 2, H, d])
        t = f.sb("t", [P, 4, H, max(1, na), 16])
        wr = f.sb("wr", [P, d])
        gr = f.sb("gr", [P, 2, H, d]) if gate else None
        gt = f.sb("gt", [P, 2, H, d]) if gate else None
        gr_in, gt_done = f.sem2("gr_in"), f.sem("gt_done")
        NB = len(blocks)
        pt = f.ps("pt", [P, 4, HALF])
        c_in, x_in, sq_done, ss_done = f.sem("c_in"), f.sem2("x_in"), f.sem("sq_done"), f.sem("ss_done")
        ms_done, rs_done, ready, turned, moved = f.sem("ms_done"), f.sem("rs_done"), f.sem("ready"), f.sem("turned"), f.sem("moved")
        v_chain = f.sem("v_chain")
        with nc.Block() as block:
            @block.sync
            def _(sp):
                sp.dma_start(wr[:, :], row_bcast(weight)).then_inc(c_in, 16)
                for i in range(n):
                    if i >= 2:
                        sp.wait_ge(ready, i - 1)
                    for h0, hn, c0, cn, src in loads(i):
                        sp.dma_start(x[:, i % 2, h0:h0 + hn, c0:c0 + cn], src).then_inc(x_in[i % 2], 16)
                    if gate:
                        sp.dma_start(gr[:, i % 2], gate(i)).then_inc(gr_in[i % 2], 16)

            @block.scalar
            def _(act):
                def move(i):
                    for b, (c0, cn, parts) in enumerate(blocks):
                        j = i * NB + b
                        act.wait_ge(turned, j + 1)
                        for (p0, p1), dst in parts:
                            e = act.copy(dst(i), pt[p0:p1, j % 4, 0:P])
                        e.then_inc(moved, 1)

                for i in range(n):
                    act.wait_ge(x_in[i % 2], 16 * npiece * (i // 2 + 1))
                    if i >= 2:
                        act.wait_ge(ss_done, i - 1)
                    act.activation(sq[:, i % 2], x[:, i % 2], ACT.Square).then_inc(sq_done, 1)
                    if gate:
                        act.wait_ge(gr_in[i % 2], 16 * (i // 2 + 1))
                        if i >= 2:
                            act.wait_ge(ready, i - 1)
                        act.activation(gt[:, i % 2], gr[:, i % 2], ACT.Tanh, scale=0.5).then_inc(gt_done, 1)
                    if i >= 1:
                        move(i - 1)
                move(n - 1)

            @block.gpsimd
            def _(g):
                for i in range(n):
                    g.wait_ge(ss_done, i + 1)
                    g.tensor_scalar(ms[:, i], ss[:, i], 1.0 / d, EPS, ALU.mult, ALU.add).then_inc(ms_done, 1)
                    g.wait_ge(ms_done, i + 1)
                    g.tensor_tensor(rs[:, i], ms[:, i], C["neghalf"][:, 0:H], ALU.pow).then_inc(rs_done, 1)

            @block.vector
            def _(v):
                ch = Chain(v, v_chain)
                v.wait_ge(c_in, 16)

                def reduce(i):
                    v.wait_ge(sq_done, i + 1)
                    v.tensor_reduce(ss[:, i], sq[:, i % 2], AX.X, ALU.add).then_inc(ss_done, 1)

                reduce(0)
                for i in range(n):
                    if i + 1 < n:
                        reduce(i + 1)
                    v.wait_ge(rs_done, i + 1)
                    v.wait_ge(x_in[i % 2], 16 * npiece * (i // 2 + 1))
                    if i >= 2:
                        v.wait_ge(turned, NB * (i - 1))
                    ch.done(v.tensor_tensor(y[:, i % 2], x[:, i % 2], rs[:, i].rearrange("p (h a) -> p h a", a=1).to_broadcast([P, H, d]), ALU.mult))
                    e = v.tensor_tensor(z[:, i % 2], y[:, i % 2], wr[:, :].rearrange("p (a d) -> p a d", a=1).to_broadcast([P, H, d]), ALU.mult)
                    if gate:
                        ch.done(e)
                        v.wait_ge(gt_done, i + 1)
                        ch.done(v.scalar_tensor_tensor(out=gt[:, i % 2], in0=gt[:, i % 2], scalar=1.0, in1=gr[:, i % 2], op0=ALU.add, op1=ALU.mult))
                        v.scalar_tensor_tensor(out=z[:, i % 2], in0=z[:, i % 2], scalar=0.5, in1=gt[:, i % 2], op0=ALU.mult, op1=ALU.mult).then_inc(ready, 1)
                        continue
                    tab = rope[2](i) if rope else None
                    if tab is None:
                        e.then_inc(ready, 1)
                        continue
                    ch.done(e)
                    o = rope[0]
                    zz = z[:, i % 2, :, o:o + 32 * na].rearrange("p h (a b q) -> p h a b q", a=na, b=2)
                    x1, x2 = zz[:, :, :, 0, :], zz[:, :, :, 1, :]
                    cs, sn = (u.rearrange("p (o a q) -> p o a q", o=1, a=na).to_broadcast([P, H, na, 16]) for u in tab)
                    v.tensor_tensor(t[:, 0], x1, cs, ALU.mult)
                    v.tensor_tensor(t[:, 1], x2, sn, ALU.mult)
                    v.tensor_tensor(t[:, 2], x1, sn, ALU.mult)
                    ch.done(v.tensor_tensor(t[:, 3], x2, cs, ALU.mult))
                    v.tensor_tensor(x1, t[:, 0], t[:, 1], ALU.subtract)
                    v.tensor_tensor(x2, t[:, 2], t[:, 3], ALU.add).then_inc(ready, 1)
                    v.wait_ge(ready, i + 1)

            @block.tensor
            def _(pe):
                for i in range(n):
                    pe.wait_ge(ready, i + 1)
                    zf = z[:, i % 2].rearrange("p h d -> p (h d)")
                    for b, (c0, cn, parts) in enumerate(blocks):
                        j = i * NB + b
                        if j >= 4:
                            pe.wait_ge(moved, j - 3)
                        pe.transpose(pt[0:cn, j % 4, 0:P], zf[:, c0:c0 + cn], C["ident"]).then_inc(turned, 1)


def project_heads(nc, name, C, hT, cols, w, d, chunk, weight, put, rope=None, copies=0, extra=None, values=None):
    K, N = w.shape
    kt = -(-K // P)
    kp = [min(P, K - k * P) for k in range(kt)]
    chunks = [(a, a + chunk) for a in range(0, N, chunk)]
    m = len(cols)
    de = extra.shape[-1] if extra is not None else 0
    dw = d - de
    hw = dw if values is None else 128
    hc = chunk // hw
    na = rope[1] if rope else 0
    steps = [(c, j) for c in range(len(chunks)) for j in range(m)]
    n = len(steps)
    width = hc * d * (2 * copies if copies else 1)
    bw = P if width % P == 0 and (copies or d % P == 0) else d
    nblk = width // bw
    groups = [(a, min(a + 4, nblk)) for a in range(0, nblk, 4)]
    G = len(groups)
    NX = 3
    with Phase(nc, name) as f:
        wb = f.sb("w", [P, 2, kt, chunk])
        x = f.sb("x", [P, NX, hc, d])
        sq = f.sb("sq", [P, 2, hc, d])
        ss, ms, rs = (f.sb(s, [P, n, hc]) for s in ("ss", "ms", "rs"))
        y = f.sb("y", [P, hc, d])
        z = f.sb("z", [P, 2, hc, d])
        zz = f.sb("zz", [P, 2, hc, 2, copies, d]) if copies else z
        t = f.sb("t", [P, 4, hc, max(1, na), 16])
        wr = f.sb("wr", [P, d])
        acc = f.ps("acc", [P, 4, HALF])
        pt = f.ps("pt", [P, 4, HALF])
        w_in, c_in, mm_done, x_done, sq_done = f.sem2("w_in"), f.sem("c_in"), f.sem("mm_done"), f.sem("x_done"), f.sem("sq_done")
        ss_done, ms_done, rs_done, y_done, z_done = (f.sem(s) for s in ("ss_done", "ms_done", "rs_done", "y_done", "z_done"))
        first_done, ready, turned, moved, v_chain = (f.sem(s) for s in ("first_done", "ready", "turned", "moved", "v_chain"))
        NXD = 1 + (1 if extra is not None else 0)
        with nc.Block() as block:
            @block.sync
            def _(sp):
                full = K // P
                for c, (a, b) in enumerate(chunks):
                    if c >= 2:
                        sp.wait_ge(mm_done, (c - 1) * m)
                    sp.dma_start(wb[:, c % 2, 0:full], w[0:full * P, a:b].rearrange("(k p) n -> p k n", p=P)).then_inc(w_in[c % 2], 16)
                    if full < kt:
                        sp.dma_start(wb[0:kp[-1], c % 2, full], w[full * P:, a:b]).then_inc(w_in[c % 2], 16)
                    if c == 0:
                        sp.dma_start(wr[:, :], row_bcast(weight)).then_inc(c_in, 16)

            @block.tensor
            def _(pe):
                def turn(i):
                    pe.wait_ge(ready, i + 1)
                    zf = (zz[:, i % 2].rearrange("p h s r d -> p (h s r d)") if copies else z[:, i % 2].rearrange("p h d -> p (h d)"))
                    for g, (a, b) in enumerate(groups):
                        j = i * G + g
                        if j >= 4:
                            pe.wait_ge(moved, j - 3)
                        for u in range(a, b):
                            e = pe.transpose(pt[0:bw, j % 4, (u - a) * P:(u - a + 1) * P], zf[:, u * bw:(u + 1) * bw], C["ident"])
                        e.then_inc(turned, 1)

                for i in range(n + 3):
                    if i < n:
                        c, j = steps[i]
                        pe.wait_ge(w_in[c % 2], 16 * (1 if K % P == 0 else 2) * (c // 2 + 1))
                        if i >= 4:
                            pe.wait_ge(x_done, NXD * (i - 3))
                        for k in range(kt):
                            mm = pe.matmul(acc[:, i % 4, 0:chunk], hT[0:kp[k], k, cols[j]:cols[j] + P], wb[0:kp[k], c % 2, k], start=(k == 0), stop=(k == kt - 1))
                        mm.then_inc(mm_done, 1)
                    if i >= 3:
                        turn(i - 3)

            @block.scalar
            def _(act):
                for i in range(n + 3):
                    if i < n:
                        c, j = steps[i]
                        act.wait_ge(mm_done, i + 1)
                        if i >= NX:
                            act.wait_ge(y_done, i - NX + 1)
                        src = acc[:, i % 4, 0:chunk].rearrange("p (h d) -> p h d", h=hc)
                        if values is not None:
                            act.copy(values(c, j), src[:, :, dw:hw])
                        if extra is not None:
                            act.copy(x[:, i % NX, :, dw:d], extra[:, j].rearrange("p (o e) -> p o e", o=1).to_broadcast([P, hc, de])).then_inc(x_done, 1)
                        act.copy(x[:, i % NX, :, 0:dw], src[:, :, 0:dw]).then_inc(x_done, 1)
                        act.wait_ge(x_done, NXD * (i + 1))
                        if i >= 2:
                            act.wait_ge(ss_done, i - 1)
                        act.activation(sq[:, i % 2], x[:, i % NX], ACT.Square).then_inc(sq_done, 1)
                    if copies and 1 <= i <= n:
                        k = i - 1
                        act.wait_ge(z_done, k + 1)
                        if k >= 2:
                            act.wait_ge(turned, G * (k - 1))
                        act.copy(zz[:, k % 2, :, 0].bitcast(F32R), z[:, k % 2].rearrange("p h (r d) -> p h r d", r=1).to_broadcast([P, hc, copies, d])).then_inc(first_done, 1)
                    if i >= 3:
                        c, j = steps[i - 3]
                        for g, (a, b) in enumerate(groups):
                            q = (i - 3) * G + g
                            act.wait_ge(turned, q + 1)
                            act.copy(put(c, j, g), pt[0:bw, q % 4, 0:(b - a) * P].rearrange("p (b t) -> p b t", b=b - a)).then_inc(moved, 1)

            @block.gpsimd
            def _(g):
                for i in range(n):
                    g.wait_ge(ss_done, i + 1)
                    g.tensor_scalar(ms[:, i], ss[:, i], 1.0 / d, EPS, ALU.mult, ALU.add).then_inc(ms_done, 1)
                    g.wait_ge(ms_done, i + 1)
                    g.tensor_tensor(rs[:, i], ms[:, i], C["neghalf"][:, 0:hc], ALU.pow).then_inc(rs_done, 1)

            @block.vector
            def _(v):
                ch = Chain(v, v_chain)
                v.wait_ge(c_in, 16)

                def second(i):
                    v.wait_ge(first_done, i + 1)
                    v.tensor_tensor(zz[:, i % 2, :, 1].bitcast(F32R), z[:, i % 2].rearrange("p h (r d) -> p h r d", r=1).to_broadcast([P, hc, copies, d]), zz[:, i % 2, :, 0], ALU.subtract).then_inc(ready, 1)

                def main(i):
                    c, j = steps[i]
                    last = z_done if copies else ready
                    v.wait_ge(rs_done, i + 1)
                    if not copies and i >= 2:
                        v.wait_ge(turned, G * (i - 1))
                    if copies and i >= 2:
                        v.wait_ge(ready, i - 1)
                    if i:
                        v.wait_ge(z_done if copies else ready, i)
                    v.tensor_tensor(y[:, :, :], x[:, i % NX], rs[:, i].rearrange("p (h a) -> p h a", a=1).to_broadcast([P, hc, d]), ALU.mult).then_inc(y_done, 1)
                    v.wait_ge(y_done, i + 1)
                    e = v.tensor_tensor(z[:, i % 2], y[:, :, :], wr[:, :].rearrange("p (a d) -> p a d", a=1).to_broadcast([P, hc, d]), ALU.mult)
                    tab = rope[2](j) if rope else None
                    if tab is None:
                        e.then_inc(last, 1)
                        return
                    ch.done(e)
                    o = rope[0]
                    q = z[:, i % 2, :, o:o + 32 * na].rearrange("p h (a b q) -> p h a b q", a=na, b=2)
                    x1, x2 = q[:, :, :, 0, :], q[:, :, :, 1, :]
                    cs, sn = (u.rearrange("p (o a q) -> p o a q", o=1, a=na).to_broadcast([P, hc, na, 16]) for u in tab)
                    v.tensor_tensor(t[:, 0], x1, cs, ALU.mult)
                    v.tensor_tensor(t[:, 1], x2, sn, ALU.mult)
                    v.tensor_tensor(t[:, 2], x1, sn, ALU.mult)
                    ch.done(v.tensor_tensor(t[:, 3], x2, cs, ALU.mult))
                    v.tensor_tensor(x1, t[:, 0], t[:, 1], ALU.subtract)
                    v.tensor_tensor(x2, t[:, 2], t[:, 3], ALU.add).then_inc(last, 1)

                for i in range(n + 2):
                    if i < n:
                        v.wait_ge(sq_done, i + 1)
                        v.tensor_reduce(ss[:, i], sq[:, i % 2], AX.X, ALU.add).then_inc(ss_done, 1)
                    if copies and i >= 2:
                        second(i - 2)
                    if 1 <= i <= n:
                        main(i - 1)


def attend(nc, name, C, heads, nq, nkeys, scale):
    kt = nkeys // P
    banks = [(a, min(a + HALF, nkeys)) for a in range(0, nkeys, HALF)]
    nb = len(banks)
    NV = len(heads[0][1])
    m = heads[0][1][0][1]
    steps = [(h, q) for h in range(len(heads)) for q in range(nq)]
    n = len(steps)
    groups = [(a, min(a + 4, kt)) for a in range(0, kt, 4)]
    with Phase(nc, name) as f:
        pr = f.sb("pr", [P, 2, nkeys])
        pT = f.sb("pT", [P, 2, kt, P])
        mx, nm, sm, rc = (f.sb(x, [P, n]) for x in ("mx", "nm", "sm", "rc"))
        o = f.sb("o", [m, 2, NV, nq * P])
        S = [f.ps(f"S{b}", [P, nb, HALF]) for b in range(2)]
        O = f.ps("O", [P, 2, HALF])
        s_done, mx_done, nm_done, e_done, rc_done, p_done, turned = (f.sem(x) for x in ("s_done", "mx_done", "nm_done", "e_done", "rc_done", "p_done", "turned"))
        ev_a, ev_v, o_done, o_out, stored = f.sem("ev_a"), f.sem("ev_v"), f.sem("o_done"), f.sem("o_out"), f.sem2("stored")
        ga = [x for x in range(len(groups)) if x % 2 == 0]
        gv = [x for x in range(len(groups)) if x % 2 == 1]
        with nc.Block() as block:
            @block.tensor
            def _(pe):
                def scores(i):
                    h, q = steps[i]
                    if i >= 2:
                        pe.wait_ge(ev_a, i - 1)
                        if gv:
                            pe.wait_ge(ev_v, i - 1)
                    for b, (a, z) in enumerate(banks):
                        for c, (qT, kT) in enumerate(heads[h][0]):
                            mm = pe.matmul(S[i % 2][:, b, 0:z - a], qT[:, q * P:(q + 1) * P], kT[:, a:z], start=(c == 0), stop=(c == len(heads[h][0]) - 1))
                    mm.then_inc(s_done, 1)

                def turn(i):
                    pe.wait_ge(p_done, i + 1)
                    for g, (a, z) in enumerate(groups):
                        for k in range(a, z):
                            mm = pe.transpose(S[i % 2][:, g, (k - a) * P:(k - a + 1) * P], pr[:, i % 2, k * P:(k + 1) * P], C["ident"])
                    mm.then_inc(turned, 1)

                def values(i):
                    h, q = steps[i]
                    pe.wait_ge(ev_a, i + 1)
                    if gv:
                        pe.wait_ge(ev_v, i + 1)
                    if i >= 2:
                        pe.wait_ge(o_out, i - 1)
                    for w, (vf, mm_) in enumerate(heads[h][1]):
                        for k in range(kt):
                            mm = pe.matmul(O[0:m, i % 2, w * P:w * P + P], vf(k), pT[:, i % 2, k], start=(k == 0), stop=(k == kt - 1))
                    mm.then_inc(o_done, 1)

                for i in range(n + 2):
                    if i < n:
                        scores(i)
                    if 1 <= i <= n:
                        turn(i - 1)
                    if i >= 2:
                        values(i - 2)

            @block.vector
            def _(v):
                def evict(i):
                    v.wait_ge(turned, i + 1)
                    if i >= 2:
                        v.wait_ge(o_done, i - 1)
                    for g in gv:
                        a, z = groups[g]
                        e = v.tensor_copy(pT[:, i % 2, a:z], S[i % 2][:, g, 0:(z - a) * P].rearrange("p (k q) -> p k q", k=z - a))
                    if gv:
                        e.then_inc(ev_v, 1)

                def out(i):
                    h, q = steps[i]
                    v.wait_ge(o_done, i + 1)
                    if h >= 2:
                        v.wait_ge(stored[h % 2], 16 * NV * (h // 2))
                    v.tensor_copy(o[:, h % 2, :, q * P:(q + 1) * P], O[0:m, i % 2, 0:NV * P].rearrange("p (w q) -> p w q", w=NV)).then_inc(o_out, 1)

                for i in range(n + 2):
                    if i < n:
                        v.wait_ge(s_done, i + 1)
                        v.tensor_reduce(mx[:, i:i + 1], S[i % 2][:, :, :].rearrange("p b n -> p (b n)")[:, 0:nkeys], AX.X, ALU.max).then_inc(mx_done, 1)
                        v.wait_ge(mx_done, i + 1)
                        v.tensor_scalar(nm[:, i:i + 1], mx[:, i:i + 1], -scale, None, ALU.mult).then_inc(nm_done, 1)
                    if 1 <= i <= n:
                        evict(i - 1)
                    if i < n:
                        v.wait_ge(e_done, i + 1)
                        v.reciprocal(rc[:, i:i + 1], sm[:, i:i + 1]).then_inc(rc_done, 1)
                        v.wait_ge(rc_done, i + 1)
                        v.tensor_scalar(pr[:, i % 2], pr[:, i % 2], rc[:, i:i + 1], None, ALU.mult).then_inc(p_done, 1)
                    if i >= 2:
                        out(i - 2)

            @block.scalar
            def _(act):
                def evict(i):
                    act.wait_ge(turned, i + 1)
                    if i >= 2:
                        act.wait_ge(o_done, i - 1)
                    for g in ga:
                        a, z = groups[g]
                        e = act.copy(pT[:, i % 2, a:z], S[i % 2][:, g, 0:(z - a) * P].rearrange("p (k q) -> p k q", k=z - a))
                    e.then_inc(ev_a, 1)

                for i in range(n + 1):
                    if i >= 1:
                        evict(i - 1)
                    if i < n:
                        act.wait_ge(nm_done, i + 1)
                        if i >= 2:
                            act.wait_ge(turned, i - 1)
                        act.activation(pr[:, i % 2], S[i % 2][:, :, :].rearrange("p b n -> p (b n)")[:, 0:nkeys], ACT.Exp, bias=nm[:, i:i + 1], scale=scale, accum_out=sm[:, i:i + 1]).then_inc(e_done, 1)

            @block.gpsimd
            def _(g):
                for h in range(len(heads)):
                    g.wait_ge(o_out, nq * (h + 1))
                    for w in range(NV):
                        g.dma_start(heads[h][2][w], o[:, h % 2, w]).then_inc(stored[h % 2], 16)
                for b in range(2):
                    g.wait_ge(stored[b], 16 * NV * len(range(b, len(heads), 2)))


def out_project_t(nc, name, C, aT_dram, w, n, resid, dst, gate=None, silu_rows=None):
    K = w.shape[0]
    kt = K // P
    G = kt // 4
    with Phase(nc, name) as f:
        wb = f.sb("w", [P, kt, D])
        a = f.sb("a", [P, 2, kt, P])
        b_ = f.sb("b", [P, 2, kt, P]) if silu_rows is not None else a
        g_ = f.sb("g", [P, 2, K]) if silu_rows is not None else None
        th = f.sb("th", [P, 2, K]) if silu_rows is not None else None
        r, y, gb = f.sb("r", [P, 2, D]), f.sb("y", [P, 2, D]), f.sb("gb", [P, D])
        pt = f.ps("pt", [P, 2, 4, P])
        acc = f.ps("acc", [P, 2, 2, HALF])
        w_in, c_in, a_in, g_in, th_done, gs_done = f.sem("w_in"), f.sem("c_in"), f.sem2("a_in"), f.sem2("g_in"), f.sem("th_done"), f.sem("gs_done")
        turned, at_done, mm_done, v_chain, y_done, stored = f.sem("turned"), f.sem("at_done"), f.sem("mm_done"), f.sem("v_chain"), f.sem("y_done"), f.sem2("stored")
        with nc.Block() as block:
            @block.sync
            def _(sp):
                if gate is not None:
                    sp.dma_start(gb[:, :], row_bcast(gate)).then_inc(c_in, 16)
                for i in range(n):
                    if i >= 2:
                        sp.wait_ge(mm_done, i - 1)
                        sp.wait_ge(y_done, i - 1)
                    if g_ is not None:
                        sp.dma_start(g_[:, i % 2], silu_rows[i * P:(i + 1) * P, :]).then_inc(g_in[i % 2], 16)
                    sp.dma_start(a[:, i % 2], aT_dram[:, i * P:(i + 1) * P].rearrange("(k p) t -> p k t", p=P)).then_inc(a_in[i % 2], 16)
                    sp.dma_start(r[:, i % 2], resid[i * P:(i + 1) * P, :]).then_inc(a_in[i % 2], 16)
                    if i == 0:
                        sp.dma_start(wb[:, :, :], w.rearrange("(k p) n -> p k n", p=P)).then_inc(w_in, 16)

            @block.tensor
            def _(pe):
                def turn(i):
                    pe.wait_ge(gs_done, i + 1)
                    for q in range(G):
                        j = i * G + q
                        if j >= 2:
                            pe.wait_ge(at_done, j - 1)
                        for u in range(4):
                            k = 4 * q + u
                            e = pe.transpose(pt[:, j % 2, u], th[:, i % 2, k * P:(k + 1) * P], C["ident"])
                        e.then_inc(turned, 1)

                if g_ is not None:
                    turn(0)
                pe.wait_ge(w_in, 16)
                for i in range(n):
                    if g_ is not None:
                        if i + 1 < n:
                            turn(i + 1)
                        pe.wait_ge(at_done, G * (i + 1))
                    else:
                        pe.wait_ge(a_in[i % 2], 32 * (i // 2 + 1))
                    if i >= 2:
                        pe.wait_ge(y_done, i - 1)
                    for h in range(2):
                        for k in range(kt):
                            mm = pe.matmul(acc[:, i % 2, h], b_[:, i % 2, k], wb[:, k, h * HALF:(h + 1) * HALF], start=(k == 0), stop=(k == kt - 1))
                    mm.then_inc(mm_done, 1)

            @block.scalar
            def _(act):
                if g_ is not None:
                    for i in range(n):
                        act.wait_ge(g_in[i % 2], 16 * (i // 2 + 1))
                        if i >= 2:
                            act.wait_ge(turned, G * (i - 1))
                        act.activation(th[:, i % 2], g_[:, i % 2], ACT.Tanh, scale=0.5).then_inc(th_done, 1)

            @block.vector
            def _(v):
                ch = Chain(v, v_chain)
                if gate is not None:
                    v.wait_ge(c_in, 16)

                def silu(i):
                    v.wait_ge(th_done, i + 1)
                    v.scalar_tensor_tensor(out=th[:, i % 2], in0=th[:, i % 2], scalar=1.0, in1=g_[:, i % 2], op0=ALU.add, op1=ALU.mult).then_inc(gs_done, 1)

                def merge(i):
                    for q in range(G):
                        j = i * G + q
                        v.wait_ge(turned, j + 1)
                        v.wait_ge(a_in[i % 2], 32 * (i // 2 + 1))
                        if i >= 2:
                            v.wait_ge(mm_done, i - 1)
                        v.scalar_tensor_tensor(out=b_[:, i % 2, 4 * q:4 * q + 4], in0=pt[:, j % 2], scalar=0.5, in1=a[:, i % 2, 4 * q:4 * q + 4], op0=ALU.mult, op1=ALU.mult).then_inc(at_done, 1)

                if g_ is not None:
                    silu(0)
                    merge(0)
                for i in range(n):
                    if g_ is not None and i + 1 < n:
                        silu(i + 1)
                        merge(i + 1)
                    v.wait_ge(mm_done, i + 1)
                    v.wait_ge(a_in[i % 2], 32 * (i // 2 + 1))
                    if i >= 2:
                        v.wait_ge(stored[i % 2], 16 * (i // 2))
                    z = acc[:, i % 2].rearrange("p h n -> p (h n)")
                    if gate is not None:
                        ch.done(v.tensor_tensor(y[:, i % 2], z, gb[:, :], ALU.mult))
                        z = y[:, i % 2]
                    v.tensor_tensor(y[:, i % 2], z, r[:, i % 2], ALU.add).then_inc(y_done, 1)

            @block.gpsimd
            def _(g):
                for i in range(n):
                    g.wait_ge(y_done, i + 1)
                    g.dma_start(dst[i * P:(i + 1) * P, :], y[:, i % 2]).then_inc(stored[i % 2], 16)
                for b in range(2):
                    g.wait_ge(stored[b], 16 * len(range(b, n, 2)))


def move(nc, name, pairs, zero=()):
    with Phase(nc, name) as f:
        s, z = f.sem("moved"), f.sem("zeroed")
        with nc.Block() as block:
            @block.vector
            def _(v):
                for i, a in enumerate(zero):
                    v.memset(a, 0.0).then_inc(z, 1)
                if zero:
                    v.wait_ge(z, len(zero))

            @block.sync
            def _(sp):
                for dst, src in pairs:
                    sp.dma_start(dst, src).then_inc(s, 16)
                sp.wait_ge(s, 16 * len(pairs))


def attention_layer(nc, C, A, S, hT):
    W, KW = D, D // 4
    with ExitStack() as c2:
        sb = lambda name, shape: c2.enter_context(nc.sbuf_tensor(name, shape, F32))
        w = A["a_in_w"][0]
        project(nc, "a_g", hT, [CTX + i * P for i in range(LT)], w[:, W + 2 * KW:], S["ag"])
        cs, sn = C["ropec"], C["ropes"]
        table = lambda j: (cs[:, 32 * j:32 * j + 32], sn[:, 32 * j:32 * j + 32])
        vv = sb("a_v", [P, TT, KW])
        project(nc, "a_vp", hT, [i * P for i in range(TT)], w[:, W + KW:W + 2 * KW], chunk=KW, put=lambda j, a, b: vv[:, j, a:b])
        kT = c2.enter_context(nc.sbuf_tensor("a_kT", [P, 4, 2, T], F32R))
        project_heads(nc, "a_k", C, hT, [i * P for i in range(TT)], w[:, W:W + KW], 64, KW, A["a_k_norm"][0],
                      lambda c, j, g: kT[:, 2 * g:2 * g + 2, :, j * P:(j + 1) * P].rearrange("p g s t -> p (g s) t"),
                      rope=(0, 2, lambda j: None if j < CT else table(j - CT)), copies=2)
        qT = c2.enter_context(nc.sbuf_tensor("a_qT", [P, 16, LAT], F32R))
        project_heads(nc, "a_q", C, hT, [CTX + i * P for i in range(LT)], w[:, 0:W], 64, KW, A["a_q_norm"][0],
                      lambda c, j, g: qT[:, 4 * c:4 * c + 4, j * P:(j + 1) * P], rope=(0, 2, table), copies=1)
        heads = [([(qT[:, h], kT[:, h // 4, s]) for s in range(2)],
                  [((lambda g: lambda k: vv[:, k, g * 64:(g + 1) * 64])(h // 4), 64)],
                  [S["aoT"][h * 64:(h + 1) * 64, :]]) for h in range(16)]
        attend(nc, "a_at", C, heads, LT, T, 64 ** -0.5)
    out_project_t(nc, "a_out", C, S["aoT"], A["a_out_w"][0], LT, S["h1"][CTX:T, :], S["h2"], gate=S["mod"][0, 1, 2 * D:3 * D], silu_rows=S["ag"])


NG, NHG, HD, NS_, DI = 8, 4, 64, 128, 2 * D
NH = NG * NHG
GW = NHG * HD
CONV = 5
XBC = 2 * DI


def mamba_steps(nc, C, A, hT, dt, la, ecum, tend, edec):
    c0 = DI + XBC
    H2 = 2 * NH
    with Phase(nc, "dt") as f:
        w = f.sb("w", [P, KD, H2])
        bias, al = f.sb("bias", [P, H2]), f.sb("al", [P, H2])
        x, e, u, t1, t2 = (f.sb(n, [P, TT, H2]) for n in ("x", "e", "u", "t1", "t2"))
        raw = f.ps("raw", [P, 2, 8, H2])
        cum = f.ps("cum", [P, 2, HALF])
        tot = f.ps("tot", [P, 2, HALF])
        c_in, r_done, v_chain, a_chain, cum_done = f.sem("c_in"), f.sem("r_done"), f.sem("v_chain"), f.sem("a_chain"), f.sem("cum_done")
        with nc.Block() as block:
            @block.sync
            def _(sp):
                with nc.allow_non_contiguous_dma(reason="64 columns"):
                    sp.dma_start(w[:, :, :], A["m_in_w"][0][:, c0:c0 + H2].rearrange("(k p) n -> p k n", p=P)).then_inc(c_in, 16)
                sp.dma_start(bias[:, :], row_bcast(A["m_dt_bias"][0].rearrange("a h -> (a h)"))).then_inc(c_in, 16)
                sp.dma_start(al[:, :], row_bcast(A["m_a_log"][0].rearrange("a h -> (a h)"))).then_inc(c_in, 16)

            @block.tensor
            def _(pe):
                pe.wait_ge(c_in, 48)
                for j in range(TT):
                    for k in range(KD):
                        mm = pe.matmul(raw[:, j // 8, j % 8], hT[:, k, j * P:(j + 1) * P], w[:, k], start=(k == 0), stop=(k == KD - 1))
                mm.then_inc(r_done, 1)
                pe.wait_ge(v_chain, 12)
                for d, m in ((0, "le"), (1, "ge")):
                    sl = slice(d * NH, (d + 1) * NH)
                    pe.matmul(cum[:, d, 0:TT * NH].rearrange("p (j h) -> p j h", j=TT), C[m], la[:, :, sl], start=True, stop=True)
                    mm = pe.matmul(tot[:, d, 0:TT * NH].rearrange("p (j h) -> p j h", j=TT), C["ones"], la[:, :, sl], start=True, stop=True)
                mm.then_inc(cum_done, 1)

            @block.vector
            def _(v):
                ch = Chain(v, v_chain)
                v.wait_ge(c_in, 48)
                v.wait_ge(r_done, 1)
                for b, (j0, j1) in enumerate(((0, 8), (8, TT))):
                    ch.done(v.tensor_tensor(x[:, j0:j1], raw[:, b, 0:j1 - j0], bias[:, :].rearrange("p (a h) -> p a h", a=1).to_broadcast([P, j1 - j0, H2]), ALU.add))
                v.wait_ge(a_chain, 3)
                ch.done(v.tensor_scalar(u[:, :, :], e[:, :, :], 1.0, None, ALU.add))
                v.wait_ge(a_chain, 4)
                ch.done(v.scalar_tensor_tensor(out=t2[:, :, :], in0=u[:, :, :], scalar=-1.0, in1=e[:, :, :], op0=ALU.add, op1=ALU.subtract))
                ch.done(v.reciprocal(u[:, :, :], u[:, :, :]))
                ch.done(v.tensor_tensor(t2[:, :, :], t2[:, :, :], u[:, :, :], ALU.mult))
                ch.done(v.tensor_tensor(t1[:, :, :], t1[:, :, :], t2[:, :, :], ALU.subtract))
                ch.done(v.scalar_tensor_tensor(out=dt, in0=x[:, :, :], scalar=0.0, in1=t1[:, :, :], op0=ALU.max, op1=ALU.add))
                ch.done(v.tensor_scalar(al[:, :], al[:, :], -1.0, None, ALU.mult))
                ch.done(v.tensor_tensor(la, dt, al[:, :].rearrange("p (a h) -> p a h", a=1).to_broadcast([P, TT, H2]), ALU.mult))
                ch.done(v.tensor_copy(t2[:, :, :], la))
                ch.done(v.tensor_copy(t2[:, :, :], la))
                v.wait_ge(cum_done, 1)
                for d in range(2):
                    sl = slice(d * NH, (d + 1) * NH)
                    ch.done(v.tensor_copy(x[:, :, sl], cum[:, d, 0:TT * NH].rearrange("p (j h) -> p j h", j=TT)))
                    ch.done(v.tensor_copy(e[:, :, sl], tot[:, d, 0:TT * NH].rearrange("p (j h) -> p j h", j=TT)))
                ch.done(v.tensor_tensor(t1[:, :, :], e[:, :, :], x[:, :, :], ALU.subtract))
                v.wait_ge(a_chain, 5)
                ch.done(v.tensor_tensor(tend, t2[:, :, :], dt, ALU.mult))

            @block.scalar
            def _(act):
                ch = Chain(act, a_chain)
                act.wait_ge(c_in, 48)
                ch.done(act.activation(al[:, :], al[:, :], ACT.Exp))
                act.wait_ge(v_chain, 2)
                ch.done(act.activation(e[:, :, :], x[:, :, :], ACT.Abs))
                ch.done(act.activation(e[:, :, :], e[:, :, :], ACT.Exp, scale=-1.0))
                act.wait_ge(v_chain, 3)
                ch.done(act.activation(t1[:, :, :], u[:, :, :], ACT.Ln))
                act.wait_ge(v_chain, 17)
                ch.done(act.activation(t2[:, :, :], t1[:, :, :], ACT.Exp))
                ch.done(act.activation(ecum, x[:, :, :], ACT.Exp))
                ch.done(act.activation(edec, e[:, :, :], ACT.Exp))


SCAN = [s for k in range(TT) for s in ((0, k), (1, (CT - 1 - k) if k < CT else TT - 1 - (k - CT)))]
PAD = CONV // 2
UW = T + 4 * PAD
LAT0 = CTX + 3 * PAD


def mamba_groups(nc, C, A, S, hT, dt, la, ecum, tend, edec):
    w_in_w = A["m_in_w"][0]
    H2 = 2 * NH
    TILES = 4
    spans = [(0, CTX, PAD), (CTX, CTX + HALF, LAT0), (CTX + HALF, T, LAT0 + HALF)]
    OUTS = [(0, CTX, 0), (LAT0 - PAD, LAT0 - PAD + LAT, CTX)]

    def chan(g, c):
        return (g * GW + c * P, g * GW + c * P, DI + g * NS_, DI + NG * NS_ + g * NS_)[c] if c >= 2 else g * GW + c * P

    with Phase(nc, "mg") as f:
        wx = f.sb("wx", [P, KD, TILES, P])
        wz = f.sb("wz", [P, KD, GW])
        u = f.sb("u", [P, TILES, UW])
        cv = f.sb("cv", [P, TILES, T])
        acc_ = f.sb("ca", [P, UW - 2 * PAD])
        th = f.sb("th", [P, UW - 2 * PAD])
        cw = f.sb("cw", [P, NG * TILES, CONV + 1])
        xt = f.sb("xt", [P, TT, GW])
        bt = f.sb("bt", [P, TT, NS_])
        cb = f.sb("cb", [P, 2, TT, P])
        zr, zt = f.sb("zr", [P, TT, GW]), f.sb("zt", [P, TT, GW])
        yy = f.sb("yy", [P, TT, GW])
        dsk = f.sb("dsk", [P, NH])
        L, E, W = f.sb("L", [P, 2, NHG, P]), f.sb("E", [P, 2, NHG, P]), f.sb("W", [P, 2, NHG, P])
        xd, xe = f.sb("xd", [P, 2, GW]), f.sb("xe", [P, 2, GW])
        st = f.sb("st", [P, 2, GW])
        tmp = f.sb("tmp", [P, GW])
        acc = f.ps("acc", [P, 2, HALF])
        tr = f.ps("tr", [P, HALF])
        seg = f.ps("seg", [P, 2, NHG, P])
        Yp = f.ps("Y", [P, 2, 2, GW])
        Sp = f.ps("S", [P, HALF])
        c_in, wx_in, wz_in = f.sem("c_in"), f.sem("wx_in"), f.sem("wz_in")
        p_mm, u_done, conv_done, z_mm, z_done, zs_done, tr_mm, tr_done = (f.sem(n) for n in ("p_mm", "u_done", "conv_done", "z_mm", "z_done", "zs_done", "tr_mm", "tr_done"))
        cb_mm, cb_done, L_done, seg_mm, E_done, W_done, xe_done, y_mm, s_mm, s_done, y_done = (f.sem(n) for n in ("cb_mm", "cb_done", "L_done", "seg_mm", "E_done", "W_done", "xe_done", "y_mm", "s_mm", "s_done", "y_done"))
        v_chain, a_chain, th_done, g_done, stored, y_init, mt, ca_done = (f.sem(n) for n in ("v_chain", "a_chain", "th_done", "g_done", "stored", "y_init", "mt", "ca_done"))
        n3 = len(spans)
        NSC = len(SCAN)

        with nc.Block() as block:
            @block.sync
            def _(sp):
                with nc.allow_non_contiguous_dma(reason="taps by channel"):
                    for g in range(NG):
                        for c in range(TILES):
                            a = chan(g, c)
                            sp.dma_start(cw[:, g * TILES + c, 0:CONV], A["m_conv_w"][0][:, a:a + P].rearrange("t p -> p t")).then_inc(c_in, 16)
                            sp.dma_start(cw[:, g * TILES + c, CONV:CONV + 1], A["m_conv_b"][0][a:a + P].rearrange("(p a) -> p a", a=1)).then_inc(c_in, 16)
                sp.dma_start(dsk[:, :], row_bcast(A["m_d"][0])).then_inc(c_in, 16)

                def load_x(g):
                    if g >= 1:
                        sp.wait_ge(p_mm, TILES * n3 * g)
                    for c in range(TILES):
                        a = DI + chan(g, c)
                        sp.dma_start(wx[:, :, c], w_in_w[:, a:a + P].rearrange("(k p) n -> p k n", p=P)).then_inc(wx_in, 16)

                def load_z(g):
                    if g >= 1:
                        sp.wait_ge(z_mm, TT * g)
                    sp.dma_start(wz[:, :, :], w_in_w[:, g * GW:(g + 1) * GW].rearrange("(k p) n -> p k n", p=P)).then_inc(wz_in, 16)

                load_x(0)
                load_z(0)
                for g in range(NG):
                    if g + 1 < NG:
                        load_x(g + 1)
                        load_z(g + 1)

            @block.tensor
            def _(pe):
                pa = [0]

                def bank():
                    i = pa[0]
                    pa[0] += 1
                    return i % 2

                hist = []

                def claim(sem, value):
                    if len(hist) >= 2:
                        pe.wait_ge(*hist[-2])
                    hist.append((sem, value))
                    return bank()

                def proj(g, piece):
                    if piece == 0:
                        pe.wait_ge(wx_in, 16 * TILES * (g + 1))
                    c, s = piece // n3, piece % n3
                    a, b, _ = spans[s]
                    i = (g * TILES + c) * n3 + s
                    q = claim(u_done, i + 1)
                    for k in range(KD):
                        mm = pe.matmul(acc[:, q, 0:b - a], wx[:, k, c], hT[:, k, a:b], start=(k == 0), stop=(k == KD - 1))
                    mm.then_inc(p_mm, 1)

                def gate(g):
                    pe.wait_ge(wz_in, 16 * (g + 1))
                    for j in range(TT):
                        q = claim(z_done, g * TT + j + 1)
                        for k in range(KD):
                            mm = pe.matmul(acc[:, q, 0:GW], hT[:, k, j * P:(j + 1) * P], wz[:, k], start=(k == 0), stop=(k == KD - 1))
                        mm.then_inc(z_mm, 1)

                def scan(g):
                    pe.wait_ge(conv_done, TILES * (g + 1))
                    for j in range(TT):
                        i = g * TT + j
                        t = slice(j * P, (j + 1) * P)
                        if i >= 1:
                            pe.wait_ge(cb_done, i)
                        for c in range(3):
                            mm = pe.transpose(tr[:, c * P:(c + 1) * P], cv[:, c, t], C["ident"])
                        mm.then_inc(tr_mm, 1)
                        pe.matmul(tr[:, 3 * P:4 * P], cv[:, 2, t], cv[:, 3, t], start=True, stop=True).then_inc(cb_mm, 1)
                    for k in range(NSC + 1):
                        if k < NSC:
                            d, j = SCAN[k]
                            i = g * NSC + k
                            pe.wait_ge(L_done, i + 1)
                            if i >= 2:
                                pe.wait_ge(E_done, i - 1)
                            for h in range(NHG):
                                mm = pe.matmul(seg[:, i % 2, h], L[:, i % 2, h], C["le" if d == 0 else "ge"], start=True, stop=True)
                            mm.then_inc(seg_mm, 1)
                        if k >= 1:
                            d, j = SCAN[k - 1]
                            i = g * NSC + k - 1
                            pe.wait_ge(W_done, i + 1)
                            if i >= 2:
                                pe.wait_ge(y_done, i - 1)
                            for h in range(NHG):
                                mm = pe.matmul(Yp[:, i % 2, 0, h * HD:(h + 1) * HD], W[:, i % 2, h], xd[:, i % 2, h * HD:(h + 1) * HD], start=True, stop=True)
                            if k - 1 >= 2:
                                pe.wait_ge(s_done, i - 1)
                                mm = pe.matmul(Yp[:, i % 2, 1], cv[:, 3, j * P:(j + 1) * P], st[:, d], start=True, stop=True)
                            mm.then_inc(y_mm, 1)
                            pe.wait_ge(xe_done, i + 1)
                            if i >= 1:
                                pe.wait_ge(s_done, i)
                            pe.matmul(Sp[:, 0:GW], bt[:, j], xe[:, i % 2], start=True, stop=True).then_inc(s_mm, 1)
                        if g + 1 < NG:
                            for piece in pieces_at(k):
                                proj(g + 1, piece)

                for piece in range(PIECES):
                    proj(0, piece)
                gate(0)
                for g in range(NG):
                    scan(g)
                    if g + 1 < NG:
                        gate(g + 1)

            @block.scalar
            def _(act):
                def evict_u(g, piece):
                    c, s = piece // n3, piece % n3
                    a, b, o = spans[s]
                    i = g * PIECES + piece
                    act.wait_ge(p_mm, i + 1)
                    if g >= 1:
                        act.wait_ge(ca_done, (g - 1) * TILES + c + 1)
                    act.copy(u[:, c, o:o + b - a], acc[:, bank_of[("p", i)], 0:b - a]).then_inc(u_done, 1)

                def tanh_conv(g, c):
                    i = g * TILES + c
                    act.wait_ge(ca_done, i + 1)
                    if i >= 1:
                        act.wait_ge(conv_done, i)
                    act.activation(th[:, :], acc_[:, :], ACT.Tanh).then_inc(th_done, 1)

                def gate_in(g, j):
                    i = g * TT + j
                    act.wait_ge(z_mm, i + 1)
                    if g >= 1:
                        act.wait_ge(zs_done, g)
                    q = acc[:, bank_of[("z", i)], 0:GW]
                    act.activation(zt[:, j], q, ACT.Tanh, scale=0.5)
                    act.copy(zr[:, j], q).then_inc(z_done, 1)

                def between(g):
                    for j in range(TT):
                        gate_in(g, j)
                        if j % 2 == 1 and j // 2 < TILES:
                            tanh_conv(g, j // 2)

                def scan(g):
                    for j in range(TT):
                        i = g * TT + j
                        act.wait_ge(tr_mm, i + 1)
                        act.wait_ge(cb_mm, i + 1)
                        if g >= 1 and j == 0:
                            act.wait_ge(s_mm, NSC * g)
                            act.wait_ge(xe_done, NSC * g)
                            act.wait_ge(W_done, NSC * g)
                        act.copy(xt[:, j], tr[:, 0:GW]).then_inc(tr_done, 1)
                        act.copy(bt[:, j], tr[:, GW:GW + NS_]).then_inc(tr_done, 1)
                    for k in range(NSC):
                        i = g * NSC + k
                        act.wait_ge(seg_mm, i + 1)
                        if i >= 2:
                            act.wait_ge(W_done, i - 1)
                        act.activation(E[:, i % 2], seg[:, i % 2], ACT.Exp).then_inc(E_done, 1)
                        if g + 1 < NG:
                            for piece in pieces_at(k):
                                evict_u(g + 1, piece)

                for piece in range(PIECES):
                    evict_u(0, piece)
                between(0)
                for g in range(NG):
                    scan(g)
                    if g + 1 < NG:
                        between(g + 1)

            @block.gpsimd
            def _(p):
                for g in range(NG):
                    p.wait_ge(tr_done, 2 * TT * (g + 1))
                    if g == 0:
                        p.wait_ge(c_in, 16 * (2 * NG * TILES + 1))
                    if g >= 1:
                        p.wait_ge(stored, 16 * TT * g)
                    for j in range(TT):
                        p.tensor_tensor(yy[:, j].rearrange("p (h d) -> p h d", h=NHG), xt[:, j].rearrange("p (h d) -> p h d", h=NHG), dsk[:, g * NHG:(g + 1) * NHG].rearrange("p (h a) -> p h a", a=1).to_broadcast([P, NHG, HD]), ALU.mult).then_inc(y_init, 1)
                    for k in range(NSC):
                        d, j = SCAN[k]
                        i = g * NSC + k
                        if i >= 2:
                            p.wait_ge(seg_mm, i - 1)
                        m = C["gt" if d == 0 else "lt"]
                        p.tensor_tensor(L[:, i % 2], m.rearrange("p (a s) -> p a s", a=1).to_broadcast([P, NHG, P]), la[:, j, d * NH + g * NHG:d * NH + (g + 1) * NHG].rearrange("p (h a) -> p h a", a=1).to_broadcast([P, NHG, P]), ALU.mult).then_inc(L_done, 1)
                    for j in range(TT):
                        p.wait_ge(g_done, g * TT + j + 1)
                        p.dma_start(S["my"][j * P:(j + 1) * P, g * GW:(g + 1) * GW], yy[:, j]).then_inc(stored, 16)
                p.wait_ge(stored, 16 * TT * NG)

            @block.vector
            def _(v):
                ch = Chain(v, v_chain)
                for c in range(TILES):
                    v.memset(u[:, c, 0:PAD], 0.0)
                    v.memset(u[:, c, PAD + CTX:LAT0], 0.0)
                    ch.done(v.memset(u[:, c, UW - PAD:UW], 0.0))
                v.wait_ge(c_in, 16 * (2 * NG * TILES + 1))
                ch.done(v.tensor_scalar(cw[:, :, :], cw[:, :, :], 0.5, None, ALU.mult))
                NW = UW - 2 * PAD

                def conv(g):
                    for c in range(TILES):
                        i = g * TILES + c
                        v.wait_ge(u_done, n3 * (i + 1))
                        w = cw[:, g * TILES + c]
                        ch.done(v.tensor_scalar(acc_[:, :], u[:, c, 0:NW], w[:, 0:1], w[:, CONV:CONV + 1], ALU.mult, ALU.add))
                        for t in range(1, CONV):
                            e = v.scalar_tensor_tensor(out=acc_[:, :], in0=u[:, c, t:t + NW], scalar=w[:, t:t + 1], in1=acc_[:, :], op0=ALU.mult, op1=ALU.add)
                            if t < CONV - 1:
                                ch.done(e)
                        e.then_inc(ca_done, 1)
                        v.wait_ge(ca_done, i + 1)
                        v.wait_ge(th_done, i + 1)
                        if g >= 1 and c == 0:
                            v.wait_ge(s_mm, NSC * g)
                        for a, b, o in OUTS:
                            e = v.scalar_tensor_tensor(out=cv[:, c, o:o + b - a], in0=th[:, a:b], scalar=1.0, in1=acc_[:, a:b], op0=ALU.add, op1=ALU.mult)
                        e.then_inc(conv_done, 1)
                        v.wait_ge(conv_done, i + 1)

                conv(0)
                for g in range(NG):
                    for j in range(TT):
                        i = g * TT + j
                        v.wait_ge(tr_done, 2 * (i + 1))
                        v.tensor_tensor(cb[:, 0, j], tr[:, 3 * P:4 * P], C["le"], ALU.mult)
                        v.tensor_tensor(cb[:, 1, j], tr[:, 3 * P:4 * P], C["ge"], ALU.mult).then_inc(cb_done, 1)
                    v.wait_ge(cb_done, (g + 1) * TT)
                    v.wait_ge(y_init, (g + 1) * TT)

                    def heads(x):
                        return x.rearrange("p (h d) -> p h d", h=NHG)

                    def per_head(x, j, d):
                        return x[:, j, d * NH + g * NHG:d * NH + (g + 1) * NHG].rearrange("p (h a) -> p h a", a=1).to_broadcast([P, NHG, HD])

                    def before(k):
                        d, j = SCAN[k]
                        i = g * NSC + k
                        if i >= 2:
                            v.wait_ge(y_mm, i - 1)
                            v.wait_ge(s_mm, i - 1)
                        v.tensor_tensor(heads(xd[:, i % 2]), heads(xt[:, j]), per_head(dt, j, d), ALU.mult)
                        v.tensor_tensor(heads(xe[:, i % 2]), heads(xt[:, j]), per_head(tend, j, d), ALU.mult).then_inc(xe_done, 1)
                        v.wait_ge(E_done, i + 1)
                        v.tensor_tensor(W[:, i % 2], E[:, i % 2], cb[:, d, j].rearrange("p (a s) -> p a s", a=1).to_broadcast([P, NHG, P]), ALU.mult).then_inc(W_done, 1)

                    def after(k):
                        d, j = SCAN[k]
                        i = g * NSC + k
                        v.wait_ge(s_mm, i + 1)
                        if k < 2:
                            v.tensor_copy(st[:, d], Sp[:, 0:GW]).then_inc(s_done, 1)
                        else:
                            v.wait_ge(y_mm, i + 1)
                            ch.done(v.tensor_tensor(heads(st[:, d]), heads(st[:, d]), per_head(edec, j, d), ALU.mult))
                            v.tensor_tensor(st[:, d], st[:, d], Sp[:, 0:GW], ALU.add).then_inc(s_done, 1)
                        v.wait_ge(s_done, i + 1)
                        v.wait_ge(y_mm, i + 1)
                        if k >= 2:
                            ch.done(v.tensor_tensor(heads(tmp[:, :]), heads(Yp[:, i % 2, 1]), per_head(ecum, j, d), ALU.mult))
                            ch.done(v.tensor_tensor(yy[:, j], yy[:, j], tmp[:, :], ALU.add))
                        v.tensor_tensor(yy[:, j], yy[:, j], Yp[:, i % 2, 0], ALU.add).then_inc(y_done, 1)
                        v.wait_ge(y_done, i + 1)

                    for k in range(NSC + 1):
                        if k < NSC:
                            before(k)
                        if k >= 1:
                            after(k - 1)
                    v.wait_ge(z_done, TT * (g + 1))
                    ch.done(v.scalar_tensor_tensor(out=zt[:, :, :], in0=zt[:, :, :], scalar=1.0, in1=zr[:, :, :], op0=ALU.add, op1=ALU.mult))
                    for j in range(TT):
                        e = v.scalar_tensor_tensor(out=yy[:, j], in0=yy[:, j], scalar=0.5, in1=zt[:, j], op0=ALU.mult, op1=ALU.mult).then_inc(g_done, 1)
                    v.wait_ge(g_done, TT * (g + 1))
                    v.tensor_copy(tmp[:, 0:1], tmp[:, 1:2]).then_inc(zs_done, 1)
                    v.wait_ge(g_done, TT * (g + 1))
                    if g + 1 < NG:
                        conv(g + 1)


PIECES = 12


def pieces_at(k):
    return [p for p in range(PIECES) if p * len(SCAN) // PIECES == k]


def projection_banks():
    order = [("p", i) for i in range(PIECES)] + [("z", j) for j in range(TT)]
    for g in range(1, NG):
        order += [("p", g * PIECES + i) for i in range(PIECES)] + [("z", g * TT + j) for j in range(TT)]
    return {use: n % 2 for n, use in enumerate(order)}


bank_of = projection_banks()


def mamba_layer(nc, C, A, S, hT):
    with ExitStack() as c2:
        dt, la, ecum, tend, edec = (c2.enter_context(nc.sbuf_tensor("m_" + n, [P, TT, 2 * NH], F32))[:, :, :] for n in ("dt", "la", "ecum", "tend", "edec"))
        mamba_steps(nc, C, A, hT, dt, la, ecum, tend, edec)
        mamba_groups(nc, C, A, S, hT, dt, la, ecum, tend, edec)


def project_t(nc, name, hT, w, out):
    K, N = w.shape
    kt, nt, ns = K // P, N // P, LAT // HALF
    with Phase(nc, name) as f:
        wb = f.sb("w", [P, 2, kt, P])
        st = f.sb("st", [P, 4, HALF])
        acc = f.ps("acc", [P, 4, HALF])
        w_in, mm_done, copied, stored = f.sem2("w_in"), f.sem("mm_done"), f.sem2("copied"), f.sem2("stored", 4)
        steps = [(c, s) for c in range(nt) for s in range(ns)]
        with nc.Block() as block:
            @block.sync
            def _(sp):
                for c in range(nt):
                    if c >= 2:
                        sp.wait_ge(mm_done, (c - 1) * ns)
                    sp.dma_start(wb[:, c % 2], w[:, c * P:(c + 1) * P].rearrange("(k p) n -> p k n", p=P)).then_inc(w_in[c % 2], 16)

            @block.tensor
            def _(pe):
                for i, (c, s) in enumerate(steps):
                    pe.wait_ge(w_in[c % 2], 16 * (c // 2 + 1))
                    if i >= 4:
                        pe.wait_ge(copied[i % 2], (i - 4) // 2 + 1)
                    for k in range(kt):
                        mm = pe.matmul(acc[:, i % 4], wb[:, c % 2, k], hT[:, k, s * HALF:(s + 1) * HALF], start=(k == 0), stop=(k == kt - 1))
                    mm.then_inc(mm_done, 1)

            def copy(eng, par):
                for i in range(par, len(steps), 2):
                    eng.wait_ge(mm_done, i + 1)
                    if i >= 4:
                        eng.wait_ge(stored[i % 4], 16 * (i // 4))
                    (eng.copy if par == 0 else eng.tensor_copy)(st[:, i % 4], acc[:, i % 4]).then_inc(copied[par], 1)

            @block.scalar
            def _(act):
                copy(act, 0)

            @block.vector
            def _(v):
                copy(v, 1)

            @block.gpsimd
            def _(g):
                for i, (c, s) in enumerate(steps):
                    g.wait_ge(copied[i % 2], i // 2 + 1)
                    g.dma_start(out[c * P:(c + 1) * P, s * HALF:(s + 1) * HALF], st[:, i % 4]).then_inc(stored[i % 4], 16)
                for s in range(4):
                    g.wait_ge(stored[s], 16 * len(range(s, len(steps), 4)))


def rope_tables(nc, C, A, cos, sin):
    ROUND = 1.5 * 2.0 ** 23
    TWO_PI = (6.28125, 0.00193500518798828125, 3.0199159819e-07)
    with Phase(nc, "rope") as f:
        pi = f.sb("pi", [P, LT], I32)
        pf = f.sb("pf", [P, LT])
        a, k, h = f.sb("a", [P, LT, 16]), f.sb("k", [P, LT, 16]), f.sb("h", [P, LT, 16])
        p_in, v_chain, s_done = f.sem("p_in"), f.sem("v_chain"), f.sem("s_done")
        with nc.Block() as block:
            @block.sync
            def _(sp):
                with nc.allow_non_contiguous_dma(reason="positions by token"):
                    sp.dma_start(pi[:, :], A["positions_2"][0].rearrange("(j p) -> p j", p=P)).then_inc(p_in, 16)

            @block.vector
            def _(v):
                ch = Chain(v, v_chain)
                v.wait_ge(p_in, 16)
                ch.done(v.tensor_copy(pf[:, :], pi[:, :]))
                ch.done(v.tensor_tensor(a[:, :, :], pf[:, :].rearrange("p (j o) -> p j o", o=1).to_broadcast([P, LT, 16]), C["inv2"].rearrange("p (o q) -> p o q", o=1).to_broadcast([P, LT, 16]), ALU.mult))
                ch.done(v.tensor_scalar(k[:, :, :], a[:, :, :], 1.0 / (2.0 * np.pi), None, ALU.mult))
                ch.done(v.tensor_scalar(k[:, :, :], k[:, :, :], ROUND, None, ALU.add))
                ch.done(v.tensor_scalar(k[:, :, :], k[:, :, :], -ROUND, None, ALU.add))
                for c in TWO_PI:
                    ch.done(v.scalar_tensor_tensor(out=a[:, :, :], in0=k[:, :, :], scalar=-c, in1=a[:, :, :], op0=ALU.mult, op1=ALU.add))
                ch.done(v.tensor_scalar(a[:, :, :], a[:, :, :], 3.1415925, -3.1415925, ALU.min, ALU.max))
                v.wait_ge(s_done, 2)
                ch.done(v.tensor_tensor(h[:, :, :], h[:, :, :], h[:, :, :], ALU.mult))
                ch.done(v.tensor_scalar(cos, h[:, :, :], -2.0, 1.0, ALU.mult, ALU.add))

            @block.scalar
            def _(act):
                act.wait_ge(v_chain, 9)
                act.activation(sin, a[:, :, :], ACT.Sin).then_inc(s_done, 1)
                act.activation(h[:, :, :], a[:, :, :], ACT.Sin, scale=0.5).then_inc(s_done, 1)


HH = 4
LEV = 7


def recurrence(nc, C, A, S, masks):
    combos = [(h, d) for h in range(HH) for d in range(2)]
    NC = len(combos)
    with Phase(nc, "hg") as f:
        lg, lb, ol, oh = f.sb("lg", [P, 2, 2, HH]), f.sb("lb", [P, 2, HH]), f.sb("ol", [P, 2, HH]), f.sb("oh", [P, 2, HH])
        qr, qs = f.sb("qr", [P, 2, LAT]), f.sb("qs", [P, 2, LAT])
        z, k_, b_ = f.sb("z", [P, 2, LAT]), f.sb("k", [P, 2, LAT]), f.sb("b", [P, 2, LAT])
        t1 = f.sb("t1", [P, LAT])
        rst = f.sb("rst", [P, 2, LAT])
        qb = f.sb("qb", [P, 2, LAT])
        X = f.sb("X", [P, 2, LEV + 1, LAT])
        kt = f.sb("kt", [P, LT, P])
        vv = f.sb("v", [P, LT, HH * P])
        M = f.sb("M", [P, 2, LEV + 1, P])
        st = f.sb("st", [P, P])
        eb = f.sb("eb", [P, 2, LT])
        o = f.sb("o", [P, 2, LT, P])
        Aps = f.ps("A", [P, 2, LEV + 1, P])
        Ops = f.ps("O", [P, 2, HALF])
        Sps = f.ps("S", [P, HALF])
        Tps = f.ps("T", [P, 4, P])
        c_in, q_in, z_in, z2_in = f.sem("c_in"), f.sem2("q_in"), f.sem2("z_in"), f.sem("z2_in")
        a_step, v_step, dl_done, x_exp, x_done, k_mm, k_ev = (f.sem(n) for n in ("a_step", "v_step", "dl_done", "x_exp", "x_done", "k_mm", "k_ev"))
        l_mm, m_done, o_mm, s_mm, s_done, o_done, stored, init = (f.sem(n) for n in ("l_mm", "m_done", "o_mm", "s_mm", "s_done", "o_done", "stored", "init"))
        b_done, g_done, lbe = f.sem("b_done"), f.sem("g_done"), f.sem("lbe")
        order = [list(range(LT)), list(range(LT - 1, -1, -1))]

        with nc.Block() as block:
            @block.sync
            def _(sp):
                with nc.allow_non_contiguous_dma(reason="logits by channel"):
                    for l in range(2):
                        for d in range(2):
                            sp.dma_start(lg[:, l, d], col_view(A["hg_lb_logits_2"][l, d], HH)).then_inc(c_in, 16)
                for c, (h, d) in enumerate(combos):
                    if d == 0:
                        if h >= 2:
                            sp.wait_ge(v_step, 10 * (h - 1))
                        sp.dma_start(qr[:, h % 2], S["hfT"][h * P:(h + 1) * P, :]).then_inc(q_in[h % 2], 16)
                    if c >= 2:
                        sp.wait_ge(a_step, 6 * (c - 2) + 4)
                    r = HH * P * (d + 1) + h * P
                    sp.dma_start(z[:, c % 2], S["hfT"][r:r + P, :]).then_inc(z_in[c % 2], 16)
                    if c == 0:
                        sp.dma_start(vv[:, :, :], S["hih"][:, 0:HH * P].rearrange("(j p) n -> p j n", p=P)).then_inc(z2_in, 16)
                for h in range(HH):
                    sp.wait_ge(o_done, 2 * LT * (h + 1))
                    sp.dma_start(S["ho"][:, h * P:(h + 1) * P].rearrange("(j p) n -> p j n", p=P), o[:, h % 2]).then_inc(stored, 16)
                    sp.wait_ge(stored, 16 * (h + 1))

            @block.scalar
            def _(act):
                ch = Chain(act, a_step)
                act.wait_ge(init, 1)
                act.activation(lb[:, :, :], lb[:, :, :], ACT.Exp, scale=-1.0).then_inc(lbe, 1)
                act.activation(ol[:, :, :], ol[:, :, :], ACT.Exp).then_inc(lbe, 1)

                def prep_decay(c):
                    act.wait_ge(z_in[c % 2], 16 * (c // 2 + 1))
                    if c >= 1:
                        act.wait_ge(b_done, c)
                    ch.done(act.activation(t1[:, :], z[:, c % 2], ACT.Exp, scale=-1.0))
                    ch.done(act.activation(t1[:, :], t1[:, :], ACT.Identity, bias=C["ones"][:, 0:1]))

                def prep_qk(c):
                    h, d = combos[c]
                    act.wait_ge(q_in[h % 2], 16 * (h // 2 + 1))
                    if c >= 2:
                        act.wait_ge(o_mm, LT * (c - 1))
                    ch.done(act.activation(qb[:, c % 2], qr[:, h % 2], ACT.Tanh, scale=0.5))
                    if c >= 2:
                        act.wait_ge(x_done, (LEV + 1) * (c - 1))
                    ch.done(act.activation(k_[:, c % 2], z[:, c % 2], ACT.Exp))
                    ch.done(act.activation(k_[:, c % 2], k_[:, c % 2], ACT.Identity, bias=C["ones"][:, 0:1]))
                    act.wait_ge(v_step, 5 * c + 2)
                    ch.done(act.activation(t1[:, :], t1[:, :], ACT.Ln))

                def exps(c):
                    act.wait_ge(b_done, c + 1)
                    act.wait_ge(v_step, 5 * c + 5)
                    act.activation(qb[:, c % 2], b_[:, c % 2], ACT.Exp).then_inc(g_done, 1)
                    d = combos[c][1]
                    e = (P - 1) if d == 0 else 0
                    act.activation(eb[:, c % 2], b_[:, c % 2].rearrange("p (j t) -> p j t", t=P)[:, :, e], ACT.Exp).then_inc(g_done, 1)
                    for l in range(LEV + 1):
                        act.wait_ge(dl_done, (LEV + 1) * c + l + 1)
                        act.activation(X[:, c % 2, l], X[:, c % 2, l], ACT.Exp).then_inc(x_exp, 1)

                def turned(c):
                    for g in range(2):
                        i = 2 * c + g
                        act.wait_ge(k_mm, i + 1)
                        if c >= 1:
                            act.wait_ge(s_mm, LT * c)
                        act.copy(kt[:, 4 * g:4 * g + 4], Tps[:, :, :]).then_inc(k_ev, 1)

                prep_decay(0)
                prep_qk(0)
                exps(0)
                for c in range(NC):
                    if c + 1 < NC:
                        prep_decay(c + 1)
                    turned(c)
                    if c + 1 < NC:
                        prep_qk(c + 1)
                        exps(c + 1)

            @block.gpsimd
            def _(g):
                for c in range(NC):
                    h, d = combos[c]
                    g.wait_ge(b_done, c + 1)
                    if c >= 2:
                        g.wait_ge(l_mm, LT * (c - 1))
                        g.wait_ge(k_mm, 2 * (c - 1))
                    for l in range(LEV):
                        m = 1 << l
                        bv = b_[:, c % 2].rearrange("p (n t) -> p n t", t=2 * m)
                        xv = X[:, c % 2, l].rearrange("p (n t) -> p n t", t=2 * m)
                        r = m - 1 if d == 0 else m
                        ref = bv[:, :, r:r + 1].to_broadcast([P, LAT // (2 * m), m])
                        lo, hi = (ref, bv[:, :, 0:m]), (bv[:, :, m:2 * m], ref)
                        if d == 1:
                            lo, hi = lo[::-1], hi[::-1]
                        g.tensor_tensor(xv[:, :, 0:m], lo[0], lo[1], ALU.subtract)
                        g.tensor_tensor(xv[:, :, m:2 * m], hi[0], hi[1], ALU.subtract).then_inc(dl_done, 1)
                    bv = b_[:, c % 2].rearrange("p (n t) -> p n t", t=P)
                    e = P - 1 if d == 0 else 0
                    g.tensor_tensor(X[:, c % 2, LEV].rearrange("p (n t) -> p n t", t=P), bv[:, :, e:e + 1].to_broadcast([P, LT, P]), bv, ALU.subtract).then_inc(dl_done, 1)

            @block.vector
            def _(v):
                ch = Chain(v, v_step)
                v.wait_ge(c_in, 64)
                v.tensor_tensor(lb[:, :, :], lg[:, 0], lg[:, 1], ALU.subtract)
                v.tensor_tensor(ol[:, :, :], lg[:, 0], lg[:, 1], ALU.subtract).then_inc(init, 1)
                v.wait_ge(lbe, 2)
                for x in (lb, ol):
                    v.tensor_scalar(x[:, :, :], x[:, :, :], 1.0, None, ALU.add).then_inc(init, 1)
                v.wait_ge(init, 3)
                for x in (lb, ol):
                    v.reciprocal(x[:, :, :], x[:, :, :]).then_inc(init, 1)
                v.wait_ge(init, 5)
                v.tensor_scalar(oh[:, :, :], ol[:, :, :], 0.5, None, ALU.mult).then_inc(init, 1)
                for d in range(2):
                    v.memset(rst[:, d], 1.0).then_inc(init, 1)
                v.wait_ge(init, 8)
                v.memset(rst[:, 0].rearrange("p (j t) -> p j t", t=P)[:, :, 0:1], 0.0).then_inc(init, 1)
                v.memset(rst[:, 1].rearrange("p (j t) -> p j t", t=P)[:, :, P - 1:P], 0.0).then_inc(init, 1)
                v.wait_ge(init, 10)

                def decay(c):
                    h, d = combos[c]
                    v.wait_ge(a_step, 6 * c + 2)
                    ch.done(v.reciprocal(t1[:, :], t1[:, :]))
                    ch.done(v.tensor_scalar(t1[:, :], t1[:, :], ol[:, d, h:h + 1], lb[:, d, h:h + 1], ALU.mult, ALU.add))

                def keys(c):
                    h, d = combos[c]
                    kk = k_[:, c % 2]
                    v.wait_ge(a_step, 6 * c + 5)
                    ch.done(v.reciprocal(kk, kk))
                    ch.done(v.tensor_scalar(kk, kk, oh[:, d, h:h + 1], None, ALU.mult))

                def queries(c):
                    h, d = combos[c]
                    if c >= 2:
                        v.wait_ge(l_mm, LT * (c - 1))
                    ch.done(v.scalar_tensor_tensor(out=qs[:, c % 2], in0=qb[:, c % 2], scalar=1.0, in1=qr[:, h % 2], op0=ALU.add, op1=ALU.mult))
                    v.wait_ge(a_step, 6 * c + 6)
                    if c >= 2:
                        v.wait_ge(dl_done, (LEV + 1) * (c - 1))
                        v.wait_ge(g_done, 2 * (c - 1))
                    s = slice(None) if d == 0 else slice(None, None, -1)
                    v.tensor_tensor_scan(b_[:, c % 2][:, s], rst[:, d][:, s], t1[:, s], 0.0, ALU.mult, ALU.add).then_inc(b_done, 1)

                def weigh(c, l):
                    h, d = combos[c]
                    v.wait_ge(x_exp, (LEV + 1) * c + l + 1)
                    if l == LEV:
                        v.tensor_tensor(X[:, c % 2, LEV], X[:, c % 2, LEV], k_[:, c % 2], ALU.mult).then_inc(x_done, 1)
                        return
                    m = 1 << l
                    xv, kv, qv = (a.rearrange("p (n t) -> p n t", t=2 * m) for a in (X[:, c % 2, l], k_[:, c % 2], qs[:, c % 2]))
                    lo, hi = (kv, qv) if d == 0 else (qv, kv)
                    v.tensor_tensor(xv[:, :, 0:m], xv[:, :, 0:m], lo[:, :, 0:m], ALU.mult)
                    v.tensor_tensor(xv[:, :, m:2 * m], xv[:, :, m:2 * m], hi[:, :, m:2 * m], ALU.mult).then_inc(x_done, 1)

                def weigh_queries(c):
                    v.wait_ge(g_done, 2 * (c + 1))
                    v.tensor_tensor(qb[:, c % 2], qb[:, c % 2], qs[:, c % 2], ALU.mult)

                DECAY, KEYS, QUERIES, WEIGH_Q = -4, -3, -2, -1
                WITH = [[DECAY], [KEYS], [QUERIES], [], [0], [WEIGH_Q, 1, 2], [3, 4], [5, 6], [7]]

                def ahead(c, what):
                    if what == DECAY:
                        decay(c)
                    elif what == KEYS:
                        keys(c)
                    elif what == QUERIES:
                        queries(c)
                    elif what == WEIGH_Q:
                        weigh_queries(c)
                    else:
                        weigh(c, what)

                def chunks(c):
                    h, d = combos[c]
                    for n in range(LT + 1):
                        if n < LT:
                            i = c * LT + n
                            v.wait_ge(l_mm, i + 1)
                            if i >= 2:
                                v.wait_ge(o_mm, i - 1)
                            for half in range(2):
                                sl = slice(4 * half, 4 * half + 4)
                                e = v.tensor_tensor(M[:, i % 2, sl], Aps[:, i % 2, sl], masks[d].rearrange("p (l t) -> p l t", t=P)[:, sl], ALU.mult)
                            e.then_inc(m_done, 1)
                        if n >= 1:
                            i = c * LT + n - 1
                            j = order[d][n - 1]
                            v.wait_ge(s_mm, i + 1)
                            v.wait_ge(o_mm, i + 1)
                            if n == 1:
                                v.tensor_copy(st[:, :], Sps[:, 0:P]).then_inc(s_done, 1)
                            else:
                                v.scalar_tensor_tensor(out=st[:, :], in0=st[:, :], scalar=eb[:, c % 2, j:j + 1], in1=Sps[:, 0:P], op0=ALU.mult, op1=ALU.add).then_inc(s_done, 1)
                            v.wait_ge(s_done, i + 1)
                            if d == 0:
                                if h >= 2:
                                    v.wait_ge(stored, 16 * (h - 1))
                                v.tensor_copy(o[:, h % 2, j], Ops[:, i % 2, 0:P]).then_inc(o_done, 1)
                            else:
                                v.wait_ge(o_done, c * LT)
                                v.tensor_tensor(o[:, h % 2, j], o[:, h % 2, j], Ops[:, i % 2, 0:P], ALU.add).then_inc(o_done, 1)
                        if c + 1 < NC:
                            for what in WITH[n]:
                                ahead(c + 1, what)

                for step in WITH:
                    for what in step:
                        ahead(0, what)
                for c in range(NC):
                    chunks(c)

            @block.tensor
            def _(pe):
                pe.wait_ge(z2_in, 16)
                for c in range(NC):
                    h, d = combos[c]
                    pe.wait_ge(x_done, (LEV + 1) * (c + 1))
                    for g in range(2):
                        if 2 * c + g >= 1:
                            pe.wait_ge(k_ev, 2 * c + g)
                        for u in range(4):
                            j = 4 * g + u
                            mm = pe.transpose(Tps[:, u], X[:, c % 2, LEV, j * P:(j + 1) * P], C["ident"])
                        mm.then_inc(k_mm, 1)
                    for n in range(LT + 1):
                        if n < LT:
                            i, j = c * LT + n, order[d][n]
                            t = slice(j * P, (j + 1) * P)
                            if i >= 2:
                                pe.wait_ge(m_done, i - 1)
                            pe.matmul(Aps[:, i % 2, 0], k_[:, c % 2, t], qs[:, c % 2, t], start=True, stop=True)
                            for l in range(LEV):
                                mm = pe.matmul(Aps[:, i % 2, l + 1], X[:, c % 2, l, t], X[:, c % 2, l, t], start=True, stop=True)
                            mm.then_inc(l_mm, 1)
                        if n >= 1:
                            i, j = c * LT + n - 1, order[d][n - 1]
                            t = slice(j * P, (j + 1) * P)
                            pe.wait_ge(m_done, i + 1)
                            if i >= 2:
                                pe.wait_ge(o_done, i - 1)
                            vj = vv[:, j, h * P:(h + 1) * P]
                            for l in range(LEV + 1):
                                mm = pe.matmul(Ops[:, i % 2, 0:P], M[:, i % 2, l], vj, start=(l == 0), stop=(l == LEV and n == 1))
                            if n >= 2:
                                pe.wait_ge(s_done, i)
                                mm = pe.matmul(Ops[:, i % 2, 0:P], qb[:, c % 2, t], st[:, :], start=False, stop=True)
                            mm.then_inc(o_mm, 1)
                            pe.wait_ge(k_ev, 2 * (c + 1))
                            if i >= 1:
                                pe.wait_ge(s_done, i)
                            pe.matmul(Sps[:, 0:P], kt[:, j], vj, start=True, stop=True).then_inc(s_mm, 1)


def mixer_layer(nc, C, A, S):
    w = A["w_in_2"][0]
    QR, KR, RD, MH, QK = 192, 128, 32, 8, 96
    with ExitStack() as c1:
        hT = c1.enter_context(nc.sbuf_tensor("h2T", [P, KD, LAT], F32))
        norm_turn(nc, "n2", C, [(S["h2"][i * P:(i + 1) * P, :], 0, i * P) for i in range(LT)], [(A["norm_mix_2"][0], None, None)], hT,
                  first=(A["final_norm_w"], S["x1"]))
        cols = [i * P for i in range(LT)]
        project(nc, "w_a", hT, cols, w[:, 0:352], S["pa"])
        project_t(nc, "w_f", hT, w[:, 352:1888], S["hfT"])
        project(nc, "w_i", hT, cols, w[:, 1888:2912], S["hih"])
    with ExitStack() as c1:
        mask = c1.enter_context(nc.sbuf_tensor("levels", [P, 2, (LEV + 1) * P], F32))
        move(nc, "lv", [(mask[:, :, :], A["levels"].rearrange("p (d n) -> p d n", d=2))])
        recurrence(nc, C, A, S, [mask[:, 0], mask[:, 1]])
    with ExitStack() as c1:
        hoT = c1.enter_context(nc.sbuf_tensor("hoT", [P, HH, LAT], F32))
        turn_heads(nc, "h_o", C, LT, HH, P, lambda i: [(0, HH, 0, P, S["ho"][i * P:(i + 1) * P, :].rearrange("p (h d) -> p h d", h=HH))],
                   A["hg_o_norm_2"][0], [(b * P, P, [((0, P), (lambda b: lambda i: hoT[:, b, i * P:(i + 1) * P])(b))]) for b in range(HH)],
                   gate=lambda i: S["hih"][i * P:(i + 1) * P, HH * P:2 * HH * P].rearrange("p (h d) -> p h d", h=HH))
        move(nc, "h_s", [(S["mixT"][HH * P:2 * HH * P, :].rearrange("(k p) t -> p k t", p=P), hoT[:, :, :])])
    with ExitStack() as c1:
        sb = lambda name, shape: c1.enter_context(nc.sbuf_tensor(name, shape, F32))
        cos, sin = sb("cos", [P, LT, 16]), sb("sin", [P, LT, 16])
        rope_tables(nc, C, A, cos[:, :, :], sin[:, :, :])
        qT, kT, vv = sb("mqT", [P, MH, LAT]), sb("mkT", [P, MH, LAT]), sb("mv", [P, LT, MH * 64])
        rot = sb("rot", [P, LT, RD])
        with ExitStack() as c2:
            cq, ckv = (c2.enter_context(nc.sbuf_tensor(x, [P, k, LAT], F32)) for x, k in (("cq", 2), ("ckv", 1)))
            move(nc, "m_r", [(rot[:, :, :], S["pa"][:, QR + KR:QR + KR + RD].rearrange("(j p) c -> p j c", p=P))], [qT[:, :, :], kT[:, :, :]])
            turn_heads(nc, "cq", C, LT, 1, QR, lambda i: [(0, 1, 0, QR, S["pa"][i * P:(i + 1) * P, 0:QR].rearrange("p (a d) -> p a d", a=1))], A["mla_q_a_norm_2"][0],
                       [(0, P, [((0, P), lambda i: cq[:, 0, i * P:(i + 1) * P])]), (P, 64, [((0, 64), lambda i: cq[0:64, 1, i * P:(i + 1) * P])])])
            turn_heads(nc, "ckv", C, LT, 1, KR, lambda i: [(0, 1, 0, KR, S["pa"][i * P:(i + 1) * P, QR:QR + KR].rearrange("p (a d) -> p a d", a=1))], A["mla_kv_a_norm_2"][0],
                       [(0, P, [((0, P), lambda i: ckv[:, 0, i * P:(i + 1) * P])])])
            tab = lambda j: (cos[:, j], sin[:, j])
            put = lambda t: lambda c, j, g: t[0:QK, 4 * c:4 * c + 4, j * P:(j + 1) * P]
            project_heads(nc, "m_q", C, cq, cols, A["mla_w_q_up_2"][0], QK, 4 * QK, A["mla_q_norm_2"][0], put(qT), rope=(64, 1, tab))
            project_heads(nc, "m_k", C, ckv, cols, A["mla_w_kv_up_2"][0], QK, 4 * P, A["mla_k_norm_2"][0], put(kT), rope=(64, 1, tab),
                          extra=rot[:, :, :], values=lambda c, j: vv[:, j, 4 * c * 64:4 * (c + 1) * 64].rearrange("p (h d) -> p h d", h=4))
        attend(nc, "m_at", C, [([(qT[:, h], kT[:, h])], [((lambda h: lambda k: vv[:, k, h * 64:(h + 1) * 64])(h), 64)], [S["mixT"][h * 64:(h + 1) * 64, :]]) for h in range(MH)],
               LT, LAT, QK ** -0.5)
    out_project_t(nc, "w_out", C, S["mixT"], A["w_out_2"][0], LT, S["x1"], S["x2"])


def cross_layer(nc, C, A, S):
    M, XH, XD = 256, 4, 256
    MT = M // P
    with ExitStack() as c1:
        sb = lambda name, shape: c1.enter_context(nc.sbuf_tensor(name, shape, F32))
        qT, kT, vv = sb("xqT", [P, 2 * XH, LAT]), sb("xkT", [P, 2 * XH, M]), sb("xv", [P, MT, D])
        with ExitStack() as c2:
            hT = c2.enter_context(nc.sbuf_tensor("h3T", [P, KD, LAT], F32))
            mT = c2.enter_context(nc.sbuf_tensor("memT", [P, KD, M], F32))
            norm_turn(nc, "n3", C, [(S["x2"][i * P:(i + 1) * P, :], 0, i * P) for i in range(LT)], [(A["norm_cross_2"][0], None, None)], hT)
            norm_turn(nc, "n4", C, [(A["mem_2"][0, i * P:(i + 1) * P, :], 0, i * P) for i in range(MT)], [(A["norm_mem_2"][0], None, None)], mT)
            by_tile = lambda t: lambda c, j, g: t[:, 4 * c:4 * c + 4, j * P:(j + 1) * P]
            project_heads(nc, "x_q", C, hT, [i * P for i in range(LT)], A["x_w_q_2"][0], XD, 2 * XD, A["x_q_norm_2"][0], by_tile(qT))
            project_heads(nc, "x_k", C, mT, [i * P for i in range(MT)], A["x_w_kv_2"][0][:, 0:D], XD, 2 * XD, A["x_k_norm_2"][0], by_tile(kT))
            project(nc, "x_v", mT, [i * P for i in range(MT)], A["x_w_kv_2"][0][:, D:2 * D], put=lambda j, a, b: vv[:, j, a:b])
        attend(nc, "x_at", C, [([(qT[:, 2 * h + u], kT[:, 2 * h + u]) for u in range(2)],
                                [((lambda h, u: lambda k: vv[:, k, h * XD + u * P:h * XD + (u + 1) * P])(h, u), P) for u in range(2)],
                                [S["xoT"][h * XD + u * P:h * XD + (u + 1) * P, :] for u in range(2)]) for h in range(XH)],
               LT, M, XD ** -0.5)
    out_project_t(nc, "x_out", C, S["xoT"], A["x_w_o_2"][0], LT, S["x2"], S["x3"])


EG, EE = 8, 8
NE = EG * EE
HID = 256
NBLK = 2 * LAT // P + NE
NONE = 5000


def route(nc, C, A, S, hT, wts):
    with Phase(nc, "route") as f:
        w = f.sb("w", [P, KD, EG + NE])
        bias = f.sb("bias", [P, EG + NE])
        lg = f.sb("lg", [P, LT, EG + NE])
        gm, gs, gd = f.sb("gm", [P, LT]), f.sb("gs", [P, LT]), f.sb("gd", [P, LT])
        g8, oh, e8, e8b = (f.sb(n, [P, LT, 8]) for n in ("g8", "oh", "e8", "e8b"))
        pr = f.sb("pr", [P, LT, EE, EG])
        m1, m2, i1, i2, ex = (f.sb(n, [P, LT]) for n in ("m1", "m2", "i1", "i2", "ex"))
        A1, A2, AA, AC, sl = (f.sb(n, [P, LT, NE]) for n in ("A1", "A2", "AA", "AC", "sl"))
        cnt, nb, pend, ps_, one = (f.sb(n, [P, NE]) for n in ("cnt", "nb", "pend", "pst", "one"))
        be, bei = f.sb("be", [P, 1]), f.sb("bei", [P, 1], I32)
        dst = f.sb("dst", [P, 2, LT])
        dsti = f.sb("dsti", [P, 2, LT], U32)
        info = f.sb("info", [P, LT, 2, 2], U32)
        none = f.sb("none", [P, NBLK * 2], U32)
        raw = f.ps("raw", [P, 2, 4, P])
        rank = f.ps("rank", [P, LT, NE])
        tot = f.ps("tot", [P, HALF])
        c_in, r_done, v_chain, a_chain, p_chain, cnt_done, init, done = (f.sem(n) for n in ("c_in", "r_done", "v_chain", "a_chain", "p_chain", "cnt_done", "init", "done"))
        iota8 = C["iota64"][:, 0:8].rearrange("p (o e) -> p o e", o=1).to_broadcast([P, LT, 8])
        col = lambda x, n: x[:, :].rearrange("p (j o) -> p j o", o=1).to_broadcast([P, LT, n])
        N_ASSIGN, N_ALL = [0], [0]
        with nc.Block() as block:
            @block.vector
            def _(v):
                ch = Chain(v, v_chain)
                v.wait_ge(c_in, 64)
                v.wait_ge(r_done, 1)
                for b in range(2):
                    ch.done(v.tensor_tensor(lg[:, 4 * b:4 * b + 4], raw[:, b, :, 0:EG + NE], bias[:, :].rearrange("p (o n) -> p o n", o=1).to_broadcast([P, 4, EG + NE]), ALU.add))
                g = lg[:, :, 0:EG]

                def first_max(x, m, idx, eq):
                    ch.done(v.tensor_reduce(m[:, :], x, AX.X, ALU.max))
                    ch.done(v.tensor_tensor(eq, x, col(m, 8), ALU.is_equal))
                    ch.done(v.scalar_tensor_tensor(out=eq, in0=eq, scalar=-64.0, in1=iota8, op0=ALU.mult, op1=ALU.add))
                    ch.done(v.tensor_reduce(idx[:, :], eq, AX.X, ALU.min))
                    ch.done(v.tensor_scalar(idx[:, :], idx[:, :], 64.0, None, ALU.add))

                first_max(g, gm, gs, g8[:, :, :])
                ch.done(v.tensor_tensor(g8[:, :, :], g, col(gm, 8), ALU.subtract))
                at_g = ch.n
                ch.done(v.tensor_tensor(oh[:, :, :], iota8, col(gs, 8), ALU.is_equal))
                for j in range(LT):
                    e = v.tensor_tensor(pr[:, j], lg[:, j, EG:].rearrange("p (g e) -> p e g", g=EG), oh[:, j].rearrange("p (o g) -> p o g", o=1).to_broadcast([P, EE, EG]), ALU.mult)
                ch.done(e)
                ch.done(v.tensor_reduce(e8[:, :, :], pr[:, :, :, :], AX.X, ALU.add))
                first_max(e8[:, :, :], m1, i1, e8b[:, :, :])
                ch.done(v.tensor_tensor(e8b[:, :, :], iota8, col(i1, 8), ALU.is_equal))
                ch.done(v.scalar_tensor_tensor(out=e8[:, :, :], in0=e8b[:, :, :], scalar=-1e30, in1=e8[:, :, :], op0=ALU.mult, op1=ALU.add))
                first_max(e8[:, :, :], m2, i2, e8b[:, :, :])
                ch.done(v.tensor_tensor(ex[:, :], m2[:, :], m1[:, :], ALU.subtract))
                at_e = ch.n
                v.wait_ge(a_chain, 2)
                ch.done(v.tensor_reduce(gd[:, :], g8[:, :, :], AX.X, ALU.add))
                ch.done(v.tensor_scalar(m1[:, :], ex[:, :], 1.0, None, ALU.add))
                ch.done(v.tensor_tensor(m1[:, :], m1[:, :], gd[:, :], ALU.mult))
                ch.done(v.reciprocal(wts[:, :, 0], m1[:, :]))
                ch.done(v.tensor_tensor(wts[:, :, 1], wts[:, :, 0], ex[:, :], ALU.mult))
                ch.done(v.scalar_tensor_tensor(out=i1[:, :], in0=gs[:, :], scalar=float(EE), in1=i1[:, :], op0=ALU.mult, op1=ALU.add))
                ch.done(v.scalar_tensor_tensor(out=i2[:, :], in0=gs[:, :], scalar=float(EE), in1=i2[:, :], op0=ALU.mult, op1=ALU.add))
                i64 = C["iota64"].rearrange("p (o e) -> p o e", o=1).to_broadcast([P, LT, NE])
                ch.done(v.tensor_tensor(A1[:, :, :], i64, col(i1, NE), ALU.is_equal))
                ch.done(v.tensor_tensor(A2[:, :, :], i64, col(i2, NE), ALU.is_equal))
                ch.done(v.tensor_tensor(AA[:, :, :], A1[:, :, :], A2[:, :, :], ALU.add))
                ch.done(v.memset(AC[:, 0], 0.0))
                for j in range(1, LT):
                    ch.done(v.tensor_tensor(AC[:, j], AC[:, j - 1], AA[:, j - 1], ALU.add))
                ch.done(v.tensor_tensor(sl[:, 0], AC[:, LT - 1], AA[:, LT - 1], ALU.add))
                at_c = ch.n
                v.wait_ge(cnt_done, 1)
                ch.done(v.tensor_copy(cnt[:, :], tot[:, 0:NE]))
                ch.done(v.tensor_scalar(nb[:, :], cnt[:, :], 0.0, None, ALU.is_gt))
                for j in range(1, LAT // P):
                    ch.done(v.scalar_tensor_tensor(out=nb[:, :], in0=cnt[:, :], scalar=float(P * j), in1=nb[:, :], op0=ALU.is_gt, op1=ALU.add))
                ch.done(v.memset(one[:, :], 1.0))
                ch.done(v.tensor_tensor_scan(pend[:, :], one[:, :], nb[:, :], 0.0, ALU.mult, ALU.add))
                ch.done(v.tensor_tensor(ps_[:, :], pend[:, :], nb[:, :], ALU.subtract))
                ch.done(v.tensor_scalar(ps_[:, :], ps_[:, :], float(P), None, ALU.mult))
                ch.done(v.tensor_tensor(sl[:, :, :], rank[:, :, :], ps_[:, :].rearrange("p (o e) -> p o e", o=1).to_broadcast([P, LT, NE]), ALU.add))
                for k, a in enumerate((A1, A2)):
                    ch.done(v.tensor_tensor(a[:, :, :], a[:, :, :], sl[:, :, :], ALU.mult))
                    ch.done(v.tensor_reduce(dst[:, k], a[:, :, :], AX.X, ALU.add))
                ch.done(v.tensor_copy(dsti[:, :, :], dst[:, :, :]))
                ch.done(v.tensor_scalar(one[:, :], pend[:, :], C["pidx"], None, ALU.is_le))
                ch.done(v.tensor_reduce(be[:, :], one[:, :], AX.X, ALU.add))
                ch.done(v.tensor_scalar(be[:, :], be[:, :], float(NE - 1), None, ALU.min))
                ch.done(v.tensor_copy(bei[:, :], be[:, :]))
                N_ALL[0] = ch.n
                N_ASSIGN[0] = (at_g, at_e, at_c)

            at_g, at_e, at_c = N_ASSIGN[0]

            @block.scalar
            def _(act):
                ch = Chain(act, a_chain)
                act.wait_ge(v_chain, at_g)
                ch.done(act.activation(g8[:, :, :], g8[:, :, :], ACT.Exp))
                act.wait_ge(v_chain, at_e)
                ch.done(act.activation(ex[:, :], ex[:, :], ACT.Exp))

            @block.tensor
            def _(pe):
                pe.wait_ge(c_in, 64)
                for j in range(LT):
                    for k in range(KD):
                        mm = pe.matmul(raw[:, j // 4, j % 4, 0:EG + NE], hT[:, k, j * P:(j + 1) * P], w[:, k], start=(k == 0), stop=(k == KD - 1))
                mm.then_inc(r_done, 1)
                pe.wait_ge(v_chain, at_c)
                pe.matmul(rank[:, :, :], C["lt"], AA[:, :, :], start=True, stop=False)
                pe.matmul(rank[:, :, :], C["ones"], AC[:, :, :], start=False, stop=True)
                pe.matmul(tot[:, 0:NE], C["ones"], sl[:, 0], start=True, stop=True).then_inc(cnt_done, 1)

            @block.gpsimd
            def _(g):
                ch = Chain(g, p_chain)
                ch.done(g.memset(none[:, :], NONE))
                for j in range(LT):
                    for k in range(2):
                        g.iota(info[:, j, k, 0:1], [[0, 1]], base=j * P, channel_multiplier=1)
                        e = g.iota(info[:, j, k, 1:2], [[0, 1]], base=2 * j * P + k, channel_multiplier=2)
                ch.done(e)
                g.dma_start(S["idx"].rearrange("(p n) c -> p (n c)", p=P), none[:, :]).then_inc(init, 16)
                g.wait_ge(init, 16)
                g.wait_ge(v_chain, N_ALL[0])
                for j in range(LT):
                    for k in range(2):
                        g.indirect_dma_start(out=S["idx"], out_offset=bass.IndirectOffsetOnAxis(ap=dsti[:, k, j:j + 1], axis=0),
                                             in_=info[:, j, k, :], in_offset=None, bounds_check=NBLK * P - 1, oob_is_err=False).then_inc(done, 16)
                g.dma_start(S["be"], bei[:, :]).then_inc(done, 16)
                g.wait_ge(done, 16 * (2 * LT + 1))

            @block.sync
            def _(sp):
                sp.dma_start(w[:, :, 0:EG], A["moe_w_group_2"][0].rearrange("(k p) n -> p k n", p=P)).then_inc(c_in, 16)
                sp.dma_start(w[:, :, EG:], A["moe_w_expert_2"][0].rearrange("(k p) n -> p k n", p=P)).then_inc(c_in, 16)
                sp.dma_start(bias[:, 0:EG], row_bcast(A["moe_b_group_2"][0])).then_inc(c_in, 16)
                sp.dma_start(bias[:, EG:], row_bcast(A["moe_b_expert_2"][0])).then_inc(c_in, 16)


def experts(nc, C, A, S):
    TURNS = NBLK // 2
    HT = HID // P
    with Phase(nc, "moe") as f:
        nw = f.sb("nw", [P, KD])
        be = f.sb("be", [1, P], I32)
        wg, wu, wd = f.sb("wg", [P, 2, KD, HID]), f.sb("wu", [P, 2, KD, HID]), f.sb("wd", [P, 2, HT, D])
        idx = [f.sb(f"idx{u}", [P, 2], U32) for u in range(2)]
        sidx = [f.sb(f"sidx{u}", [P, 1], U32) for u in range(2)]
        xg = [f.sb(f"xg{u}", [P, D]) for u in range(2)]
        xT = f.sb("xT", [P, 2, KD, P])
        th, sg = f.sb("th", [P, 2, HT * P]), f.sb("sg", [P, 2, HT * P])
        hh = f.sb("h", [P, 2, HT, P])
        y = [f.sb(f"y{u}", [P, D]) for u in range(2)]
        pt = f.ps("pt", [P, 2, 4, P])
        gu = f.ps("gu", [P, 2, 2, HT * P])
        acc = f.ps("acc", [P, 2, 2, HALF])
        c_in, w_in, idx_in, sidx_done, got = f.sem("c_in"), f.sem2("w_in"), f.sem2("idx_in"), f.sem("sidx_done"), f.sem2("got")
        turned, ev_a, ev_v, gu_mm, th_done, sg_done, h_done, d_mm, y_a, y_v, zero = (f.sem(n) for n in ("turned", "ev_a", "ev_v", "gu_mm", "th_done", "sg_done", "h_done", "d_mm", "y_a", "y_v", "zero"))
        put, passed = f.sem2("put"), f.sem("passed")

        def turns(eng, body):
            body(0, True, False)
            with eng.Fori(1, TURNS - 1) as i:
                body(i, False, False)
            body(TURNS - 1, False, True)

        with nc.Block() as block:
            @block.sync
            def _(sp):
                with nc.allow_non_contiguous_dma(reason="a vector by channel, and the blocks' experts"):
                    sp.dma_start(nw[:, :], col_view(A["norm_ffn_2"][0], KD)).then_inc(c_in, 16)
                    sp.dma_start(be[:, :], S["be"].rearrange("b o -> o b")).then_inc(c_in, 16)
                sp.wait_ge(c_in, 32)

                def body(i, first, last):
                    for u in range(2):
                        b = 2 * i + u
                        e = sp.value_load(be[0:1, bass.ds(b, 1)], min_val=0, max_val=NE - 1)
                        if not first:
                            sp.wait_ge(got[u], 16 * i)
                            sp.sem_inc(passed, 1)
                            sp.wait_ge(sidx_done, b - 1)
                            sp.sem_inc(passed, 1)
                        sp.dma_start(idx[u][:, :], S["idx"][bass.ds(b * P, P), :]).then_inc(idx_in[u], 16)
                        if not first:
                            sp.wait_ge(gu_mm, b - 1)
                            sp.sem_inc(passed, 1)
                        sp.dma_start(wg[:, u], A["moe_w_gate_2"][0, bass.ds(e, 1), :, :].rearrange("a (k p) n -> p (a k) n", p=P)).then_inc(w_in[u], 16)
                        sp.dma_start(wu[:, u], A["moe_w_up_2"][0, bass.ds(e, 1), :, :].rearrange("a (k p) n -> p (a k) n", p=P)).then_inc(w_in[u], 16)
                        if not first:
                            sp.wait_ge(d_mm, b - 1)
                            sp.sem_inc(passed, 1)
                        sp.dma_start(wd[:, u], A["moe_w_down_2"][0, bass.ds(e, 1), :, :].rearrange("a (k p) n -> p (a k) n", p=P)).then_inc(w_in[u], 16)

                turns(sp, body)

            @block.gpsimd
            def _(g):
                for u in range(2):
                    g.memset(xg[u][:, :], 0.0).then_inc(zero, 1)
                g.wait_ge(zero, 2)

                def gather(i, u):
                    g.wait_ge(idx_in[u], 16 * (i + 1))
                    g.sem_inc(passed, 1)
                    g.indirect_dma_start(out=xg[u][:, :], out_offset=None, in_=S["xn"], in_offset=bass.IndirectOffsetOnAxis(ap=idx[u][:, 0:1], axis=0),
                                         bounds_check=LAT - 1, oob_is_err=False).then_inc(got[u], 16)

                def scatter(i, u):
                    b = 2 * i + u
                    g.wait_ge(y_a, b + 1)
                    g.wait_ge(y_v, b + 1)
                    g.sem_inc(passed, 1)
                    g.indirect_dma_start(out=S["Y"], out_offset=bass.IndirectOffsetOnAxis(ap=sidx[u][:, :], axis=0), in_=y[u][:, :], in_offset=None,
                                         bounds_check=2 * LAT - 1, oob_is_err=False).then_inc(put[u], 16)

                def body(i, first, last):
                    for u in range(2):
                        b = 2 * i + u
                        if not first:
                            g.wait_ge(turned, 2 * (b - 1))
                        gather(i, u)
                        if first and u == 0:
                            continue
                        if u == 0:
                            scatter(i - 1, 1)
                        else:
                            scatter(i, 0)
                    if last:
                        scatter(i, 1)

                turns(g, body)
                for u in range(2):
                    g.wait_ge(put[u], 16 * TURNS)

            @block.tensor
            def _(pe):
                def turn(i, u, first):
                    b = 2 * i + u
                    pe.wait_ge(got[u], 16 * (i + 1))
                    for q in range(2):
                        if not (first and u == 0):
                            pe.wait_ge(ev_a if q == 0 else ev_v, b)
                        for k in range(4):
                            mm = pe.transpose(pt[:, q, k], xg[u][:, (4 * q + k) * P:(4 * q + k + 1) * P], C["ident"])
                        mm.then_inc(turned, 1)

                def body(i, first, last):
                    for u in range(2):
                        b = 2 * i + u
                        pe.wait_ge(w_in[u], 48 * (i + 1))
                        pe.wait_ge(ev_a, b + 1)
                        pe.wait_ge(ev_v, b + 1)
                        if not first:
                            pe.wait_ge(h_done, b - 1)
                        for w, m in enumerate((wg, wu)):
                            for n in range(HT):
                                for k in range(KD):
                                    mm = pe.matmul(gu[:, u, w, n * P:(n + 1) * P], m[:, u, k, n * P:(n + 1) * P], xT[:, u, k], start=(k == 0), stop=(k == KD - 1))
                        mm.then_inc(gu_mm, 1)
                        if u == 0:
                            turn(i, 1, first)
                        elif not last:
                            turn(i + 1, 0, False)
                        pe.wait_ge(h_done, b + 1)
                        if not first:
                            pe.wait_ge(y_a, b - 1)
                            pe.wait_ge(y_v, b - 1)
                        for n in range(2):
                            for k in range(HT):
                                mm = pe.matmul(acc[:, u, n], hh[:, u, k], wd[:, u, k, n * HALF:(n + 1) * HALF], start=(k == 0), stop=(k == HT - 1))
                        mm.then_inc(d_mm, 1)

                turn(0, 0, True)
                turns(pe, body)

            @block.scalar
            def _(act):
                act.wait_ge(c_in, 32)

                def rows(i, u, first):
                    b = 2 * i + u
                    act.wait_ge(turned, 2 * b + 1)
                    if not first:
                        act.wait_ge(gu_mm, b - 1)
                    for k in range(4):
                        e = act.activation(xT[:, u, k], pt[:, 0, k], ACT.Copy, scale=nw[:, k:k + 1])
                    e.then_inc(ev_a, 1)

                def body(i, first, last):
                    for u in range(2):
                        b = 2 * i + u
                        act.wait_ge(gu_mm, b + 1)
                        if not first:
                            act.wait_ge(h_done, b - 1)
                        act.activation(th[:, u], gu[:, u, 0], ACT.Tanh, scale=0.5).then_inc(th_done, 1)
                        if u == 0:
                            rows(i, 1, first)
                        elif not last:
                            rows(i + 1, 0, False)
                        act.wait_ge(d_mm, b + 1)
                        if not first:
                            act.wait_ge(put[u], 16 * i)
                        act.copy(y[u][:, 0:HALF], acc[:, u, 0]).then_inc(y_a, 1)

                rows(0, 0, True)
                turns(act, body)

            @block.vector
            def _(v):
                v.wait_ge(c_in, 32)

                def rows(i, u, first):
                    b = 2 * i + u
                    v.wait_ge(turned, 2 * b + 2)
                    if not first:
                        v.wait_ge(gu_mm, b - 1)
                    for k in range(4, KD):
                        e = v.tensor_scalar(xT[:, u, k], pt[:, 1, k - 4], nw[:, k:k + 1], None, ALU.mult)
                    e.then_inc(ev_v, 1)

                def body(i, first, last):
                    for u in range(2):
                        b = 2 * i + u
                        v.wait_ge(idx_in[u], 16 * (i + 1))
                        if not first:
                            v.wait_ge(put[u], 16 * i)
                        v.tensor_copy(sidx[u][:, :], idx[u][:, 1:2]).then_inc(sidx_done, 1)
                        v.wait_ge(th_done, b + 1)
                        if not first:
                            v.wait_ge(d_mm, b - 1)
                        v.scalar_tensor_tensor(out=sg[:, u], in0=th[:, u], scalar=1.0, in1=gu[:, u, 0], op0=ALU.add, op1=ALU.mult).then_inc(sg_done, 1)
                        v.wait_ge(sg_done, b + 1)
                        v.scalar_tensor_tensor(out=hh[:, u].rearrange("p k t -> p (k t)"), in0=sg[:, u], scalar=0.5, in1=gu[:, u, 1], op0=ALU.mult, op1=ALU.mult).then_inc(h_done, 1)
                        if u == 0:
                            rows(i, 1, first)
                        elif not last:
                            rows(i + 1, 0, False)
                        v.wait_ge(d_mm, b + 1)
                        v.tensor_copy(y[u][:, HALF:D], acc[:, u, 1]).then_inc(y_v, 1)

                rows(0, 0, True)
                turns(v, body)


def combine(nc, C, A, S, wts, out):
    with Phase(nc, "comb") as f:
        Y, r = f.sb("Y", [P, 2, 2, D]), f.sb("r", [P, 2, D])
        a, o = f.sb("a", [P, 2, D]), f.sb("o", [P, 2, D])
        y_in, mid, done, stored = f.sem2("y_in"), f.sem("mid"), f.sem("done"), f.sem2("stored")
        with nc.Block() as block:
            @block.sync
            def _(sp):
                for i in range(LT):
                    if i >= 2:
                        sp.wait_ge(done, i - 1)
                    sp.dma_start(Y[:, i % 2], S["Y"][2 * i * P:2 * (i + 1) * P, :].rearrange("(p k) n -> p k n", k=2)).then_inc(y_in[i % 2], 16)
                    sp.dma_start(r[:, i % 2], S["x3"][i * P:(i + 1) * P, :]).then_inc(y_in[i % 2], 16)

            @block.vector
            def _(v):
                for i in range(LT):
                    v.wait_ge(y_in[i % 2], 32 * (i // 2 + 1))
                    v.scalar_tensor_tensor(out=a[:, i % 2], in0=Y[:, i % 2, 0], scalar=wts[:, i, 0:1], in1=r[:, i % 2], op0=ALU.mult, op1=ALU.add).then_inc(mid, 1)
                    v.wait_ge(mid, i + 1)
                    if i >= 2:
                        v.wait_ge(stored[i % 2], 16 * (i // 2))
                    v.scalar_tensor_tensor(out=o[:, i % 2], in0=Y[:, i % 2, 1], scalar=wts[:, i, 1:2], in1=a[:, i % 2], op0=ALU.mult, op1=ALU.add).then_inc(done, 1)

            @block.gpsimd
            def _(g):
                for i in range(LT):
                    g.wait_ge(done, i + 1)
                    g.dma_start(out[i * P:(i + 1) * P, :], o[:, i % 2]).then_inc(stored[i % 2], 16)
                for b in range(2):
                    g.wait_ge(stored[b], 16 * (LT // 2))


def moe_layer(nc, C, A, S, out):
    with ExitStack() as c1:
        wts = c1.enter_context(nc.sbuf_tensor("wts", [P, LT, 2], F32))
        with ExitStack() as c2:
            hT = c2.enter_context(nc.sbuf_tensor("h5T", [P, KD, LAT], F32))
            norm_turn(nc, "n5", C, [(S["x3"][i * P:(i + 1) * P, :], 0, i * P) for i in range(LT)], [(A["norm_ffn_2"][0], None, None)], hT, keep=S["xn"])
            route(nc, C, A, S, hT, wts)
        experts(nc, C, A, S)
        combine(nc, C, A, S, wts, out)


def first_layer(nc, C, A, S):
    m = lambda c, l, j: S["mod"][c, l, j * D:(j + 1) * D]
    rows = [A["ctx"][0, i * P:(i + 1) * P, :] if i < CT else A["x"][0, (i - CT) * P:(i - CT + 1) * P, :] for i in range(TT)]
    with nc.sbuf_tensor("h0T", [P, KD, T], F32) as hT:
        norm_turn(nc, "n0", C, [(rows[i], 0 if i < CT else 1, i * P) for i in range(TT)],
                  [(A["norm_w"][0], m(1, 0, 1), m(1, 0, 0)), (A["norm_w"][0], m(0, 0, 1), m(0, 0, 0))], hT)
        mamba_layer(nc, C, A, S, hT)
    out_project(nc, "m_out", C, [S["my"][i * P:(i + 1) * P, :] for i in range(TT)], A["m_out_w"][0],
                [(i, rows[i], m(1 if i < CT else 0, 0, 2)) for i in range(TT)], S["h1"], norm_w=A["m_norm_w"][0])


def second_layer(nc, C, A, S):
    m = lambda c, l, j: S["mod"][c, l, j * D:(j + 1) * D]
    with nc.sbuf_tensor("h1T", [P, KD, T], F32) as hT:
        norm_turn(nc, "n1", C, [(S["h1"][i * P:(i + 1) * P, :], 0 if i < CT else 1, i * P) for i in range(TT)],
                  [(A["norm_w"][1], m(1, 1, 1), m(1, 1, 0)), (A["norm_w"][1], m(0, 1, 1), m(0, 1, 0))], hT)
        attention_layer(nc, C, A, S, hT)


SCRATCH = {
    "mod": (2, 2, 3 * D), "my": (T, DI), "h1": (T, D), "ag": (LAT, D), "aoT": (D, LAT), "h2": (LAT, D),
    "x1": (LAT, D), "pa": (LAT, 352), "hfT": (1536, LAT), "hih": (LAT, D), "ho": (LAT, D // 2), "mixT": (D, LAT),
    "x2": (LAT, D), "xoT": (D, LAT), "x3": (LAT, D), "xn": (LAT, D), "Y": (2 * LAT, D),
}


def program(nc, A, out, offsets):
    S = {k: nc.dram_tensor("scratch_" + k, s, F32).ap() for k, s in SCRATCH.items()}
    S["idx"] = nc.dram_tensor("scratch_idx", (NBLK * P, 2), U32).ap()
    S["be"] = nc.dram_tensor("scratch_be", (P, 1), I32).ap()
    with ExitStack() as ctx:
        C = load_constants(nc, ctx, A, offsets)
        modulation(nc, A, S)
        first_layer(nc, C, A, S)
        second_layer(nc, C, A, S)
        mixer_layer(nc, C, A, S)
        cross_layer(nc, C, A, S)
        moe_layer(nc, C, A, S, out[0])


_INS = ['x', 'c', 'ctx', 'c_ctx', 'norm_w', 'mod_w', 'mod_b', 'final_norm_w', 'm_in_w', 'm_conv_w', 'm_conv_b', 'm_a_log',
        'm_dt_bias', 'm_d', 'm_norm_w', 'm_out_w', 'a_in_w', 'a_q_norm', 'a_k_norm', 'a_out_w',
        'mem_2', 'positions_2', 'norm_mix_2', 'w_in_2', 'mla_q_a_norm_2', 'mla_w_q_up_2', 'mla_kv_a_norm_2',
        'mla_w_kv_up_2', 'mla_q_norm_2', 'mla_k_norm_2', 'hg_lb_logits_2', 'hg_o_norm_2', 'w_out_2',
        'norm_cross_2', 'norm_mem_2', 'x_w_q_2', 'x_w_kv_2', 'x_q_norm_2', 'x_k_norm_2', 'x_w_o_2', 'norm_ffn_2',
        'moe_w_group_2', 'moe_b_group_2', 'moe_w_expert_2', 'moe_b_expert_2', 'moe_w_gate_2', 'moe_w_up_2', 'moe_w_down_2']
_OUTS = [((1, LAT, D), 'float32')]


def kernel(**inputs):
    import numpy as _np
    import concourse.bacc as _bacc
    from concourse import mybir as _mybir
    from concourse.bass_utils import run_bass_kernel_spmd as _run

    nc = _bacc.Bacc("TRN2", target_bir_lowering=False, num_devices=1)
    constants, levels, offsets = shape_constants()
    given = {name: _np.ascontiguousarray(inputs[name]) for name in _INS}
    given["constants"], given["levels"] = constants, levels
    arrays, A = {}, {}
    for name, a in given.items():
        arrays[f"in_{name}_dram"] = a
        A[name] = nc.dram_tensor(f"in_{name}_dram", a.shape, _mybir.dt.from_np(a.dtype), kind="ExternalInput").ap()
    outs = [nc.dram_tensor(f"out_{i}_dram", s, _mybir.dt.from_np(_np.dtype(t)), kind="ExternalOutput").ap() for i, (s, t) in enumerate(_OUTS)]
    program(nc, A, outs[0], offsets)
    r = _run(nc, [arrays], core_ids=[0])
    return r.results[0]["out_0_dram"]
```

```python
from contextlib import ExitStack

import numpy as np
import concourse.bass as bass
from concourse import mybir

F32 = mybir.dt.float32
I32 = mybir.dt.int32
U32 = mybir.dt.uint32
F32R = mybir.dt.float32r
ALU = mybir.AluOpType
ACT = mybir.ActivationFunctionType
AX = mybir.AxisListType

P = 128
D = 1024
KD = D // P
CTX, LAT = 256, 1024
T = CTX + LAT
CT, LT, TT = CTX // P, LAT // P, T // P
EPS = 1e-6
HALF = 512


class Chain:

    def __init__(self, eng, sem, turn=0, per=0):
        self.eng, self.sem, self.turn, self.per, self.n = eng, sem, turn, per, 0

    def done(self, ins):
        ins.then_inc(self.sem, 1)
        self.n += 1
        self.eng.wait_ge(self.sem, self.turn * self.per + self.n)

    def close(self):
        assert self.n == self.per, (self.n, self.per)


class Phase:

    def __init__(self, nc, name):
        self.nc, self.name, self.ctx = nc, name, ExitStack()
        self.sems = []

    def __enter__(self):
        self.ctx.__enter__()
        return self

    def __exit__(self, *a):
        r = self.ctx.__exit__(*a)
        if a[0] is None and self.sems:
            self.nc.clear_and_free_semaphores(self.sems)
            self.nc.all_engine_barrier()
        return r

    def sb(self, name, shape, dt=F32):
        return self.ctx.enter_context(self.nc.sbuf_tensor(f"{self.name}_{name}", shape, dt))

    def ps(self, name, shape, dt=F32):
        return self.ctx.enter_context(self.nc.psum_tensor(f"{self.name}_{name}", shape, dt))

    def sem(self, name):
        s = self.nc.alloc_semaphore(f"{self.name}_{name}")
        self.sems.append(s)
        return s

    def sem2(self, name, n=2):
        return [self.sem(f"{name}{i}") for i in range(n)]


def shape_constants():
    p = np.arange(P)[:, None]
    f = np.arange(P)[None, :]
    parts = {
        "ident": p == f,
        "ones": np.ones((P, P)),
        "le": p <= f,
        "ge": p >= f,
        "gt": p > f,
        "lt": p < f,
    }
    levels = []
    for lo, hi in ((0, 1), (1, 0)):
        m = [p == f]
        for l in range(7):
            same = (p >> (l + 1)) == (f >> (l + 1))
            m.append(same & (((p >> l) & 1) == lo) & (((f >> l) & 1) == hi))
        levels += m
    parts["iota"] = np.tile(np.arange(P)[None, :], (P, 1))
    parts["pidx"] = p
    parts["neghalf"] = np.full((P, 64), -0.5)
    inv = 10000.0 ** (-np.arange(0, 32, 2, dtype=np.float32) / np.float32(32))
    t = np.arange(LAT)
    ang = np.concatenate([(t // 64)[:, None] * inv, (t % 64)[:, None] * inv], 1).astype(np.float32)
    parts["ropec"] = np.cos(ang).reshape(LT, P, 32).transpose(1, 0, 2).reshape(P, LT * 32)
    parts["ropes"] = np.sin(ang).reshape(LT, P, 32).transpose(1, 0, 2).reshape(P, LT * 32)
    inv2 = 1.0 / (10000.0 ** (np.arange(16, dtype=np.float32) / np.float32(16)))
    parts["inv2"] = np.tile(inv2[None, :], (P, 1))
    at, off = 0, {}
    for k, v in parts.items():
        off[k] = (at, at + v.shape[1])
        at += v.shape[1]
    return np.concatenate([v.astype(np.float32) for v in parts.values()], 1), np.concatenate(levels, 1).astype(np.float32), off


def col_view(row, n):
    return row.rearrange("(k p) -> p k", p=P)


def row_bcast(row):
    return row.rearrange("(a n) -> a n", a=1).to_broadcast([P, row.shape[0]])


def modulation(nc, A, S):
    NCH = 3 * D // HALF
    with Phase(nc, "mod") as f:
        cT = f.sb("cT", [P, 2, KD])
        th = f.sb("th", [P, 2, KD])
        sT = f.sb("sT", [P, KD, 2])
        w = f.sb("w", [P, 2, KD, HALF])
        bias = f.sb("bias", [2, 2, 3 * D])
        rows = f.sb("rows", [2, 2, 3 * D])
        acc = f.ps("acc", [2, 2, HALF])
        c_in, c_th, v_chain, s_ready = f.sem("c_in"), f.sem("c_th"), f.sem("v_chain"), f.sem("s_ready")
        w_in, mm_done, row_done, out_done = f.sem2("w_in"), f.sem("mm_done"), f.sem("row_done"), f.sem("out_done")
        steps = [(l, n) for l in range(2) for n in range(NCH)]
        with nc.Block() as block:
            @block.sync
            def _(sp):
                with nc.allow_non_contiguous_dma(reason="two short vectors"):
                    sp.dma_start(cT[:, 0, :], col_view(A["c"][0], KD)).then_inc(c_in, 16)
                    sp.dma_start(cT[:, 1, :], col_view(A["c_ctx"], KD)).then_inc(c_in, 16)
                for a in range(2):
                    sp.dma_start(bias[a:a + 1, :, :], A["mod_b"][:, :].rearrange("(a l) n -> a l n", a=1)).then_inc(c_in, 16)
                for i, (l, n) in enumerate(steps):
                    if i >= 2:
                        sp.wait_ge(mm_done, i - 1)
                    sp.dma_start(w[:, i % 2], A["mod_w"][l, :, n * HALF:(n + 1) * HALF].rearrange("(k p) n -> p k n", p=P)).then_inc(w_in[i % 2], 16)
                sp.wait_ge(row_done, len(steps))
                sp.dma_start(S["mod"], rows[:, :, :]).then_inc(out_done, 16)
                sp.wait_ge(out_done, 16)

            @block.scalar
            def _(act):
                act.wait_ge(c_in, 64)
                act.activation(th[:, :, :], cT[:, :, :], ACT.Tanh, scale=0.5).then_inc(c_th, 1)

            @block.vector
            def _(v):
                ch = Chain(v, v_chain)
                v.wait_ge(c_th, 1)
                ch.done(v.scalar_tensor_tensor(out=th[:, :, :], in0=th[:, :, :], scalar=1.0, in1=cT[:, :, :], op0=ALU.add, op1=ALU.mult))
                v.tensor_scalar(sT[:, :, :].rearrange("p k a -> p a k"), th[:, :, :], 0.5, None, ALU.mult).then_inc(s_ready, 1)
                for i, (l, n) in enumerate(steps):
                    v.wait_ge(mm_done, i + 1)
                    at = slice(n * HALF, (n + 1) * HALF)
                    v.tensor_tensor(rows[:, l, at], acc[:, i % 2], bias[:, l, at], ALU.add).then_inc(row_done, 1)

            @block.tensor
            def _(pe):
                pe.wait_ge(s_ready, 1)
                for i in range(len(steps)):
                    pe.wait_ge(w_in[i % 2], 16 * (i // 2 + 1))
                    if i >= 2:
                        pe.wait_ge(row_done, i - 1)
                    for k in range(KD):
                        mm = pe.matmul(acc[:, i % 2], sT[:, k, :], w[:, i % 2, k], start=(k == 0), stop=(k == KD - 1))
                    mm.then_inc(mm_done, 1)


def norm_turn(nc, name, C, tiles, sets, hT, keep=None, first=None):
    n = len(tiles)
    ns = len(sets)
    with Phase(nc, name) as f:
        x = f.sb("x", [P, 2, D])
        x2 = f.sb("x2", [P, 2, D]) if first else x
        sq = f.sb("sq", [P, D])
        xn = f.sb("xn", [P, 2, D])
        ss, ms, rs = f.sb("ss", [P, 2 * n]), f.sb("ms", [P, 2 * n]), f.sb("rs", [P, 2 * n])
        cols = f.sb("cols", [P, ns, 3, KD])
        gain = f.sb("gain", [P, ns, KD])
        wrow = f.sb("wrow", [P, D]) if first else None
        pt = f.ps("pt", [P, 2, KD, P])
        c_in, x_in, v_chain, ss_done = f.sem("c_in"), f.sem2("x_in"), f.sem("v_chain"), f.sem("ss_done")
        rs_done, p_chain, xn_done, turned = f.sem("rs_done"), f.sem("p_chain"), f.sem("xn_done"), f.sem("turned")
        ev_a, ev_v, kept, resid = f.sem("ev_a"), f.sem("ev_v"), f.sem2("kept"), f.sem2("resid")
        ncol = sum(1 for s in sets for r in s if r is not None)
        R = 2 if first else 1
        with nc.Block() as block:
            @block.sync
            def _(sp):
                with nc.allow_non_contiguous_dma(reason="vectors by channel"):
                    for i, s in enumerate(sets):
                        for j, r in enumerate(s):
                            if r is not None:
                                sp.dma_start(cols[:, i, j], col_view(r, KD)).then_inc(c_in, 16)
                if first:
                    sp.dma_start(wrow[:, :], row_bcast(first[0])).then_inc(c_in, 16)
                for i, (src, s, col) in enumerate(tiles):
                    if i >= 2:
                        sp.wait_ge(xn_done, R * (i - 1))
                        sp.wait_ge(ss_done, R * (i - 2) + 1)
                    sp.dma_start(x[:, i % 2], src).then_inc(x_in[i % 2], 16)

            @block.gpsimd
            def _(g):
                ch = Chain(g, p_chain)
                for j in range(R * n):
                    g.wait_ge(ss_done, j + 1)
                    ch.done(g.tensor_scalar(ms[:, j:j + 1], ss[:, j:j + 1], 1.0 / D, EPS, ALU.mult, ALU.add))
                    g.tensor_tensor(rs[:, j:j + 1], ms[:, j:j + 1], C["neghalf"][:, 0:1], ALU.pow).then_inc(rs_done, 1)
                    i = j // R
                    if first and j % 2 == 0:
                        g.wait_ge(xn_done, j + 1)
                        g.dma_start(first[1][i * P:(i + 1) * P, :], x2[:, i % 2]).then_inc(resid[i % 2], 16)
                    if keep is not None and j % R == R - 1:
                        g.wait_ge(xn_done, j + 1)
                        g.dma_start(keep[i * P:(i + 1) * P, :], xn[:, i % 2]).then_inc(kept[i % 2], 16)
                for b in range(2):
                    if keep is not None:
                        g.wait_ge(kept[b], 16 * ((n - b + 1) // 2))
                    if first:
                        g.wait_ge(resid[b], 16 * ((n - b + 1) // 2))

            @block.scalar
            def _(act):
                def evict(i):
                    src, s, col = tiles[i]
                    act.wait_ge(turned, i + 1)
                    act.wait_ge(v_chain, ns)
                    for k in range(KD // 2):
                        if sets[s][2] is None:
                            e = act.activation(hT[:, k, col:col + P], pt[:, i % 2, k], ACT.Copy, scale=gain[:, s, k:k + 1])
                        else:
                            e = act.activation(hT[:, k, col:col + P], pt[:, i % 2, k], ACT.Identity, scale=gain[:, s, k:k + 1], bias=cols[:, s, 2, k:k + 1])
                    e.then_inc(ev_a, 1)

                for i in range(n):
                    act.wait_ge(x_in[i % 2], 16 * (i // 2 + 1))
                    if i >= 1:
                        act.wait_ge(ss_done, R * i)
                    act.activation(sq[:, :], x[:, i % 2], ACT.Square, accum_out=ss[:, R * i:R * i + 1]).then_inc(ss_done, 1)
                    if first:
                        act.wait_ge(xn_done, R * i + 1)
                        act.wait_ge(ss_done, R * i + 1)
                        act.activation(sq[:, :], x2[:, i % 2], ACT.Square, accum_out=ss[:, 2 * i + 1:2 * i + 2]).then_inc(ss_done, 1)
                    if i >= 1:
                        evict(i - 1)
                evict(n - 1)

            @block.vector
            def _(v):
                ch = Chain(v, v_chain)
                v.wait_ge(c_in, 16 * (ncol + (1 if first else 0)))
                for i, s in enumerate(sets):
                    if s[1] is None:
                        e = v.tensor_copy(gain[:, i], cols[:, i, 0])
                    else:
                        e = v.scalar_tensor_tensor(out=gain[:, i], in0=cols[:, i, 1], scalar=1.0, in1=cols[:, i, 0], op0=ALU.add, op1=ALU.mult)
                    ch.done(e)

                def evict(i):
                    src, s, col = tiles[i]
                    v.wait_ge(turned, i + 1)
                    for k in range(KD // 2, KD):
                        if sets[s][2] is None:
                            e = v.tensor_scalar(hT[:, k, col:col + P], pt[:, i % 2, k], gain[:, s, k:k + 1], None, ALU.mult)
                        else:
                            e = v.tensor_scalar(hT[:, k, col:col + P], pt[:, i % 2, k], gain[:, s, k:k + 1], cols[:, s, 2, k:k + 1], ALU.mult, ALU.add)
                    e.then_inc(ev_v, 1)

                for i in range(n):
                    j = R * i
                    if i >= 2 and keep is not None:
                        v.wait_ge(kept[i % 2], 16 * (i // 2))
                    if i >= 2 and first:
                        v.wait_ge(resid[i % 2], 16 * (i // 2))
                    if first:
                        v.wait_ge(rs_done, j + 1)
                        if i >= 2:
                            v.wait_ge(ss_done, j - 2)
                        v.scalar_tensor_tensor(out=x2[:, i % 2], in0=x[:, i % 2], scalar=rs[:, j:j + 1], in1=wrow[:, :], op0=ALU.mult, op1=ALU.mult).then_inc(xn_done, 1)
                        v.wait_ge(xn_done, j + 1)
                        j += 1
                    v.wait_ge(rs_done, j + 1)
                    if i >= 2:
                        v.wait_ge(turned, i - 1)
                    v.tensor_scalar(xn[:, i % 2], x2[:, i % 2], rs[:, j:j + 1], None, ALU.mult).then_inc(xn_done, 1)
                    if i >= 1:
                        evict(i - 1)
                evict(n - 1)

            @block.tensor
            def _(pe):
                for i in range(n):
                    pe.wait_ge(xn_done, R * (i + 1))
                    if i >= 2:
                        pe.wait_ge(ev_a, i - 1)
                        pe.wait_ge(ev_v, i - 1)
                    for k in range(KD):
                        e = pe.transpose(pt[:, i % 2, k], xn[:, i % 2, k * P:(k + 1) * P], C["ident"])
                    e.then_inc(turned, 1)


def split_rows(nc, name, a, a1, a2):
    n = a.shape[1]
    with Phase(nc, name) as f:
        rounded = f.sem("rounded")
        with nc.Block() as block:
            @block.scalar
            def _(act):
                for k in range(n):
                    act.copy(a1[:, k], a[:, k]).then_inc(rounded, 1)

            @block.vector
            def _(v):
                for k in range(n):
                    v.wait_ge(rounded, k + 1)
                    v.tensor_tensor(a2[:, k], a[:, k], a1[:, k].bitcast(F32), ALU.subtract)


def project(nc, name, hT, cols, w, out=None, chunk=HALF, put=None):
    pair = isinstance(hT, tuple)
    K, N = w.shape
    kt = -(-K // P)
    kp = [min(P, K - k * P) for k in range(kt)]
    chunks = [(a, min(a + chunk, N)) for a in range(0, N, chunk)]
    m = len(cols)
    with Phase(nc, name) as f:
        wb = f.sb("w", [P, 2, kt, HALF])
        w1, w2_ = (f.sb(x, [P, 2, kt, HALF], F32R) for x in ("w1", "w2")) if pair else (None, None)
        rounded, w_split = f.sem("rounded"), f.sem("w_split")
        NS = 4
        st = f.sb("st", [P, NS, HALF])
        acc = f.ps("acc", [P, NS, HALF])
        w_in, mm_done, copied, stored = f.sem2("w_in"), f.sem("mm_done"), f.sem2("copied"), f.sem2("stored", NS)
        steps = [(c, j) for c in range(len(chunks)) for j in range(m)]
        with nc.Block() as block:
            @block.sync
            def _(sp):
                for c, (a, b) in enumerate(chunks):
                    if c >= 2:
                        sp.wait_ge(mm_done, (c - 1) * m)
                    full = K // P
                    sp.dma_start(wb[:, c % 2, 0:full, 0:b - a], w[0:full * P, a:b].rearrange("(k p) n -> p k n", p=P)).then_inc(w_in[c % 2], 16)
                    if full < kt:
                        sp.dma_start(wb[0:kp[-1], c % 2, full, 0:b - a], w[full * P:, a:b]).then_inc(w_in[c % 2], 16)

            @block.tensor
            def _(pe):
                for i, (c, j) in enumerate(steps):
                    a, b = chunks[c]
                    if pair:
                        pe.wait_ge(w_split, c + 1)
                    else:
                        pe.wait_ge(w_in[c % 2], (16 if K % P == 0 else 32) * (c // 2 + 1))
                    if i >= NS:
                        pe.wait_ge(copied[i % 2], (i - NS) // 2 + 1)
                    if pair:
                        w2 = w2_[:, c % 2]
                        terms = [(x[:, k, cols[j]:cols[j] + P], y[:, k, 0:b - a]) for x, y in ((hT[0], w1[:, c % 2]), (hT[0], w2), (hT[1], w1[:, c % 2])) for k in range(kt)]
                        for q, (x, y) in enumerate(terms):
                            mm = pe.matmul(acc[:, i % NS, 0:b - a], x, y, start=(q == 0), stop=(q == len(terms) - 1))
                        mm.then_inc(mm_done, 1)
                        continue
                    for k in range(kt):
                        mm = pe.matmul(acc[:, i % NS, 0:b - a], hT[0:kp[k], k, cols[j]:cols[j] + P], wb[0:kp[k], c % 2, k, 0:b - a], start=(k == 0), stop=(k == kt - 1))
                    mm.then_inc(mm_done, 1)

            def split(eng, par, c):
                a, b = chunks[c]
                first, whole = w1[:, c % 2, :, 0:b - a], wb[:, c % 2, :, 0:b - a]
                if par == 0:
                    eng.wait_ge(w_in[c % 2], 16 * (c // 2 + 1))
                    if c >= 2:
                        eng.wait_ge(mm_done, (c - 1) * m)
                    eng.copy(first, whole).then_inc(rounded, 1)
                else:
                    eng.wait_ge(rounded, c + 1)
                    eng.tensor_tensor(w2_[:, c % 2, :, 0:b - a], whole, first.bitcast(F32), ALU.subtract).then_inc(w_split, 1)

            def copy(eng, par):
                if pair:
                    split(eng, par, 0)
                for i, (c, j) in enumerate(steps):
                    if i % 2 != par:
                        continue
                    a, b = chunks[c]
                    eng.wait_ge(mm_done, i + 1)
                    if i >= NS and put is None:
                        eng.wait_ge(stored[i % NS], 16 * (i // NS))
                    fn = eng.copy if par == 0 else eng.tensor_copy
                    fn(st[:, i % NS, 0:b - a] if put is None else put(j, a, b), acc[:, i % NS, 0:b - a]).then_inc(copied[par], 1)
                    if pair and j in (2, 3) and c + 1 < len(chunks):
                        split(eng, par, c + 1)

            @block.scalar
            def _(act):
                copy(act, 0)

            @block.vector
            def _(v):
                copy(v, 1)

            @block.gpsimd
            def _(g):
                if put is not None:
                    return
                for i, (c, j) in enumerate(steps):
                    a, b = chunks[c]
                    g.wait_ge(copied[i % 2], i // 2 + 1)
                    g.dma_start(out[j * P:(j + 1) * P, a:b], st[:, i % NS, 0:b - a]).then_inc(stored[i % NS], 16)
                for s in range(NS):
                    g.wait_ge(stored[s], 16 * len(range(s, len(steps), NS)))


def out_project(nc, name, C, act_rows, w, tiles, dst, norm_w):
    K = w.shape[0]
    kt = K // P
    gates = []
    for _, _, g in tiles:
        if g is not None and g not in [x for x in gates]:
            gates.append(g)
    n = len(tiles)
    with Phase(nc, name) as f:
        wb = f.sb("w", [P, 2, 2, HALF])
        a = f.sb("a", [P, K])
        w1, w2 = (f.sb(x, [P, kt, D], F32R) for x in ("w1", "w2"))
        aT1, aT2 = f.sb("aT1", [P, 2, kt, P], F32R), f.sb("aT2", [P, 2, kt, P], F32R)
        rounded, w_split, a1_done = f.sem("rounded"), f.sem("w_split"), f.sem("a1_done")
        r = f.sb("r", [P, 2, D])
        y = f.sb("y", [P, D])
        gb = f.sb("gb", [P, max(1, len(gates)), D])
        sq = f.sb("sq", [P, K], mybir.dt.bfloat16)
        ss, ms, rs = f.sb("ss", [P, n]), f.sb("ms", [P, n]), f.sb("rs", [P, n])
        nw = f.sb("nw", [P, kt])
        pt = f.ps("pt", [P, 2, 4, P])
        acc = f.ps("acc", [P, 2, 2, HALF])
        G = kt // 4
        w_in, c_in, a_in, r_in = f.sem2("w_in"), f.sem("c_in"), f.sem("a_in"), f.sem2("r_in")
        turned, at_done, mm_done, v_chain = f.sem("turned"), f.sem("at_done"), f.sem("mm_done"), f.sem("v_chain")
        y_done, stored, ss_done, ms_done, rs_done = f.sem("y_done"), f.sem2("stored"), f.sem("ss_done"), f.sem("ms_done"), f.sem("rs_done")
        nc_in = len(gates) + (1 if norm_w is not None else 0)
        with nc.Block() as block:
            @block.sync
            def _(sp):
                def load_a(i):
                    if i >= 1:
                        sp.wait_ge(turned, G * i)
                        sp.wait_ge(ss_done, i)
                    sp.dma_start(a[:, :], act_rows[tiles[i][0]]).then_inc(a_in, 16)

                load_a(0)
                with nc.allow_non_contiguous_dma(reason="a vector by channel"):
                    sp.dma_start(nw[:, :], col_view(norm_w, kt)).then_inc(c_in, 16)
                for i, g in enumerate(gates):
                    sp.dma_start(gb[:, i], row_bcast(g)).then_inc(c_in, 16)
                for p in range(4 * G):
                    k, ns = 2 * (p % (2 * G)), slice(p // (2 * G) * HALF, (p // (2 * G) + 1) * HALF)
                    if p >= 2:
                        sp.wait_ge(w_split, p - 1)
                    sp.dma_start(wb[:, p % 2], w[k * P:(k + 2) * P, ns].rearrange("(k p) n -> p k n", p=P)).then_inc(w_in[p % 2], 16)
                    if p == 3:
                        load_a(1)
                for i in range(n):
                    if i >= 1 and i + 1 < n:
                        load_a(i + 1)
                    if i >= 2:
                        sp.wait_ge(stored[i % 2], 16 * (i // 2))
                    sp.dma_start(r[:, i % 2], tiles[i][1]).then_inc(r_in[i % 2], 16)

            @block.tensor
            def _(pe):
                def turn(i, q):
                    pe.wait_ge(a_in, 16 * (i + 1))
                    j = i * G + q
                    if j >= 2:
                        pe.wait_ge(at_done, j - 1)
                    for u in range(4):
                        k = 4 * q + u
                        e = pe.transpose(pt[:, j % 2, u], a[:, k * P:(k + 1) * P], C["ident"])
                    e.then_inc(turned, 1)

                for q in range(G):
                    turn(0, q)
                for i in range(n):
                    if i >= 2:
                        pe.wait_ge(y_done, i - 1)
                    for h in range(2):
                        for q in range(G):
                            if i == 0:
                                pe.wait_ge(w_split, 2 * (h * G + q + 1))
                            if h == 0:
                                pe.wait_ge(at_done, G * i + q + 1)
                            ns = slice(h * HALF, (h + 1) * HALF)
                            for t, (x, y_) in enumerate(((aT1, w1), (aT1, w2), (aT2, w1))):
                                for k in range(4 * q, 4 * q + 4):
                                    mm = pe.matmul(acc[:, i % 2, h], x[:, i % 2, k], y_[:, k, ns], start=(t == 0 and k == 0), stop=(t == 2 and k == kt - 1))
                            if i + 1 < n and (h * G + q) % 2 == 1:
                                turn(i + 1, (h * G + q) // 2)
                    mm.then_inc(mm_done, 1)

            def piece(p):
                h, q = p // (2 * G), p % (2 * G)
                at = (slice(None), slice(2 * q, 2 * q + 2), slice(h * HALF, (h + 1) * HALF))
                return w1[at], w2[at], wb[:, p % 2]

            @block.scalar
            def _(act):
                def squares(i):
                    act.wait_ge(a_in, 16 * (i + 1))
                    if i:
                        act.wait_ge(ss_done, i)
                    act.activation(sq[:, :], a[:, :], ACT.Square, accum_out=ss[:, i:i + 1]).then_inc(ss_done, 1)

                def first_parts(i, q):
                    j = i * G + q
                    act.wait_ge(turned, j + 1)
                    if i >= 2:
                        act.wait_ge(mm_done, i - 1)
                    for u in range(4):
                        k = 4 * q + u
                        e = act.activation(aT1[:, i % 2, k], pt[:, j % 2, u], ACT.Copy, scale=nw[:, k:k + 1])
                    e.then_inc(a1_done, 1)

                act.wait_ge(c_in, 16 * nc_in)
                squares(0)
                for q in range(G):
                    first_parts(0, q)
                for p in range(4 * G):
                    act.wait_ge(w_in[p % 2], 16 * (p // 2 + 1))
                    first, _, whole = piece(p)
                    act.copy(first, whole).then_inc(rounded, 1)
                for i in range(1, n):
                    squares(i)
                    for q in range(G):
                        first_parts(i, q)

            @block.vector
            def _(v):
                ch = Chain(v, v_chain)
                v.wait_ge(c_in, 16 * nc_in)

                def second_parts(i, q):
                    j = i * G + q
                    v.wait_ge(a1_done, j + 1)
                    for u in range(4):
                        k = 4 * q + u
                        e = v.scalar_tensor_tensor(out=aT2[:, i % 2, k], in0=pt[:, j % 2, u], scalar=nw[:, k:k + 1], in1=aT1[:, i % 2, k].bitcast(F32), op0=ALU.mult, op1=ALU.subtract)
                    e.then_inc(at_done, 1)

                for q in range(G):
                    second_parts(0, q)
                for p in range(4 * G):
                    v.wait_ge(rounded, p + 1)
                    first, second, whole = piece(p)
                    v.tensor_tensor(second, whole, first.bitcast(F32), ALU.subtract).then_inc(w_split, 1)
                for i, (_, _, g) in enumerate(tiles):
                    if i + 1 < n:
                        for q in range(G):
                            second_parts(i + 1, q)
                    v.wait_ge(mm_done, i + 1)
                    v.wait_ge(r_in[i % 2], 16 * (i // 2 + 1))
                    v.wait_ge(rs_done, i + 1)
                    ch.done(v.scalar_tensor_tensor(out=y[:, :], in0=acc[:, i % 2].rearrange("p h n -> p (h n)"), scalar=rs[:, i:i + 1], in1=gb[:, gates.index(g)], op0=ALU.mult, op1=ALU.mult))
                    v.tensor_tensor(r[:, i % 2], y[:, :], r[:, i % 2], ALU.add).then_inc(y_done, 1)
                    v.wait_ge(y_done, i + 1)

            @block.gpsimd
            def _(g):
                for i in range(n):
                    if norm_w is not None:
                        g.wait_ge(ss_done, i + 1)
                        g.tensor_scalar(ms[:, i:i + 1], ss[:, i:i + 1], 1.0 / K, EPS, ALU.mult, ALU.add).then_inc(ms_done, 1)
                        g.wait_ge(ms_done, i + 1)
                        g.tensor_tensor(rs[:, i:i + 1], ms[:, i:i + 1], C["neghalf"][:, 0:1], ALU.pow).then_inc(rs_done, 1)
                    g.wait_ge(y_done, i + 1)
                    g.dma_start(dst[i * P:(i + 1) * P, :], r[:, i % 2]).then_inc(stored[i % 2], 16)
                for b in range(2):
                    g.wait_ge(stored[b], 16 * len(range(b, n, 2)))


def load_constants(nc, ctx, A, off):
    n = max(b for _, b in off.values())
    buf = ctx.enter_context(nc.sbuf_tensor("constants", [P, n], F32))
    with Phase(nc, "const") as f:
        got = f.sem("got")
        with nc.Block() as block:
            @block.sync
            def _(sp):
                sp.dma_start(buf[:, :], A["constants"]).then_inc(got, 16)
                sp.wait_ge(got, 16)
    return {k: buf[:, a:b] for k, (a, b) in off.items()}


def turn_heads(nc, name, C, n, H, d, loads, weight, blocks, rope=None, gate=None):
    npiece = len(loads(0))
    na = rope[1] if rope else 0
    with Phase(nc, name) as f:
        x = f.sb("x", [P, 2, H, d])
        sq = f.sb("sq", [P, 2, H, d])
        ss, ms, rs = f.sb("ss", [P, n, H]), f.sb("ms", [P, n, H]), f.sb("rs", [P, n, H])
        y = f.sb("y", [P, 2, H, d])
        z = f.sb("z", [P, 2, H, d])
        t = f.sb("t", [P, 4, H, max(1, na), 16])
        wr = f.sb("wr", [P, d])
        gr = f.sb("gr", [P, 2, H, d]) if gate else None
        gt = f.sb("gt", [P, 2, H, d]) if gate else None
        gr_in, gt_done = f.sem2("gr_in"), f.sem("gt_done")
        NB = len(blocks)
        pt = f.ps("pt", [P, 4, HALF])
        c_in, x_in, sq_done, ss_done = f.sem("c_in"), f.sem2("x_in"), f.sem("sq_done"), f.sem("ss_done")
        ms_done, rs_done, ready, turned, moved = f.sem("ms_done"), f.sem("rs_done"), f.sem("ready"), f.sem("turned"), f.sem("moved")
        v_chain = f.sem("v_chain")
        with nc.Block() as block:
            @block.sync
            def _(sp):
                sp.dma_start(wr[:, :], row_bcast(weight)).then_inc(c_in, 16)
                for i in range(n):
                    if i >= 2:
                        sp.wait_ge(ready, i - 1)
                    for h0, hn, c0, cn, src in loads(i):
                        sp.dma_start(x[:, i % 2, h0:h0 + hn, c0:c0 + cn], src).then_inc(x_in[i % 2], 16)
                    if gate:
                        sp.dma_start(gr[:, i % 2], gate(i)).then_inc(gr_in[i % 2], 16)

            @block.scalar
            def _(act):
                def move(i):
                    for b, (c0, cn, parts) in enumerate(blocks):
                        j = i * NB + b
                        act.wait_ge(turned, j + 1)
                        for (p0, p1), dst in parts:
                            e = act.copy(dst(i), pt[p0:p1, j % 4, 0:P])
                        e.then_inc(moved, 1)

                for i in range(n):
                    act.wait_ge(x_in[i % 2], 16 * npiece * (i // 2 + 1))
                    if i >= 2:
                        act.wait_ge(ss_done, i - 1)
                    act.activation(sq[:, i % 2], x[:, i % 2], ACT.Square).then_inc(sq_done, 1)
                    if gate:
                        act.wait_ge(gr_in[i % 2], 16 * (i // 2 + 1))
                        if i >= 2:
                            act.wait_ge(ready, i - 1)
                        act.activation(gt[:, i % 2], gr[:, i % 2], ACT.Tanh, scale=0.5).then_inc(gt_done, 1)
                    if i >= 1:
                        move(i - 1)
                move(n - 1)

            @block.gpsimd
            def _(g):
                for i in range(n):
                    g.wait_ge(ss_done, i + 1)
                    g.tensor_scalar(ms[:, i], ss[:, i], 1.0 / d, EPS, ALU.mult, ALU.add).then_inc(ms_done, 1)
                    g.wait_ge(ms_done, i + 1)
                    g.tensor_tensor(rs[:, i], ms[:, i], C["neghalf"][:, 0:H], ALU.pow).then_inc(rs_done, 1)

            @block.vector
            def _(v):
                ch = Chain(v, v_chain)
                v.wait_ge(c_in, 16)

                def reduce(i):
                    v.wait_ge(sq_done, i + 1)
                    v.tensor_reduce(ss[:, i], sq[:, i % 2], AX.X, ALU.add).then_inc(ss_done, 1)

                reduce(0)
                for i in range(n):
                    if i + 1 < n:
                        reduce(i + 1)
                    v.wait_ge(rs_done, i + 1)
                    v.wait_ge(x_in[i % 2], 16 * npiece * (i // 2 + 1))
                    if i >= 2:
                        v.wait_ge(turned, NB * (i - 1))
                    ch.done(v.tensor_tensor(y[:, i % 2], x[:, i % 2], rs[:, i].rearrange("p (h a) -> p h a", a=1).to_broadcast([P, H, d]), ALU.mult))
                    e = v.tensor_tensor(z[:, i % 2], y[:, i % 2], wr[:, :].rearrange("p (a d) -> p a d", a=1).to_broadcast([P, H, d]), ALU.mult)
                    if gate:
                        ch.done(e)
                        v.wait_ge(gt_done, i + 1)
                        ch.done(v.scalar_tensor_tensor(out=gt[:, i % 2], in0=gt[:, i % 2], scalar=1.0, in1=gr[:, i % 2], op0=ALU.add, op1=ALU.mult))
                        v.scalar_tensor_tensor(out=z[:, i % 2], in0=z[:, i % 2], scalar=0.5, in1=gt[:, i % 2], op0=ALU.mult, op1=ALU.mult).then_inc(ready, 1)
                        continue
                    tab = rope[2](i) if rope else None
                    if tab is None:
                        e.then_inc(ready, 1)
                        continue
                    ch.done(e)
                    o = rope[0]
                    zz = z[:, i % 2, :, o:o + 32 * na].rearrange("p h (a b q) -> p h a b q", a=na, b=2)
                    x1, x2 = zz[:, :, :, 0, :], zz[:, :, :, 1, :]
                    cs, sn = (u.rearrange("p (o a q) -> p o a q", o=1, a=na).to_broadcast([P, H, na, 16]) for u in tab)
                    v.tensor_tensor(t[:, 0], x1, cs, ALU.mult)
                    v.tensor_tensor(t[:, 1], x2, sn, ALU.mult)
                    v.tensor_tensor(t[:, 2], x1, sn, ALU.mult)
                    ch.done(v.tensor_tensor(t[:, 3], x2, cs, ALU.mult))
                    v.tensor_tensor(x1, t[:, 0], t[:, 1], ALU.subtract)
                    v.tensor_tensor(x2, t[:, 2], t[:, 3], ALU.add).then_inc(ready, 1)
                    v.wait_ge(ready, i + 1)

            @block.tensor
            def _(pe):
                for i in range(n):
                    pe.wait_ge(ready, i + 1)
                    zf = z[:, i % 2].rearrange("p h d -> p (h d)")
                    for b, (c0, cn, parts) in enumerate(blocks):
                        j = i * NB + b
                        if j >= 4:
                            pe.wait_ge(moved, j - 3)
                        pe.transpose(pt[0:cn, j % 4, 0:P], zf[:, c0:c0 + cn], C["ident"]).then_inc(turned, 1)


def project_heads(nc, name, C, hT, cols, w, d, chunk, weight, put, rope=None, copies=0, extra=None, values=None):
    K, N = w.shape
    kt = -(-K // P)
    kp = [min(P, K - k * P) for k in range(kt)]
    chunks = [(a, a + chunk) for a in range(0, N, chunk)]
    m = len(cols)
    de = extra.shape[-1] if extra is not None else 0
    dw = d - de
    hw = dw if values is None else 128
    hc = chunk // hw
    na = rope[1] if rope else 0
    steps = [(c, j) for c in range(len(chunks)) for j in range(m)]
    n = len(steps)
    width = hc * d * (2 * copies if copies else 1)
    bw = P if width % P == 0 and (copies or d % P == 0) else d
    nblk = width // bw
    groups = [(a, min(a + 4, nblk)) for a in range(0, nblk, 4)]
    G = len(groups)
    NX = 3
    LAG = 4 if copies else 3
    with Phase(nc, name) as f:
        wb = f.sb("w", [P, 2, kt, chunk])
        x = f.sb("x", [P, NX, hc, d])
        sq = f.sb("sq", [P, 2, hc, d])
        ss, ms, rs = (f.sb(s, [P, n, hc]) for s in ("ss", "ms", "rs"))
        y = f.sb("y", [P, hc, d])
        z = f.sb("z", [P, 2, hc, d])
        zz = f.sb("zz", [P, 2, hc, 2, copies, d]) if copies else z
        t = f.sb("t", [P, 4, hc, max(1, na), 16])
        wr = f.sb("wr", [P, d])
        acc = f.ps("acc", [P, 4, HALF])
        pt = f.ps("pt", [P, 4, HALF])
        w_in, c_in, mm_done, x_done, sq_done = f.sem2("w_in"), f.sem("c_in"), f.sem("mm_done"), f.sem("x_done"), f.sem("sq_done")
        ss_done, ms_done, rs_done, y_done, z_done = (f.sem(s) for s in ("ss_done", "ms_done", "rs_done", "y_done", "z_done"))
        first_done, ready, turned, moved, v_chain = (f.sem(s) for s in ("first_done", "ready", "turned", "moved", "v_chain"))
        NXD = 1 + (1 if extra is not None else 0)
        with nc.Block() as block:
            @block.sync
            def _(sp):
                full = K // P
                for c, (a, b) in enumerate(chunks):
                    if c >= 2:
                        sp.wait_ge(mm_done, (c - 1) * m)
                    sp.dma_start(wb[:, c % 2, 0:full], w[0:full * P, a:b].rearrange("(k p) n -> p k n", p=P)).then_inc(w_in[c % 2], 16)
                    if full < kt:
                        sp.dma_start(wb[0:kp[-1], c % 2, full], w[full * P:, a:b]).then_inc(w_in[c % 2], 16)
                    if c == 0:
                        sp.dma_start(wr[:, :], row_bcast(weight)).then_inc(c_in, 16)

            @block.tensor
            def _(pe):
                def turn(i):
                    pe.wait_ge(ready, i + 1)
                    zf = (zz[:, i % 2].rearrange("p h s r d -> p (h s r d)") if copies else z[:, i % 2].rearrange("p h d -> p (h d)"))
                    for g, (a, b) in enumerate(groups):
                        j = i * G + g
                        if j >= 4:
                            pe.wait_ge(moved, j - 3)
                        for u in range(a, b):
                            e = pe.transpose(pt[0:bw, j % 4, (u - a) * P:(u - a + 1) * P], zf[:, u * bw:(u + 1) * bw], C["ident"])
                        e.then_inc(turned, 1)

                for i in range(n + LAG):
                    if i < n:
                        c, j = steps[i]
                        pe.wait_ge(w_in[c % 2], 16 * (1 if K % P == 0 else 2) * (c // 2 + 1))
                        if i >= 4:
                            pe.wait_ge(x_done, NXD * (i - 3))
                        for k in range(kt):
                            mm = pe.matmul(acc[:, i % 4, 0:chunk], hT[0:kp[k], k, cols[j]:cols[j] + P], wb[0:kp[k], c % 2, k], start=(k == 0), stop=(k == kt - 1))
                        mm.then_inc(mm_done, 1)
                    if i >= LAG:
                        turn(i - LAG)

            @block.scalar
            def _(act):
                for i in range(n + LAG):
                    if i < n:
                        c, j = steps[i]
                        act.wait_ge(mm_done, i + 1)
                        if i >= NX:
                            act.wait_ge(y_done, i - NX + 1)
                        src = acc[:, i % 4, 0:chunk].rearrange("p (h d) -> p h d", h=hc)
                        if values is not None:
                            act.copy(values(c, j), src[:, :, dw:hw])
                        if extra is not None:
                            act.copy(x[:, i % NX, :, dw:d], extra[:, j].rearrange("p (o e) -> p o e", o=1).to_broadcast([P, hc, de])).then_inc(x_done, 1)
                        act.copy(x[:, i % NX, :, 0:dw], src[:, :, 0:dw]).then_inc(x_done, 1)
                        act.wait_ge(x_done, NXD * (i + 1))
                        if i >= 2:
                            act.wait_ge(ss_done, i - 1)
                        act.activation(sq[:, i % 2], x[:, i % NX], ACT.Square).then_inc(sq_done, 1)
                    if copies and 2 <= i <= n + 1:
                        k = i - 2
                        act.wait_ge(z_done, k + 1)
                        if k >= 2:
                            act.wait_ge(turned, G * (k - 1))
                        act.copy(zz[:, k % 2, :, 0].bitcast(F32R), z[:, k % 2].rearrange("p h (r d) -> p h r d", r=1).to_broadcast([P, hc, copies, d])).then_inc(first_done, 1)
                    if i >= LAG:
                        c, j = steps[i - LAG]
                        for g, (a, b) in enumerate(groups):
                            q = (i - LAG) * G + g
                            act.wait_ge(turned, q + 1)
                            act.copy(put(c, j, g), pt[0:bw, q % 4, 0:(b - a) * P].rearrange("p (b t) -> p b t", b=b - a)).then_inc(moved, 1)

            @block.gpsimd
            def _(g):
                for i in range(n):
                    g.wait_ge(ss_done, i + 1)
                    g.tensor_scalar(ms[:, i], ss[:, i], 1.0 / d, EPS, ALU.mult, ALU.add).then_inc(ms_done, 1)
                    g.wait_ge(ms_done, i + 1)
                    g.tensor_tensor(rs[:, i], ms[:, i], C["neghalf"][:, 0:hc], ALU.pow).then_inc(rs_done, 1)

            @block.vector
            def _(v):
                ch = Chain(v, v_chain)
                v.wait_ge(c_in, 16)

                def second(i):
                    v.wait_ge(first_done, i + 1)
                    v.tensor_tensor(zz[:, i % 2, :, 1].bitcast(F32R), z[:, i % 2].rearrange("p h (r d) -> p h r d", r=1).to_broadcast([P, hc, copies, d]), zz[:, i % 2, :, 0], ALU.subtract).then_inc(ready, 1)

                def main(i):
                    c, j = steps[i]
                    last = z_done if copies else ready
                    v.wait_ge(rs_done, i + 1)
                    if not copies and i >= 2:
                        v.wait_ge(turned, G * (i - 1))
                    if copies and i >= 2:
                        v.wait_ge(ready, i - 1)
                    if i:
                        v.wait_ge(z_done if copies else ready, i)
                    v.tensor_tensor(y[:, :, :], x[:, i % NX], rs[:, i].rearrange("p (h a) -> p h a", a=1).to_broadcast([P, hc, d]), ALU.mult).then_inc(y_done, 1)
                    v.wait_ge(y_done, i + 1)
                    e = v.tensor_tensor(z[:, i % 2], y[:, :, :], wr[:, :].rearrange("p (a d) -> p a d", a=1).to_broadcast([P, hc, d]), ALU.mult)
                    tab = rope[2](j) if rope else None
                    if tab is None:
                        e.then_inc(last, 1)
                        return
                    ch.done(e)
                    o = rope[0]
                    q = z[:, i % 2, :, o:o + 32 * na].rearrange("p h (a b q) -> p h a b q", a=na, b=2)
                    x1, x2 = q[:, :, :, 0, :], q[:, :, :, 1, :]
                    cs, sn = (u.rearrange("p (o a q) -> p o a q", o=1, a=na).to_broadcast([P, hc, na, 16]) for u in tab)
                    v.tensor_tensor(t[:, 0], x1, cs, ALU.mult)
                    v.tensor_tensor(t[:, 1], x2, sn, ALU.mult)
                    v.tensor_tensor(t[:, 2], x1, sn, ALU.mult)
                    ch.done(v.tensor_tensor(t[:, 3], x2, cs, ALU.mult))
                    v.tensor_tensor(x1, t[:, 0], t[:, 1], ALU.subtract)
                    v.tensor_tensor(x2, t[:, 2], t[:, 3], ALU.add).then_inc(last, 1)

                for i in range(n + 3):
                    if i < n:
                        v.wait_ge(sq_done, i + 1)
                        v.tensor_reduce(ss[:, i], sq[:, i % 2], AX.X, ALU.add).then_inc(ss_done, 1)
                    if copies and i >= 3:
                        second(i - 3)
                    if 1 <= i <= n:
                        main(i - 1)


def attend(nc, name, C, heads, nq, nkeys, scale):
    kt = nkeys // P
    banks = [(a, min(a + HALF, nkeys)) for a in range(0, nkeys, HALF)]
    nb = len(banks)
    NV = len(heads[0][1])
    m = heads[0][1][0][1]
    steps = [(h, q) for h in range(len(heads)) for q in range(nq)]
    n = len(steps)
    groups = [(a, min(a + 4, kt)) for a in range(0, kt, 4)]
    with Phase(nc, name) as f:
        pr = f.sb("pr", [P, 2, nkeys])
        pT = f.sb("pT", [P, 2, kt, P])
        mx, nm, sm, rc = (f.sb(x, [P, n]) for x in ("mx", "nm", "sm", "rc"))
        o = f.sb("o", [m, 2, NV, nq * P])
        S = [f.ps(f"S{b}", [P, nb, HALF]) for b in range(2)]
        O = f.ps("O", [P, 2, HALF])
        s_done, mx_done, nm_done, e_done, rc_done, p_done, turned = (f.sem(x) for x in ("s_done", "mx_done", "nm_done", "e_done", "rc_done", "p_done", "turned"))
        ev_a, ev_v, o_done, o_out, stored = f.sem("ev_a"), f.sem("ev_v"), f.sem("o_done"), f.sem("o_out"), f.sem2("stored")
        ga = [x for x in range(len(groups)) if x % 2 == 0]
        gv = [x for x in range(len(groups)) if x % 2 == 1]
        with nc.Block() as block:
            @block.tensor
            def _(pe):
                def scores(i):
                    h, q = steps[i]
                    if i >= 2:
                        pe.wait_ge(ev_a, i - 1)
                        if gv:
                            pe.wait_ge(ev_v, i - 1)
                    for b, (a, z) in enumerate(banks):
                        for c, (qT, kT) in enumerate(heads[h][0]):
                            mm = pe.matmul(S[i % 2][:, b, 0:z - a], qT[:, q * P:(q + 1) * P], kT[:, a:z], start=(c == 0), stop=(c == len(heads[h][0]) - 1))
                    mm.then_inc(s_done, 1)

                def turn(i):
                    pe.wait_ge(p_done, i + 1)
                    for g, (a, z) in enumerate(groups):
                        for k in range(a, z):
                            mm = pe.transpose(S[i % 2][:, g, (k - a) * P:(k - a + 1) * P], pr[:, i % 2, k * P:(k + 1) * P], C["ident"])
                    mm.then_inc(turned, 1)

                def values(i):
                    h, q = steps[i]
                    pe.wait_ge(ev_a, i + 1)
                    if gv:
                        pe.wait_ge(ev_v, i + 1)
                    if i >= 2:
                        pe.wait_ge(o_out, i - 1)
                    for w, (vf, mm_) in enumerate(heads[h][1]):
                        for k in range(kt):
                            mm = pe.matmul(O[0:m, i % 2, w * P:w * P + P], vf(k), pT[:, i % 2, k], start=(k == 0), stop=(k == kt - 1))
                    mm.then_inc(o_done, 1)

                for i in range(n + 2):
                    if i < n:
                        scores(i)
                    if 1 <= i <= n:
                        turn(i - 1)
                    if i >= 2:
                        values(i - 2)

            @block.vector
            def _(v):
                def evict(i):
                    v.wait_ge(turned, i + 1)
                    if i >= 2:
                        v.wait_ge(o_done, i - 1)
                    for g in gv:
                        a, z = groups[g]
                        e = v.tensor_copy(pT[:, i % 2, a:z], S[i % 2][:, g, 0:(z - a) * P].rearrange("p (k q) -> p k q", k=z - a))
                    if gv:
                        e.then_inc(ev_v, 1)

                def out(i):
                    h, q = steps[i]
                    v.wait_ge(o_done, i + 1)
                    if h >= 2:
                        v.wait_ge(stored[h % 2], 16 * NV * (h // 2))
                    v.tensor_copy(o[:, h % 2, :, q * P:(q + 1) * P], O[0:m, i % 2, 0:NV * P].rearrange("p (w q) -> p w q", w=NV)).then_inc(o_out, 1)

                for i in range(n + 2):
                    if i < n:
                        v.wait_ge(s_done, i + 1)
                        v.tensor_reduce(mx[:, i:i + 1], S[i % 2][:, :, :].rearrange("p b n -> p (b n)")[:, 0:nkeys], AX.X, ALU.max).then_inc(mx_done, 1)
                        v.wait_ge(mx_done, i + 1)
                        v.tensor_scalar(nm[:, i:i + 1], mx[:, i:i + 1], -scale, None, ALU.mult).then_inc(nm_done, 1)
                    if 1 <= i <= n:
                        evict(i - 1)
                    if i < n:
                        v.wait_ge(e_done, i + 1)
                        v.reciprocal(rc[:, i:i + 1], sm[:, i:i + 1]).then_inc(rc_done, 1)
                        v.wait_ge(rc_done, i + 1)
                        v.tensor_scalar(pr[:, i % 2], pr[:, i % 2], rc[:, i:i + 1], None, ALU.mult).then_inc(p_done, 1)
                    if i >= 2:
                        out(i - 2)

            @block.scalar
            def _(act):
                def evict(i):
                    act.wait_ge(turned, i + 1)
                    if i >= 2:
                        act.wait_ge(o_done, i - 1)
                    for g in ga:
                        a, z = groups[g]
                        e = act.copy(pT[:, i % 2, a:z], S[i % 2][:, g, 0:(z - a) * P].rearrange("p (k q) -> p k q", k=z - a))
                    e.then_inc(ev_a, 1)

                for i in range(n + 1):
                    if i >= 1:
                        evict(i - 1)
                    if i < n:
                        act.wait_ge(nm_done, i + 1)
                        if i >= 2:
                            act.wait_ge(turned, i - 1)
                        act.activation(pr[:, i % 2], S[i % 2][:, :, :].rearrange("p b n -> p (b n)")[:, 0:nkeys], ACT.Exp, bias=nm[:, i:i + 1], scale=scale, accum_out=sm[:, i:i + 1]).then_inc(e_done, 1)

            @block.gpsimd
            def _(g):
                for h in range(len(heads)):
                    g.wait_ge(o_out, nq * (h + 1))
                    for w in range(NV):
                        g.dma_start(heads[h][2][w], o[:, h % 2, w]).then_inc(stored[h % 2], 16)
                for b in range(2):
                    g.wait_ge(stored[b], 16 * NV * len(range(b, len(heads), 2)))


def out_project_t(nc, name, C, aT_dram, w, n, resid, dst, gate=None, silu_rows=None):
    K = w.shape[0]
    kt = K // P
    G = kt // 4
    with Phase(nc, name) as f:
        wb = f.sb("w", [P, 2, 4, HALF])
        a = f.sb("a", [P, 2, kt, P])
        b_ = f.sb("b", [P, 2, kt, P]) if silu_rows is not None else a
        g_ = f.sb("g", [P, 2, K]) if silu_rows is not None else None
        th = f.sb("th", [P, 2, K]) if silu_rows is not None else None
        w1, w2 = (f.sb(x, [P, kt, D], F32R) for x in ("w1", "w2"))
        b1, b2 = (f.sb(x, [P, 2, kt, P], F32R) for x in ("b1", "b2"))
        rounded, w_split, merged, b1_done = f.sem("rounded"), f.sem("w_split"), f.sem("merged"), f.sem("b1_done")
        r, y, gb = f.sb("r", [P, 2, D]), f.sb("y", [P, 2, D]), f.sb("gb", [P, D])
        pt = f.ps("pt", [P, 2, 4, P])
        acc = f.ps("acc", [P, 2, 2, HALF])
        w_in, c_in, a_in, r_in, g_in, th_done, gs_done = f.sem2("w_in", 2 * G), f.sem("c_in"), f.sem2("a_in"), f.sem2("r_in"), f.sem2("g_in"), f.sem("th_done"), f.sem("gs_done")
        turned, at_done, mm_done, v_chain, y_done, stored = f.sem("turned"), f.sem("at_done"), f.sem("mm_done"), f.sem("v_chain"), f.sem("y_done"), f.sem2("stored")
        with nc.Block() as block:
            @block.sync
            def _(sp):
                def load_a(i):
                    if i >= 2 and g_ is not None:
                        sp.wait_ge(merged, G * (i - 1))
                    elif i >= 2:
                        sp.wait_ge(at_done, G * (i - 1))
                    sp.dma_start(a[:, i % 2], aT_dram[:, i * P:(i + 1) * P].rearrange("(k p) t -> p k t", p=P)).then_inc(a_in[i % 2], 16)

                def load_g(i):
                    if i >= 2:
                        sp.wait_ge(gs_done, i - 1)
                    sp.dma_start(g_[:, i % 2], silu_rows[i * P:(i + 1) * P, :]).then_inc(g_in[i % 2], 16)

                if g_ is not None:
                    load_g(0)
                load_a(0)
                for p in range(2 * G):
                    h, q = p // G, p % G
                    if p >= 2:
                        sp.wait_ge(w_split, p - 1)
                    sp.dma_start(wb[:, p % 2], w[4 * q * P:4 * (q + 1) * P, h * HALF:(h + 1) * HALF].rearrange("(k p) n -> p k n", p=P)).then_inc(w_in[p], 16)
                if gate is not None:
                    sp.dma_start(gb[:, :], row_bcast(gate)).then_inc(c_in, 16)
                for i in range(n):
                    if i + 1 < n:
                        if g_ is not None:
                            load_g(i + 1)
                        load_a(i + 1)
                    if i >= 2:
                        sp.wait_ge(y_done, i - 1)
                    sp.dma_start(r[:, i % 2], resid[i * P:(i + 1) * P, :]).then_inc(r_in[i % 2], 16)

            @block.tensor
            def _(pe):
                def turn(i, q):
                    pe.wait_ge(gs_done, i + 1)
                    j = i * G + q
                    if j >= 2:
                        pe.wait_ge(merged, j - 1)
                    for u in range(4):
                        k = 4 * q + u
                        e = pe.transpose(pt[:, j % 2, u], th[:, i % 2, k * P:(k + 1) * P], C["ident"])
                    e.then_inc(turned, 1)

                if g_ is not None:
                    for q in range(G):
                        turn(0, q)
                for i in range(n):
                    if i >= 2:
                        pe.wait_ge(y_done, i - 1)
                    for h in range(2):
                        for q in range(G):
                            if i == 0:
                                pe.wait_ge(w_split, h * G + q + 1)
                            if h == 0:
                                pe.wait_ge(at_done, G * i + q + 1)
                            ns = slice(h * HALF, (h + 1) * HALF)
                            for t, (x, y_) in enumerate(((b1, w1), (b1, w2), (b2, w1))):
                                for k in range(4 * q, 4 * q + 4):
                                    mm = pe.matmul(acc[:, i % 2, h], x[:, i % 2, k], y_[:, k, ns], start=(t == 0 and k == 0), stop=(t == 2 and k == kt - 1))
                            if g_ is not None and i + 1 < n and (h * G + q) % 2 == 0:
                                turn(i + 1, (h * G + q) // 2)
                    mm.then_inc(mm_done, 1)

            def piece(p):
                h, q = p // G, p % G
                at = (slice(None), slice(4 * q, 4 * q + 4), slice(h * HALF, (h + 1) * HALF))
                return w1[at], w2[at], wb[:, p % 2]

            @block.scalar
            def _(act):
                def tanh(i):
                    act.wait_ge(g_in[i % 2], 16 * (i // 2 + 1))
                    if i >= 2:
                        act.wait_ge(turned, G * (i - 1))
                    act.activation(th[:, i % 2], g_[:, i % 2], ACT.Tanh, scale=0.5).then_inc(th_done, 1)

                def first_parts(i):
                    for q in range(G):
                        if g_ is not None:
                            act.wait_ge(merged, G * i + q + 1)
                        else:
                            act.wait_ge(a_in[i % 2], 16 * (i // 2 + 1))
                        if i >= 2:
                            act.wait_ge(mm_done, i - 1)
                        act.copy(b1[:, i % 2, 4 * q:4 * q + 4], b_[:, i % 2, 4 * q:4 * q + 4]).then_inc(b1_done, 1)

                if g_ is not None:
                    tanh(0)
                first_parts(0)
                for p in range(2 * G):
                    act.wait_ge(w_in[p], 16)
                    first, _, whole = piece(p)
                    act.copy(first, whole).then_inc(rounded, 1)
                for i in range(1, n):
                    if g_ is not None:
                        tanh(i)
                    first_parts(i)

            @block.vector
            def _(v):
                ch = Chain(v, v_chain)
                def silu(i):
                    v.wait_ge(th_done, i + 1)
                    v.scalar_tensor_tensor(out=th[:, i % 2], in0=th[:, i % 2], scalar=1.0, in1=g_[:, i % 2], op0=ALU.add, op1=ALU.mult).then_inc(gs_done, 1)

                def merge(i):
                    for q in range(G):
                        j = i * G + q
                        v.wait_ge(turned, j + 1)
                        v.wait_ge(a_in[i % 2], 16 * (i // 2 + 1))
                        if i >= 2:
                            v.wait_ge(mm_done, i - 1)
                        v.scalar_tensor_tensor(out=b_[:, i % 2, 4 * q:4 * q + 4], in0=pt[:, j % 2], scalar=0.5, in1=a[:, i % 2, 4 * q:4 * q + 4], op0=ALU.mult, op1=ALU.mult).then_inc(merged, 1)

                def second_parts(i):
                    for q in range(G):
                        v.wait_ge(b1_done, G * i + q + 1)
                        v.tensor_tensor(b2[:, i % 2, 4 * q:4 * q + 4], b_[:, i % 2, 4 * q:4 * q + 4], b1[:, i % 2, 4 * q:4 * q + 4].bitcast(F32), ALU.subtract).then_inc(at_done, 1)

                def prepare(i):
                    if g_ is not None:
                        silu(i)
                        merge(i)
                    second_parts(i)

                prepare(0)
                for p in range(2 * G):
                    v.wait_ge(rounded, p + 1)
                    first, second, whole = piece(p)
                    v.tensor_tensor(second, whole, first.bitcast(F32), ALU.subtract).then_inc(w_split, 1)
                for i in range(n):
                    if i + 1 < n:
                        prepare(i + 1)
                    v.wait_ge(mm_done, i + 1)
                    v.wait_ge(r_in[i % 2], 16 * (i // 2 + 1))
                    if i == 0 and gate is not None:
                        v.wait_ge(c_in, 16)
                    if i >= 2:
                        v.wait_ge(stored[i % 2], 16 * (i // 2))
                    z = acc[:, i % 2].rearrange("p h n -> p (h n)")
                    if gate is not None:
                        ch.done(v.tensor_tensor(y[:, i % 2], z, gb[:, :], ALU.mult))
                        z = y[:, i % 2]
                    v.tensor_tensor(y[:, i % 2], z, r[:, i % 2], ALU.add).then_inc(y_done, 1)

            @block.gpsimd
            def _(g):
                for i in range(n):
                    g.wait_ge(y_done, i + 1)
                    g.dma_start(dst[i * P:(i + 1) * P, :], y[:, i % 2]).then_inc(stored[i % 2], 16)
                for b in range(2):
                    g.wait_ge(stored[b], 16 * len(range(b, n, 2)))


def move(nc, name, pairs, zero=()):
    with Phase(nc, name) as f:
        s, z = f.sem("moved"), f.sem("zeroed")
        with nc.Block() as block:
            @block.vector
            def _(v):
                for i, a in enumerate(zero):
                    v.memset(a, 0.0).then_inc(z, 1)
                if zero:
                    v.wait_ge(z, len(zero))

            @block.sync
            def _(sp):
                for dst, src in pairs:
                    sp.dma_start(dst, src).then_inc(s, 16)
                sp.wait_ge(s, 16 * len(pairs))


def attention_layer(nc, C, A, S, hT):
    W, KW = D, D // 4
    with ExitStack() as c2:
        sb = lambda name, shape: c2.enter_context(nc.sbuf_tensor(name, shape, F32))
        w = A["a_in_w"][0]
        project(nc, "a_g", hT, [CTX + i * P for i in range(LT)], w[:, W + 2 * KW:], S["ag"])
        cs, sn = C["ropec"], C["ropes"]
        table = lambda j: (cs[:, 32 * j:32 * j + 32], sn[:, 32 * j:32 * j + 32])
        vv = sb("a_v", [P, TT, KW])
        project(nc, "a_vp", hT, [i * P for i in range(TT)], w[:, W + KW:W + 2 * KW], chunk=KW, put=lambda j, a, b: vv[:, j, a:b])
        kT = c2.enter_context(nc.sbuf_tensor("a_kT", [P, 4, 2, T], F32R))
        project_heads(nc, "a_k", C, hT, [i * P for i in range(TT)], w[:, W:W + KW], 64, KW, A["a_k_norm"][0],
                      lambda c, j, g: kT[:, 2 * g:2 * g + 2, :, j * P:(j + 1) * P].rearrange("p g s t -> p (g s) t"),
                      rope=(0, 2, lambda j: None if j < CT else table(j - CT)), copies=2)
        qT = c2.enter_context(nc.sbuf_tensor("a_qT", [P, 16, LAT], F32R))
        project_heads(nc, "a_q", C, hT, [CTX + i * P for i in range(LT)], w[:, 0:W], 64, KW, A["a_q_norm"][0],
                      lambda c, j, g: qT[:, 4 * c:4 * c + 4, j * P:(j + 1) * P], rope=(0, 2, table), copies=1)
        heads = [([(qT[:, h], kT[:, h // 4, s]) for s in range(2)],
                  [((lambda g: lambda k: vv[:, k, g * 64:(g + 1) * 64])(h // 4), 64)],
                  [S["aoT"][h * 64:(h + 1) * 64, :]]) for h in range(16)]
        attend(nc, "a_at", C, heads, LT, T, 64 ** -0.5)
    out_project_t(nc, "a_out", C, S["aoT"], A["a_out_w"][0], LT, S["h1"][CTX:T, :], S["h2"], gate=S["mod"][0, 1, 2 * D:3 * D], silu_rows=S["ag"])


NG, NHG, HD, NS_, DI = 8, 4, 64, 128, 2 * D
NH = NG * NHG
GW = NHG * HD
CONV = 5
XBC = 2 * DI


def mamba_steps(nc, C, A, hT, dt, la, ecum, tend, edec, la1, la2, masks):
    c0 = DI + XBC
    H2 = 2 * NH
    with Phase(nc, "dt") as f:
        w = f.sb("w", [P, KD, H2])
        bias, al = f.sb("bias", [P, H2]), f.sb("al", [P, H2])
        x, e, u, t1, t2 = (f.sb(n, [P, TT, H2]) for n in ("x", "e", "u", "t1", "t2"))
        raw = f.ps("raw", [P, 2, 8, H2])
        cum = f.ps("cum", [P, 2, HALF])
        tot = f.ps("tot", [P, 2, HALF])
        c_in, r_done, v_chain, a_chain, cum_done = f.sem("c_in"), f.sem("r_done"), f.sem("v_chain"), f.sem("a_chain"), f.sem("cum_done")
        with nc.Block() as block:
            @block.sync
            def _(sp):
                with nc.allow_non_contiguous_dma(reason="64 columns"):
                    sp.dma_start(w[:, :, :], A["m_in_w"][0][:, c0:c0 + H2].rearrange("(k p) n -> p k n", p=P)).then_inc(c_in, 16)
                sp.dma_start(bias[:, :], row_bcast(A["m_dt_bias"][0].rearrange("a h -> (a h)"))).then_inc(c_in, 16)
                sp.dma_start(al[:, :], row_bcast(A["m_a_log"][0].rearrange("a h -> (a h)"))).then_inc(c_in, 16)

            @block.tensor
            def _(pe):
                pe.wait_ge(c_in, 48)
                for j in range(TT):
                    for k in range(KD):
                        mm = pe.matmul(raw[:, j // 8, j % 8], hT[:, k, j * P:(j + 1) * P], w[:, k], start=(k == 0), stop=(k == KD - 1))
                mm.then_inc(r_done, 1)
                pe.wait_ge(v_chain, 12)
                for d, m in ((0, "le"), (1, "ge")):
                    sl = slice(d * NH, (d + 1) * NH)
                    pe.matmul(cum[:, d, 0:TT * NH].rearrange("p (j h) -> p j h", j=TT), C[m], la[:, :, sl], start=True, stop=True)
                    mm = pe.matmul(tot[:, d, 0:TT * NH].rearrange("p (j h) -> p j h", j=TT), C["ones"], la[:, :, sl], start=True, stop=True)
                mm.then_inc(cum_done, 1)

            @block.vector
            def _(v):
                ch = Chain(v, v_chain)
                v.wait_ge(c_in, 48)
                v.wait_ge(r_done, 1)
                for b, (j0, j1) in enumerate(((0, 8), (8, TT))):
                    ch.done(v.tensor_tensor(x[:, j0:j1], raw[:, b, 0:j1 - j0], bias[:, :].rearrange("p (a h) -> p a h", a=1).to_broadcast([P, j1 - j0, H2]), ALU.add))
                v.wait_ge(a_chain, 3)
                ch.done(v.tensor_scalar(u[:, :, :], e[:, :, :], 1.0, None, ALU.add))
                v.wait_ge(a_chain, 4)
                ch.done(v.scalar_tensor_tensor(out=t2[:, :, :], in0=u[:, :, :], scalar=-1.0, in1=e[:, :, :], op0=ALU.add, op1=ALU.subtract))
                ch.done(v.reciprocal(u[:, :, :], u[:, :, :]))
                ch.done(v.tensor_tensor(t2[:, :, :], t2[:, :, :], u[:, :, :], ALU.mult))
                ch.done(v.tensor_tensor(t1[:, :, :], t1[:, :, :], t2[:, :, :], ALU.subtract))
                ch.done(v.scalar_tensor_tensor(out=dt, in0=x[:, :, :], scalar=0.0, in1=t1[:, :, :], op0=ALU.max, op1=ALU.add))
                ch.done(v.tensor_scalar(al[:, :], al[:, :], -1.0, None, ALU.mult))
                ch.done(v.tensor_tensor(la, dt, al[:, :].rearrange("p (a h) -> p a h", a=1).to_broadcast([P, TT, H2]), ALU.mult))
                ch.done(v.tensor_copy(la1, la))
                ch.done(v.tensor_tensor(la2, la, la1.bitcast(F32), ALU.subtract))
                for i, m in enumerate(("gt", "lt")):
                    v.tensor_copy(masks[:, i], C[m])
                v.wait_ge(cum_done, 1)
                for d in range(2):
                    sl = slice(d * NH, (d + 1) * NH)
                    ch.done(v.tensor_copy(x[:, :, sl], cum[:, d, 0:TT * NH].rearrange("p (j h) -> p j h", j=TT)))
                    ch.done(v.tensor_copy(e[:, :, sl], tot[:, d, 0:TT * NH].rearrange("p (j h) -> p j h", j=TT)))
                ch.done(v.tensor_tensor(t1[:, :, :], e[:, :, :], x[:, :, :], ALU.subtract))
                v.wait_ge(a_chain, 5)
                ch.done(v.tensor_tensor(tend, t2[:, :, :], dt, ALU.mult))

            @block.scalar
            def _(act):
                ch = Chain(act, a_chain)
                act.wait_ge(c_in, 48)
                ch.done(act.activation(al[:, :], al[:, :], ACT.Exp))
                act.wait_ge(v_chain, 2)
                ch.done(act.activation(e[:, :, :], x[:, :, :], ACT.Abs))
                ch.done(act.activation(e[:, :, :], e[:, :, :], ACT.Exp, scale=-1.0))
                act.wait_ge(v_chain, 3)
                ch.done(act.activation(t1[:, :, :], u[:, :, :], ACT.Ln))
                act.wait_ge(v_chain, 17)
                ch.done(act.activation(t2[:, :, :], t1[:, :, :], ACT.Exp))
                ch.done(act.activation(ecum, x[:, :, :], ACT.Exp))
                ch.done(act.activation(edec, e[:, :, :], ACT.Exp))


SCAN = [s for k in range(TT) for s in ((0, k), (1, (CT - 1 - k) if k < CT else TT - 1 - (k - CT)))]
PAD = CONV // 2
UW = T + 4 * PAD
LAT0 = CTX + 3 * PAD


def mamba_groups(nc, C, A, S, hT, dt, ecum, tend, edec, la1, la2, masks):
    w_in_w = A["m_in_w"][0]
    H2 = 2 * NH
    TILES = 4
    spans = [(0, CTX, PAD), (CTX, CTX + HALF, LAT0), (CTX + HALF, T, LAT0 + HALF)]
    OUTS = [(0, CTX, 0), (LAT0 - PAD, LAT0 - PAD + LAT, CTX)]

    def chan(g, c):
        return (g * GW + c * P, g * GW + c * P, DI + g * NS_, DI + NG * NS_ + g * NS_)[c] if c >= 2 else g * GW + c * P

    with Phase(nc, "mg") as f:
        wx = f.sb("wx", [P, KD, TILES, P])
        wz = f.sb("wz", [P, KD, GW])
        u = f.sb("u", [P, TILES, UW])
        cv = f.sb("cv", [P, TILES, T])
        acc_ = f.sb("ca", [P, UW - 2 * PAD])
        cw = f.sb("cw", [P, NG * TILES, CONV + 1])
        xt = f.sb("xt", [P, TT, GW])
        bt = f.sb("bt", [P, TT, NS_])
        cb = f.sb("cb", [P, 2, TT, P])
        zt = f.sb("zt", [P, TT, GW])
        yy = f.sb("yy", [P, TT, GW])
        dsk = f.sb("dsk", [P, NH])
        L = f.sb("L", [P, 2, 2, NHG, P], F32R)
        E, W = f.sb("E", [P, 2, NHG, P]), f.sb("W", [P, 2, NHG, P])
        xd, xe = f.sb("xd", [P, 2, GW]), f.sb("xe", [P, 2, GW])
        st = f.sb("st", [P, 2, GW])
        tmp = f.sb("tmp", [P, GW])
        acc = f.ps("acc", [P, 2, HALF])
        trp = f.ps("tr", [P, HALF])
        seg = f.ps("seg", [P, 2, NHG, P])
        Yp = f.ps("Y", [P, 2, 2, GW])
        Sp = f.ps("S", [P, HALF])
        c_in, wx_in, wz_in = f.sem("c_in"), f.sem("wx_in"), f.sem("wz_in")
        p_mm, u_done, conv_done, z_mm, z_done, zt_done, tr_mm, tr_done = (f.sem(n) for n in ("p_mm", "u_done", "conv_done", "z_mm", "z_done", "zt_done", "tr_mm", "tr_done"))
        cb_mm, cb_done, L_done, seg_mm, E_done, W_done, xe_done, y_mm, s_mm, s_done, y_done = (f.sem(n) for n in ("cb_mm", "cb_done", "L_done", "seg_mm", "E_done", "W_done", "xe_done", "y_mm", "s_mm", "s_done", "y_done"))
        v_chain, a_chain, th_done, g_done, stored, y_init, mt, ca_done = (f.sem(n) for n in ("v_chain", "a_chain", "th_done", "g_done", "stored", "y_init", "mt", "ca_done"))
        n3 = len(spans)

        def turn_bank(j):
            return (trp[:, :], seg[:, 0].rearrange("p h t -> p (h t)"), seg[:, 1].rearrange("p h t -> p (h t)"))[j % 3]

        NSC = len(SCAN)

        with nc.Block() as block:
            @block.sync
            def _(sp):
                with nc.allow_non_contiguous_dma(reason="taps by channel"):
                    for g in range(NG):
                        for c in range(TILES):
                            a = chan(g, c)
                            sp.dma_start(cw[:, g * TILES + c, 0:CONV], A["m_conv_w"][0][:, a:a + P].rearrange("t p -> p t")).then_inc(c_in, 16)
                            sp.dma_start(cw[:, g * TILES + c, CONV:CONV + 1], A["m_conv_b"][0][a:a + P].rearrange("(p a) -> p a", a=1)).then_inc(c_in, 16)
                sp.dma_start(dsk[:, :], row_bcast(A["m_d"][0])).then_inc(c_in, 16)

                def load_x(g):
                    if g >= 1:
                        sp.wait_ge(p_mm, TILES * n3 * g)
                    for c in range(TILES):
                        a = DI + chan(g, c)
                        sp.dma_start(wx[:, :, c], w_in_w[:, a:a + P].rearrange("(k p) n -> p k n", p=P)).then_inc(wx_in, 16)

                def load_z(g):
                    if g >= 1:
                        sp.wait_ge(z_mm, TT * g)
                    sp.dma_start(wz[:, :, :], w_in_w[:, g * GW:(g + 1) * GW].rearrange("(k p) n -> p k n", p=P)).then_inc(wz_in, 16)

                load_x(0)
                load_z(0)
                for g in range(NG):
                    if g + 1 < NG:
                        load_x(g + 1)
                        load_z(g + 1)

            @block.tensor
            def _(pe):
                pa = [0]

                def bank():
                    i = pa[0]
                    pa[0] += 1
                    return i % 2

                hist = []

                def claim(sem, value):
                    if len(hist) >= 2:
                        pe.wait_ge(*hist[-2])
                    hist.append((sem, value))
                    return bank()

                def proj(g, piece):
                    if piece == 0:
                        pe.wait_ge(wx_in, 16 * TILES * (g + 1))
                    c, s = piece // n3, piece % n3
                    a, b, _ = spans[s]
                    i = (g * TILES + c) * n3 + s
                    q = claim(u_done, i + 1)
                    for k in range(KD):
                        mm = pe.matmul(acc[:, q, 0:b - a], wx[:, k, c], hT[:, k, a:b], start=(k == 0), stop=(k == KD - 1))
                    mm.then_inc(p_mm, 1)

                def gate(g):
                    pe.wait_ge(wz_in, 16 * (g + 1))
                    for j in range(TT):
                        q = claim(z_done, g * TT + j + 1)
                        for k in range(KD):
                            mm = pe.matmul(acc[:, q, 0:GW], hT[:, k, j * P:(j + 1) * P], wz[:, k], start=(k == 0), stop=(k == KD - 1))
                        mm.then_inc(z_mm, 1)

                def scan(g):
                    pe.wait_ge(conv_done, TILES * (g + 1))
                    for j in range(TT):
                        i = g * TT + j
                        t = slice(j * P, (j + 1) * P)
                        tr = turn_bank(j)
                        if j >= 3:
                            pe.wait_ge(cb_done, i - 2)
                            pe.wait_ge(tr_done, 2 * (i - 2))
                        elif g >= 1:
                            pe.wait_ge(E_done, g * NSC)
                        for c in range(3):
                            mm = pe.transpose(tr[:, c * P:(c + 1) * P], cv[:, c, t], C["ident"])
                        mm.then_inc(tr_mm, 1)
                        pe.matmul(tr[:, 3 * P:4 * P], cv[:, 2, t], cv[:, 3, t], start=True, stop=True).then_inc(cb_mm, 1)
                    pe.wait_ge(cb_done, (g + 1) * TT)
                    pe.wait_ge(tr_done, 2 * (g + 1) * TT)
                    for k in range(NSC + 1):
                        if k < NSC:
                            d, j = SCAN[k]
                            i = g * NSC + k
                            pe.wait_ge(L_done, i + 1)
                            if i >= 2:
                                pe.wait_ge(E_done, i - 1)
                            for r in range(2):
                                mm = pe.matmul(seg[:, i % 2].rearrange("p h t -> p (h t)"), masks[:, d], L[:, i % 2, r].rearrange("p h t -> p (h t)"), start=(r == 0), stop=(r == 1))
                            mm.then_inc(seg_mm, 1)
                        if k >= 1:
                            d, j = SCAN[k - 1]
                            i = g * NSC + k - 1
                            pe.wait_ge(W_done, i + 1)
                            if i >= 2:
                                pe.wait_ge(y_done, i - 1)
                            for h in range(NHG):
                                mm = pe.matmul(Yp[:, i % 2, 0, h * HD:(h + 1) * HD], W[:, i % 2, h], xd[:, i % 2, h * HD:(h + 1) * HD], start=True, stop=True)
                            if k - 1 >= 2:
                                pe.wait_ge(s_done, i - 1)
                                mm = pe.matmul(Yp[:, i % 2, 1], cv[:, 3, j * P:(j + 1) * P], st[:, d], start=True, stop=True)
                            mm.then_inc(y_mm, 1)
                            pe.wait_ge(xe_done, i + 1)
                            if i >= 1:
                                pe.wait_ge(s_done, i)
                            pe.matmul(Sp[:, 0:GW], bt[:, j], xe[:, i % 2], start=True, stop=True).then_inc(s_mm, 1)
                        if g + 1 < NG:
                            for piece in pieces_at(k):
                                proj(g + 1, piece)

                for piece in range(PIECES):
                    proj(0, piece)
                gate(0)
                for g in range(NG):
                    scan(g)
                    if g + 1 < NG:
                        gate(g + 1)

            @block.scalar
            def _(act):
                def evict_u(g, piece):
                    c, s = piece // n3, piece % n3
                    a, b, o = spans[s]
                    i = g * PIECES + piece
                    act.wait_ge(p_mm, i + 1)
                    if g >= 1:
                        act.wait_ge(conv_done, (g - 1) * TILES + c + 1)
                    act.copy(u[:, c, o:o + b - a], acc[:, bank_of[("p", i)], 0:b - a]).then_inc(u_done, 1)

                def tanh_conv(g, c):
                    i = g * TILES + c
                    act.wait_ge(ca_done, i + 1)
                    for a, b, o in OUTS:
                        e = act.activation(u[:, c, PAD + a:PAD + b], acc_[:, a:b], ACT.Tanh)
                    e.then_inc(th_done, 1)

                def gate_in(g, j):
                    i = g * TT + j
                    act.wait_ge(z_mm, i + 1)
                    if g >= 1:
                        act.wait_ge(g_done, TT * g)
                    act.activation(zt[:, j], acc[:, bank_of[("z", i)], 0:GW], ACT.Tanh, scale=0.5).then_inc(zt_done, 1)

                def between(g):
                    for j in range(TT):
                        gate_in(g, j)
                        if g == 0 and j % 2 == 1 and j // 2 < TILES:
                            tanh_conv(g, j // 2)
                        if g >= 1 and j == 3:
                            tanh_conv(g, TILES - 1)

                def scan(g):
                    for j in range(TT):
                        i = g * TT + j
                        act.wait_ge(tr_mm, i + 1)
                        act.wait_ge(cb_mm, i + 1)
                        if g >= 1 and j == 0:
                            act.wait_ge(s_mm, NSC * g)
                            act.wait_ge(xe_done, NSC * g)
                            act.wait_ge(W_done, NSC * g)
                        tr = turn_bank(j)
                        act.copy(xt[:, j], tr[:, 0:GW]).then_inc(tr_done, 1)
                        act.copy(bt[:, j], tr[:, GW:GW + NS_]).then_inc(tr_done, 1)
                    for k in range(NSC):
                        i = g * NSC + k
                        act.wait_ge(seg_mm, i + 1)
                        if i >= 2:
                            act.wait_ge(W_done, i - 1)
                        act.activation(E[:, i % 2], seg[:, i % 2], ACT.Exp).then_inc(E_done, 1)
                        if g + 1 < NG:
                            for piece in pieces_at(k):
                                evict_u(g + 1, piece)
                            if k in TANH_AT:
                                tanh_conv(g + 1, TANH_AT.index(k))

                for piece in range(PIECES):
                    evict_u(0, piece)
                between(0)
                for g in range(NG):
                    scan(g)
                    if g + 1 < NG:
                        between(g + 1)

            @block.gpsimd
            def _(p):
                for g in range(NG):
                    def steps(k):
                        d, j = SCAN[k]
                        i = g * NSC + k
                        if i >= 2:
                            p.wait_ge(seg_mm, i - 1)
                        m = C["le" if d == 0 else "ge"].rearrange("p (a s) -> p a s", a=1).to_broadcast([P, NHG, P])
                        hs = slice(d * NH + g * NHG, d * NH + (g + 1) * NHG)
                        for r, part in enumerate((la1, la2)):
                            e = p.tensor_tensor(L[:, i % 2, r], m, part[:, j, hs].bitcast(F32).rearrange("p (h a) -> p h a", a=1).to_broadcast([P, NHG, P]), ALU.mult)
                        e.then_inc(L_done, 1)

                    steps(0)
                    steps(1)
                    p.wait_ge(tr_done, 2 * TT * (g + 1))
                    if g == 0:
                        p.wait_ge(c_in, 16 * (2 * NG * TILES + 1))
                    if g >= 1:
                        p.wait_ge(stored, 16 * TT * g)
                    for k in range(NSC):
                        d, j = SCAN[k]
                        if k in [s[1] for s in FIRST]:
                            p.tensor_tensor(yy[:, j].rearrange("p (h d) -> p h d", h=NHG), xt[:, j].rearrange("p (h d) -> p h d", h=NHG), dsk[:, g * NHG:(g + 1) * NHG].rearrange("p (h a) -> p h a", a=1).to_broadcast([P, NHG, HD]), ALU.mult).then_inc(y_init, 1)
                        if k + 2 < NSC:
                            steps(k + 2)
                    for j in range(TT):
                        p.wait_ge(g_done, g * TT + j + 1)
                        p.dma_start(S["my"][j * P:(j + 1) * P, g * GW:(g + 1) * GW], yy[:, j]).then_inc(stored, 16)
                p.wait_ge(stored, 16 * TT * NG)

            @block.vector
            def _(v):
                ch = Chain(v, v_chain)
                for c in range(TILES):
                    v.memset(u[:, c, 0:PAD], 0.0)
                    v.memset(u[:, c, PAD + CTX:LAT0], 0.0)
                    ch.done(v.memset(u[:, c, UW - PAD:UW], 0.0))
                v.wait_ge(c_in, 16 * (2 * NG * TILES + 1))
                ch.done(v.tensor_scalar(cw[:, :, :], cw[:, :, :], 0.5, None, ALU.mult))
                NW = UW - 2 * PAD

                def tap(g, c, t):
                    i = g * TILES + c
                    w = cw[:, i]
                    if t == 0:
                        v.wait_ge(u_done, n3 * (i + 1))
                        ch.done(v.tensor_scalar(acc_[:, :], u[:, c, 0:NW], w[:, 0:1], w[:, CONV:CONV + 1], ALU.mult, ALU.add))
                        return
                    e = v.scalar_tensor_tensor(out=acc_[:, :], in0=u[:, c, t:t + NW], scalar=w[:, t:t + 1], in1=acc_[:, :], op0=ALU.mult, op1=ALU.add)
                    if t < CONV - 1:
                        ch.done(e)
                    else:
                        e.then_inc(ca_done, 1)
                        v.wait_ge(ca_done, i + 1)

                def silu(g, c):
                    i = g * TILES + c
                    v.wait_ge(th_done, i + 1)
                    if g >= 1:
                        if c == TILES - 1:
                            v.wait_ge(s_mm, NSC * g)
                        else:
                            v.wait_ge(cb_mm, TT * g)
                    for a, b, o in OUTS:
                        e = v.scalar_tensor_tensor(out=cv[:, c, o:o + b - a], in0=u[:, c, PAD + a:PAD + b], scalar=1.0, in1=acc_[:, a:b], op0=ALU.add, op1=ALU.mult)
                    e.then_inc(conv_done, 1)
                    v.wait_ge(conv_done, i + 1)

                def gate(g, j):
                    i = g * TT + j
                    v.wait_ge(zt_done, i + 1)
                    v.scalar_tensor_tensor(out=zt[:, j], in0=zt[:, j], scalar=1.0, in1=acc[:, bank_of[("z", i)], 0:GW], op0=ALU.add, op1=ALU.mult).then_inc(z_done, 1)

                for c in range(TILES):
                    for j in range(2 * c, 2 * c + 2):
                        gate(0, j)
                    for t in range(CONV):
                        tap(0, c, t)
                    silu(0, c)
                for j in range(2 * TILES, TT):
                    gate(0, j)
                for g in range(NG):
                    for j in range(TT):
                        i = g * TT + j
                        tr = turn_bank(j)
                        v.wait_ge(tr_done, 2 * (i + 1))
                        v.tensor_tensor(cb[:, 0, j], tr[:, 3 * P:4 * P], C["le"], ALU.mult)
                        v.tensor_tensor(cb[:, 1, j], tr[:, 3 * P:4 * P], C["ge"], ALU.mult).then_inc(cb_done, 1)
                    v.wait_ge(cb_done, (g + 1) * TT)

                    def heads(x):
                        return x.rearrange("p (h d) -> p h d", h=NHG)

                    def per_head(x, j, d):
                        return x[:, j, d * NH + g * NHG:d * NH + (g + 1) * NHG].rearrange("p (h a) -> p h a", a=1).to_broadcast([P, NHG, HD])

                    def before(k):
                        d, j = SCAN[k]
                        i = g * NSC + k
                        if i >= 2:
                            v.wait_ge(y_mm, i - 1)
                            v.wait_ge(s_mm, i - 1)
                        v.tensor_tensor(heads(xd[:, i % 2]), heads(xt[:, j]), per_head(dt, j, d), ALU.mult)
                        v.tensor_tensor(heads(xe[:, i % 2]), heads(xt[:, j]), per_head(tend, j, d), ALU.mult).then_inc(xe_done, 1)
                        v.wait_ge(E_done, i + 1)
                        v.tensor_tensor(W[:, i % 2], E[:, i % 2], cb[:, d, j].rearrange("p (a s) -> p a s", a=1).to_broadcast([P, NHG, P]), ALU.mult).then_inc(W_done, 1)

                    def after(k):
                        d, j = SCAN[k]
                        i = g * NSC + k
                        v.wait_ge(s_mm, i + 1)
                        if k < 2:
                            v.tensor_copy(st[:, d], Sp[:, 0:GW]).then_inc(s_done, 1)
                        else:
                            v.wait_ge(y_mm, i + 1)
                            ch.done(v.tensor_tensor(heads(st[:, d]), heads(st[:, d]), per_head(edec, j, d), ALU.mult))
                            v.tensor_tensor(st[:, d], st[:, d], Sp[:, 0:GW], ALU.add).then_inc(s_done, 1)
                        v.wait_ge(s_done, i + 1)
                        v.wait_ge(y_mm, i + 1)
                        v.wait_ge(y_init, g * TT + sum(1 for s in FIRST if s[1] <= k))
                        if k >= 2:
                            ch.done(v.tensor_tensor(heads(tmp[:, :]), heads(Yp[:, i % 2, 1]), per_head(ecum, j, d), ALU.mult))
                            ch.done(v.tensor_tensor(yy[:, j], yy[:, j], tmp[:, :], ALU.add))
                        v.tensor_tensor(yy[:, j], yy[:, j], Yp[:, i % 2, 0], ALU.add).then_inc(y_done, 1)
                        v.wait_ge(y_done, i + 1)

                    for k in range(NSC + 1):
                        if k < NSC:
                            before(k)
                        if k >= 1:
                            after(k - 1)
                        if g + 1 < NG:
                            for c, t in CONV_AT.get(k, ()):
                                if t < CONV:
                                    tap(g + 1, c, t)
                                else:
                                    silu(g + 1, c)
                    for j in range(TT):
                        e = v.scalar_tensor_tensor(out=yy[:, j], in0=yy[:, j], scalar=0.5, in1=zt[:, j], op0=ALU.mult, op1=ALU.mult).then_inc(g_done, 1)
                    if g + 1 < NG:
                        for j in range(TT):
                            gate(g + 1, j)
                            if j < 3:
                                tap(g + 1, TILES - 1, 2 + j)
                        silu(g + 1, TILES - 1)


PIECES = 12


def pieces_at(k):
    return [p for p in range(PIECES) if p * len(SCAN) // PIECES == k]


FIRST = [(j, min(k for k, s in enumerate(SCAN) if s[1] == j)) for j in range(TT)]
CONV_AT = {}
for _c, _k in enumerate((4, 9, 14)):
    CONV_AT.update({_k: [(_c, 0), (_c, 1)], _k + 1: [(_c, 2), (_c, 3)], _k + 2: [(_c, 4)], _k + 4: [(_c, CONV)]})
CONV_AT[19] = [(3, 0), (3, 1)]
TANH_AT = [7, 12, 17]


def projection_banks():
    order = [("p", i) for i in range(PIECES)] + [("z", j) for j in range(TT)]
    for g in range(1, NG):
        order += [("p", g * PIECES + i) for i in range(PIECES)] + [("z", g * TT + j) for j in range(TT)]
    return {use: n % 2 for n, use in enumerate(order)}


bank_of = projection_banks()


def mamba_layer(nc, C, A, S, hT):
    with ExitStack() as c2:
        dt, ecum, tend, edec = (c2.enter_context(nc.sbuf_tensor("m_" + n, [P, TT, 2 * NH], F32))[:, :, :] for n in ("dt", "ecum", "tend", "edec"))
        la1, la2 = (c2.enter_context(nc.sbuf_tensor("m_" + n, [P, TT, 2 * NH], F32R))[:, :, :] for n in ("la1", "la2"))
        masks = c2.enter_context(nc.sbuf_tensor("m_masks", [P, 2, P], F32R))
        with nc.sbuf_tensor("m_la", [P, TT, 2 * NH], F32) as la:
            mamba_steps(nc, C, A, hT, dt, la[:, :, :], ecum, tend, edec, la1, la2, masks)
        mamba_groups(nc, C, A, S, hT, dt, ecum, tend, edec, la1, la2, masks)


def project_t(nc, name, hT, w, out):
    K, N = w.shape
    kt, nt, ns = K // P, N // P, LAT // HALF
    with Phase(nc, name) as f:
        wb = f.sb("w", [P, 2, kt, P])
        w1, w2_ = f.sb("w1", [P, 2, kt, P], F32R), f.sb("w2", [P, 2, kt, P], F32R)
        rounded, w_split = f.sem("rounded"), f.sem("w_split")
        st = f.sb("st", [P, 4, HALF])
        acc = f.ps("acc", [P, 4, HALF])
        w_in, mm_done, copied, stored = f.sem2("w_in"), f.sem("mm_done"), f.sem2("copied"), f.sem2("stored", 4)
        steps = [(c, s) for c in range(nt) for s in range(ns)]
        with nc.Block() as block:
            @block.sync
            def _(sp):
                for c in range(nt):
                    if c >= 2:
                        sp.wait_ge(mm_done, (c - 1) * ns)
                    sp.dma_start(wb[:, c % 2], w[:, c * P:(c + 1) * P].rearrange("(k p) n -> p k n", p=P)).then_inc(w_in[c % 2], 16)

            @block.tensor
            def _(pe):
                for i, (c, s) in enumerate(steps):
                    pe.wait_ge(w_split, c + 1)
                    if i >= 4:
                        pe.wait_ge(copied[i % 2], (i - 4) // 2 + 1)
                    w2 = w2_[:, c % 2]
                    terms = [(y[:, k], x[:, k, s * HALF:(s + 1) * HALF]) for x, y in ((hT[0], w1[:, c % 2]), (hT[0], w2), (hT[1], w1[:, c % 2])) for k in range(kt)]
                    for q, (y, x) in enumerate(terms):
                        mm = pe.matmul(acc[:, i % 4], y, x, start=(q == 0), stop=(q == len(terms) - 1))
                    mm.then_inc(mm_done, 1)

            def split(eng, par, c):
                if par == 0:
                    eng.wait_ge(w_in[c % 2], 16 * (c // 2 + 1))
                    if c >= 2:
                        eng.wait_ge(mm_done, (c - 1) * ns)
                    eng.copy(w1[:, c % 2], wb[:, c % 2]).then_inc(rounded, 1)
                else:
                    eng.wait_ge(rounded, c + 1)
                    eng.tensor_tensor(w2_[:, c % 2], wb[:, c % 2], w1[:, c % 2].bitcast(F32), ALU.subtract).then_inc(w_split, 1)

            def copy(eng, par):
                split(eng, par, 0)
                if nt > 1:
                    split(eng, par, 1)
                for i in range(par, len(steps), 2):
                    eng.wait_ge(mm_done, i + 1)
                    if i >= 4:
                        eng.wait_ge(stored[i % 4], 16 * (i // 4))
                    (eng.copy if par == 0 else eng.tensor_copy)(st[:, i % 4], acc[:, i % 4]).then_inc(copied[par], 1)
                    c = steps[i][0]
                    if c + 2 < nt:
                        split(eng, par, c + 2)

            @block.scalar
            def _(act):
                copy(act, 0)

            @block.vector
            def _(v):
                copy(v, 1)

            @block.gpsimd
            def _(g):
                for i, (c, s) in enumerate(steps):
                    g.wait_ge(copied[i % 2], i // 2 + 1)
                    g.dma_start(out[c * P:(c + 1) * P, s * HALF:(s + 1) * HALF], st[:, i % 4]).then_inc(stored[i % 4], 16)
                for s in range(4):
                    g.wait_ge(stored[s], 16 * len(range(s, len(steps), 4)))


def rope_tables(nc, C, A, cos, sin):
    ROUND = 1.5 * 2.0 ** 23
    TWO_PI = (6.28125, 0.00193500518798828125, 3.0199159819e-07)
    with Phase(nc, "rope") as f:
        pi = f.sb("pi", [P, LT], I32)
        pf = f.sb("pf", [P, LT])
        a, k, h = f.sb("a", [P, LT, 16]), f.sb("k", [P, LT, 16]), f.sb("h", [P, LT, 16])
        p_in, v_chain, s_done = f.sem("p_in"), f.sem("v_chain"), f.sem("s_done")
        with nc.Block() as block:
            @block.sync
            def _(sp):
                with nc.allow_non_contiguous_dma(reason="positions by token"):
                    sp.dma_start(pi[:, :], A["positions_2"][0].rearrange("(j p) -> p j", p=P)).then_inc(p_in, 16)

            @block.vector
            def _(v):
                ch = Chain(v, v_chain)
                v.wait_ge(p_in, 16)
                ch.done(v.tensor_copy(pf[:, :], pi[:, :]))
                ch.done(v.tensor_tensor(a[:, :, :], pf[:, :].rearrange("p (j o) -> p j o", o=1).to_broadcast([P, LT, 16]), C["inv2"].rearrange("p (o q) -> p o q", o=1).to_broadcast([P, LT, 16]), ALU.mult))
                ch.done(v.tensor_scalar(k[:, :, :], a[:, :, :], 1.0 / (2.0 * np.pi), None, ALU.mult))
                ch.done(v.tensor_scalar(k[:, :, :], k[:, :, :], ROUND, None, ALU.add))
                ch.done(v.tensor_scalar(k[:, :, :], k[:, :, :], -ROUND, None, ALU.add))
                for c in TWO_PI:
                    ch.done(v.scalar_tensor_tensor(out=a[:, :, :], in0=k[:, :, :], scalar=-c, in1=a[:, :, :], op0=ALU.mult, op1=ALU.add))
                ch.done(v.tensor_scalar(a[:, :, :], a[:, :, :], 3.1415925, -3.1415925, ALU.min, ALU.max))
                v.wait_ge(s_done, 2)
                ch.done(v.tensor_tensor(h[:, :, :], h[:, :, :], h[:, :, :], ALU.mult))
                ch.done(v.tensor_scalar(cos, h[:, :, :], -2.0, 1.0, ALU.mult, ALU.add))

            @block.scalar
            def _(act):
                act.wait_ge(v_chain, 9)
                act.activation(sin, a[:, :, :], ACT.Sin).then_inc(s_done, 1)
                act.activation(h[:, :, :], a[:, :, :], ACT.Sin, scale=0.5).then_inc(s_done, 1)


HH = 4
LEV = 7


def recurrence(nc, C, A, S, masks):
    combos = [(h, d) for h in range(HH) for d in range(2)]
    NC = len(combos)
    with Phase(nc, "hg") as f:
        lg, lb, ol, oh = f.sb("lg", [P, 2, 2, HH]), f.sb("lb", [P, 2, HH]), f.sb("ol", [P, 2, HH]), f.sb("oh", [P, 2, HH])
        qr, qs = f.sb("qr", [P, 2, LAT]), f.sb("qs", [P, 2, LAT])
        z, k_, b_ = f.sb("z", [P, 2, LAT]), f.sb("k", [P, 2, LAT]), f.sb("b", [P, 2, LAT])
        t1 = f.sb("t1", [P, LAT])
        rst = f.sb("rst", [P, 2, LAT])
        qb = f.sb("qb", [P, 2, LAT])
        X = f.sb("X", [P, 2, LEV + 1, LAT])
        kt = f.sb("kt", [P, LT, P])
        vv = f.sb("v", [P, LT, HH * P])
        M = f.sb("M", [P, 2, LEV + 1, P])
        st = f.sb("st", [P, P])
        eb = f.sb("eb", [P, 2, LT])
        o = f.sb("o", [P, 2, LT, P])
        Aps = f.ps("A", [P, 2, LEV + 1, P])
        Ops = f.ps("O", [P, 2, HALF])
        Sps = f.ps("S", [P, HALF])
        Tps = f.ps("T", [P, 4, P])
        c_in, q_in, z_in, z2_in = f.sem("c_in"), f.sem2("q_in"), f.sem2("z_in"), f.sem("z2_in")
        a_step, v_step, dl_done, x_exp, x_done, k_mm, k_ev = (f.sem(n) for n in ("a_step", "v_step", "dl_done", "x_exp", "x_done", "k_mm", "k_ev"))
        l_mm, m_done, o_mm, s_mm, s_done, o_done, stored, init = (f.sem(n) for n in ("l_mm", "m_done", "o_mm", "s_mm", "s_done", "o_done", "stored", "init"))
        b_done, g_done, lbe = f.sem("b_done"), f.sem("g_done"), f.sem("lbe")
        order = [list(range(LT)), list(range(LT - 1, -1, -1))]

        with nc.Block() as block:
            @block.sync
            def _(sp):
                with nc.allow_non_contiguous_dma(reason="logits by channel"):
                    for l in range(2):
                        for d in range(2):
                            sp.dma_start(lg[:, l, d], col_view(A["hg_lb_logits_2"][l, d], HH)).then_inc(c_in, 16)
                def store(h):
                    sp.wait_ge(o_done, 2 * LT * (h + 1))
                    if h:
                        sp.wait_ge(stored, 16 * h)
                    sp.dma_start(S["ho"][:, h * P:(h + 1) * P].rearrange("(j p) n -> p j n", p=P), o[:, h % 2]).then_inc(stored, 16)

                for c, (h, d) in enumerate(combos):
                    if d == 0:
                        if h >= 2:
                            sp.wait_ge(v_step, 3 * 2 * (h - 1))
                        sp.dma_start(qr[:, h % 2], S["hfT"][h * P:(h + 1) * P, :]).then_inc(q_in[h % 2], 16)
                    if c >= 2:
                        sp.wait_ge(a_step, 7 * (c - 2) + 6)
                    r = HH * P * (d + 1) + h * P
                    sp.dma_start(z[:, c % 2], S["hfT"][r:r + P, :]).then_inc(z_in[c % 2], 16)
                    if c == 0:
                        sp.dma_start(vv[:, :, :], S["hih"][:, 0:HH * P].rearrange("(j p) n -> p j n", p=P)).then_inc(z2_in, 16)
                    if c >= 3 and d == 1:
                        store((c - 3) // 2)
                store(HH - 1)
                sp.wait_ge(stored, 16 * HH)

            @block.scalar
            def _(act):
                ch = Chain(act, a_step)
                act.wait_ge(init, 1)
                act.activation(lb[:, :, :], lb[:, :, :], ACT.Exp, scale=-1.0).then_inc(lbe, 1)
                act.activation(ol[:, :, :], ol[:, :, :], ACT.Exp).then_inc(lbe, 1)
                act.wait_ge(init, 10)

                def prep_decay(c):
                    act.wait_ge(z_in[c % 2], 16 * (c // 2 + 1))
                    if c >= 1:
                        act.wait_ge(b_done, c)
                    ch.done(act.activation(t1[:, :], z[:, c % 2], ACT.Exp, scale=-1.0))
                    ch.done(act.activation(t1[:, :], t1[:, :], ACT.Identity, bias=C["ones"][:, 0:1]))

                def log_decay(c):
                    h, d = combos[c]
                    act.wait_ge(v_step, 3 * c + 1)
                    ch.done(act.activation(t1[:, :], t1[:, :], ACT.Ln, scale=ol[:, d, h:h + 1], bias=lb[:, d, h:h + 1]))

                def prep_qk(c):
                    h, d = combos[c]
                    act.wait_ge(q_in[h % 2], 16 * (h // 2 + 1))
                    if c >= 2:
                        act.wait_ge(o_mm, LT * (c - 1))
                        act.wait_ge(x_done, (LEV + 1) * (c - 1))
                    ch.done(act.activation(qb[:, c % 2], qr[:, h % 2], ACT.Tanh, scale=0.5))
                    ch.done(act.activation(qb[:, c % 2], qb[:, c % 2], ACT.Identity, scale=oh[:, d, h:h + 1], bias=oh[:, d, h:h + 1]))
                    ch.done(act.activation(k_[:, c % 2], z[:, c % 2], ACT.Exp))
                    ch.done(act.activation(k_[:, c % 2], k_[:, c % 2], ACT.Identity, bias=C["ones"][:, 0:1]))

                def exps(c):
                    act.wait_ge(b_done, c + 1)
                    act.wait_ge(v_step, 3 * c + 3)
                    act.activation(qb[:, c % 2], b_[:, c % 2], ACT.Exp).then_inc(g_done, 1)
                    d = combos[c][1]
                    e = (P - 1) if d == 0 else 0
                    act.activation(eb[:, c % 2], b_[:, c % 2].rearrange("p (j t) -> p j t", t=P)[:, :, e], ACT.Exp).then_inc(g_done, 1)
                    for l in range(LEV + 1):
                        act.wait_ge(dl_done, (LEV + 1) * c + l + 1)
                        act.activation(X[:, c % 2, l], X[:, c % 2, l], ACT.Exp).then_inc(x_exp, 1)

                def turned(c):
                    for g in range(2):
                        i = 2 * c + g
                        act.wait_ge(k_mm, i + 1)
                        if c >= 1:
                            act.wait_ge(s_mm, LT * c)
                        act.copy(kt[:, 4 * g:4 * g + 4], Tps[:, :, :]).then_inc(k_ev, 1)

                prep_decay(0)
                log_decay(0)
                prep_qk(0)
                exps(0)
                for c in range(NC):
                    if c + 1 < NC:
                        prep_decay(c + 1)
                    turned(c)
                    if c + 1 < NC:
                        log_decay(c + 1)
                        prep_qk(c + 1)
                        exps(c + 1)

            @block.gpsimd
            def _(g):
                for c in range(NC):
                    h, d = combos[c]
                    g.wait_ge(b_done, c + 1)
                    if c >= 2:
                        g.wait_ge(l_mm, LT * (c - 1))
                        g.wait_ge(k_mm, 2 * (c - 1))
                    for l in range(LEV):
                        m = 1 << l
                        bv = b_[:, c % 2].rearrange("p (n t) -> p n t", t=2 * m)
                        xv = X[:, c % 2, l].rearrange("p (n t) -> p n t", t=2 * m)
                        r = m - 1 if d == 0 else m
                        ref = bv[:, :, r:r + 1].to_broadcast([P, LAT // (2 * m), m])
                        lo, hi = (ref, bv[:, :, 0:m]), (bv[:, :, m:2 * m], ref)
                        if d == 1:
                            lo, hi = lo[::-1], hi[::-1]
                        g.tensor_tensor(xv[:, :, 0:m], lo[0], lo[1], ALU.subtract)
                        g.tensor_tensor(xv[:, :, m:2 * m], hi[0], hi[1], ALU.subtract).then_inc(dl_done, 1)
                    bv = b_[:, c % 2].rearrange("p (n t) -> p n t", t=P)
                    e = P - 1 if d == 0 else 0
                    g.tensor_tensor(X[:, c % 2, LEV].rearrange("p (n t) -> p n t", t=P), bv[:, :, e:e + 1].to_broadcast([P, LT, P]), bv, ALU.subtract).then_inc(dl_done, 1)
                    g.wait_ge(g_done, 2 * (c + 1))
                    g.wait_ge(v_step, 3 * c + 3)
                    g.tensor_tensor(qb[:, c % 2], qb[:, c % 2], qs[:, c % 2], ALU.mult)
                    g.wait_ge(x_exp, (LEV + 1) * (c + 1))
                    g.tensor_tensor(X[:, c % 2, LEV], X[:, c % 2, LEV], k_[:, c % 2], ALU.mult).then_inc(x_done, 1)

            @block.vector
            def _(v):
                ch = Chain(v, v_step)
                v.wait_ge(c_in, 64)
                v.tensor_tensor(lb[:, :, :], lg[:, 0], lg[:, 1], ALU.subtract)
                v.tensor_tensor(ol[:, :, :], lg[:, 0], lg[:, 1], ALU.subtract).then_inc(init, 1)
                v.wait_ge(lbe, 2)
                for x in (lb, ol):
                    v.tensor_scalar(x[:, :, :], x[:, :, :], 1.0, None, ALU.add).then_inc(init, 1)
                v.wait_ge(init, 3)
                for x in (lb, ol):
                    v.reciprocal(x[:, :, :], x[:, :, :]).then_inc(init, 1)
                v.wait_ge(init, 5)
                v.tensor_scalar(oh[:, :, :], ol[:, :, :], 0.5, None, ALU.mult).then_inc(init, 1)
                for d in range(2):
                    v.memset(rst[:, d], 1.0).then_inc(init, 1)
                v.wait_ge(init, 8)
                v.memset(rst[:, 0].rearrange("p (j t) -> p j t", t=P)[:, :, 0:1], 0.0).then_inc(init, 1)
                v.memset(rst[:, 1].rearrange("p (j t) -> p j t", t=P)[:, :, P - 1:P], 0.0).then_inc(init, 1)
                v.wait_ge(init, 10)

                def quarter(x, part):
                    x = x[:, part * LAT // 4:(part + 1) * LAT // 4]
                    e = v.reciprocal(x, x)
                    if part == 3:
                        ch.done(e)

                def decay(c, part):
                    v.wait_ge(a_step, 7 * c + 2)
                    quarter(t1, part)

                def sums(c):
                    h, d = combos[c]
                    v.wait_ge(a_step, 7 * c + 3)
                    if c >= 2:
                        v.wait_ge(dl_done, (LEV + 1) * (c - 1))
                        v.wait_ge(g_done, 2 * (c - 1))
                    s = slice(None) if d == 0 else slice(None, None, -1)
                    v.tensor_tensor_scan(b_[:, c % 2][:, s], rst[:, d][:, s], t1[:, s], 0.0, ALU.mult, ALU.add).then_inc(b_done, 1)

                def keys(c, part):
                    v.wait_ge(a_step, 7 * c + 7)
                    quarter(k_[:, c % 2], part)

                def queries(c):
                    h, d = combos[c]
                    if c >= 2:
                        v.wait_ge(l_mm, LT * (c - 1))
                        v.wait_ge(x_done, (LEV + 1) * (c - 1))
                    ch.done(v.tensor_tensor(qs[:, c % 2], qb[:, c % 2], qr[:, h % 2], ALU.mult))

                def weigh(c, l):
                    h, d = combos[c]
                    v.wait_ge(x_exp, (LEV + 1) * c + l + 1)
                    m = 1 << l
                    xv, kv, qv = (a.rearrange("p (n t) -> p n t", t=2 * m) for a in (X[:, c % 2, l], k_[:, c % 2], qs[:, c % 2]))
                    lo, hi = (kv, qv) if d == 0 else (qv, kv)
                    v.tensor_tensor(xv[:, :, 0:m], xv[:, :, 0:m], lo[:, :, 0:m], ALU.mult)
                    v.tensor_tensor(xv[:, :, m:2 * m], xv[:, :, m:2 * m], hi[:, :, m:2 * m], ALU.mult).then_inc(x_done, 1)

                WITH = [[(decay, 0), (decay, 1)], [(decay, 2), (decay, 3)], [(sums,), (keys, 0)], [(keys, 1), (keys, 2)], [(keys, 3), (queries,)],
                        [(weigh, 0), (weigh, 1)], [(weigh, 2), (weigh, 3)], [(weigh, 4), (weigh, 5)], [(weigh, 6)]]

                def ahead(c, what):
                    what[0](c, *what[1:])

                def chunks(c):
                    h, d = combos[c]
                    for n in range(LT + 1):
                        if n < LT:
                            i = c * LT + n
                            v.wait_ge(l_mm, i + 1)
                            if i >= 2:
                                v.wait_ge(o_mm, i - 1)
                            for half in range(2):
                                sl = slice(4 * half, 4 * half + 4)
                                e = v.tensor_tensor(M[:, i % 2, sl], Aps[:, i % 2, sl], masks[d].rearrange("p (l t) -> p l t", t=P)[:, sl], ALU.mult)
                            e.then_inc(m_done, 1)
                        if n >= 1:
                            i = c * LT + n - 1
                            j = order[d][n - 1]
                            v.wait_ge(s_mm, i + 1)
                            v.wait_ge(o_mm, i + 1)
                            if n == 1:
                                v.tensor_copy(st[:, :], Sps[:, 0:P]).then_inc(s_done, 1)
                            else:
                                v.scalar_tensor_tensor(out=st[:, :], in0=st[:, :], scalar=eb[:, c % 2, j:j + 1], in1=Sps[:, 0:P], op0=ALU.mult, op1=ALU.add).then_inc(s_done, 1)
                            v.wait_ge(s_done, i + 1)
                            if d == 0:
                                if h >= 2:
                                    v.wait_ge(stored, 16 * (h - 1))
                                v.tensor_copy(o[:, h % 2, j], Ops[:, i % 2, 0:P]).then_inc(o_done, 1)
                            else:
                                v.wait_ge(o_done, c * LT)
                                v.tensor_tensor(o[:, h % 2, j], o[:, h % 2, j], Ops[:, i % 2, 0:P], ALU.add).then_inc(o_done, 1)
                        if c + 1 < NC:
                            for what in WITH[n]:
                                ahead(c + 1, what)

                for step in WITH:
                    for what in step:
                        ahead(0, what)
                for c in range(NC):
                    chunks(c)

            @block.tensor
            def _(pe):
                pe.wait_ge(z2_in, 16)
                for c in range(NC):
                    h, d = combos[c]
                    pe.wait_ge(x_done, (LEV + 1) * (c + 1))
                    for g in range(2):
                        if 2 * c + g >= 1:
                            pe.wait_ge(k_ev, 2 * c + g)
                        for u in range(4):
                            j = 4 * g + u
                            mm = pe.transpose(Tps[:, u], X[:, c % 2, LEV, j * P:(j + 1) * P], C["ident"])
                        mm.then_inc(k_mm, 1)
                    for n in range(LT + 1):
                        if n < LT:
                            i, j = c * LT + n, order[d][n]
                            t = slice(j * P, (j + 1) * P)
                            if i >= 2:
                                pe.wait_ge(m_done, i - 1)
                            pe.matmul(Aps[:, i % 2, 0], k_[:, c % 2, t], qs[:, c % 2, t], start=True, stop=True)
                            for l in range(LEV):
                                mm = pe.matmul(Aps[:, i % 2, l + 1], X[:, c % 2, l, t], X[:, c % 2, l, t], start=True, stop=True)
                            mm.then_inc(l_mm, 1)
                        if n >= 1:
                            i, j = c * LT + n - 1, order[d][n - 1]
                            t = slice(j * P, (j + 1) * P)
                            pe.wait_ge(m_done, i + 1)
                            if i >= 2:
                                pe.wait_ge(o_done, i - 1)
                            vj = vv[:, j, h * P:(h + 1) * P]
                            for l in range(LEV + 1):
                                mm = pe.matmul(Ops[:, i % 2, 0:P], M[:, i % 2, l], vj, start=(l == 0), stop=(l == LEV and n == 1))
                            if n >= 2:
                                pe.wait_ge(s_done, i)
                                mm = pe.matmul(Ops[:, i % 2, 0:P], qb[:, c % 2, t], st[:, :], start=False, stop=True)
                            mm.then_inc(o_mm, 1)
                            pe.wait_ge(k_ev, 2 * (c + 1))
                            if i >= 1:
                                pe.wait_ge(s_done, i)
                            pe.matmul(Sps[:, 0:P], kt[:, j], vj, start=True, stop=True).then_inc(s_mm, 1)


def mixer_layer(nc, C, A, S):
    w = A["w_in_2"][0]
    QR, KR, RD, MH, QK = 192, 128, 32, 8, 96
    with ExitStack() as c1:
        h1, h2 = (c1.enter_context(nc.sbuf_tensor(x, [P, KD, LAT], F32R)) for x in ("h2T1", "h2T2"))
        with nc.sbuf_tensor("h2T", [P, KD, LAT], F32) as whole:
            norm_turn(nc, "n2", C, [(S["h2"][i * P:(i + 1) * P, :], 0, i * P) for i in range(LT)], [(A["norm_mix_2"][0], None, None)], whole,
                      first=(A["final_norm_w"], S["x1"]))
            split_rows(nc, "h_sp", whole, h1, h2)
        hT = (h1, h2)
        cols = [i * P for i in range(LT)]
        project(nc, "w_a", hT, cols, w[:, 0:352], S["pa"])
        project_t(nc, "w_f", hT, w[:, 352:1888], S["hfT"])
        project(nc, "w_i", hT, cols, w[:, 1888:2912], S["hih"])
    with ExitStack() as c1:
        mask = c1.enter_context(nc.sbuf_tensor("levels", [P, 2, (LEV + 1) * P], F32))
        move(nc, "lv", [(mask[:, :, :], A["levels"].rearrange("p (d n) -> p d n", d=2))])
        recurrence(nc, C, A, S, [mask[:, 0], mask[:, 1]])
    with ExitStack() as c1:
        hoT = c1.enter_context(nc.sbuf_tensor("hoT", [P, HH, LAT], F32))
        turn_heads(nc, "h_o", C, LT, HH, P, lambda i: [(0, HH, 0, P, S["ho"][i * P:(i + 1) * P, :].rearrange("p (h d) -> p h d", h=HH))],
                   A["hg_o_norm_2"][0], [(b * P, P, [((0, P), (lambda b: lambda i: hoT[:, b, i * P:(i + 1) * P])(b))]) for b in range(HH)],
                   gate=lambda i: S["hih"][i * P:(i + 1) * P, HH * P:2 * HH * P].rearrange("p (h d) -> p h d", h=HH))
        move(nc, "h_s", [(S["mixT"][HH * P:2 * HH * P, :].rearrange("(k p) t -> p k t", p=P), hoT[:, :, :])])
    with ExitStack() as c1:
        sb = lambda name, shape: c1.enter_context(nc.sbuf_tensor(name, shape, F32))
        cos, sin = sb("cos", [P, LT, 16]), sb("sin", [P, LT, 16])
        rope_tables(nc, C, A, cos[:, :, :], sin[:, :, :])
        qT, kT, vv = sb("mqT", [P, MH, LAT]), sb("mkT", [P, MH, LAT]), sb("mv", [P, LT, MH * 64])
        rot = sb("rot", [P, LT, RD])
        with ExitStack() as c2:
            cq, ckv = (c2.enter_context(nc.sbuf_tensor(x, [P, k, LAT], F32)) for x, k in (("cq", 2), ("ckv", 1)))
            move(nc, "m_r", [(rot[:, :, :], S["pa"][:, QR + KR:QR + KR + RD].rearrange("(j p) c -> p j c", p=P))], [qT[:, :, :], kT[:, :, :]])
            turn_heads(nc, "cq", C, LT, 1, QR, lambda i: [(0, 1, 0, QR, S["pa"][i * P:(i + 1) * P, 0:QR].rearrange("p (a d) -> p a d", a=1))], A["mla_q_a_norm_2"][0],
                       [(0, P, [((0, P), lambda i: cq[:, 0, i * P:(i + 1) * P])]), (P, 64, [((0, 64), lambda i: cq[0:64, 1, i * P:(i + 1) * P])])])
            turn_heads(nc, "ckv", C, LT, 1, KR, lambda i: [(0, 1, 0, KR, S["pa"][i * P:(i + 1) * P, QR:QR + KR].rearrange("p (a d) -> p a d", a=1))], A["mla_kv_a_norm_2"][0],
                       [(0, P, [((0, P), lambda i: ckv[:, 0, i * P:(i + 1) * P])])])
            tab = lambda j: (cos[:, j], sin[:, j])
            put = lambda t: lambda c, j, g: t[0:QK, 4 * c:4 * c + 4, j * P:(j + 1) * P]
            project_heads(nc, "m_q", C, cq, cols, A["mla_w_q_up_2"][0], QK, 4 * QK, A["mla_q_norm_2"][0], put(qT), rope=(64, 1, tab))
            project_heads(nc, "m_k", C, ckv, cols, A["mla_w_kv_up_2"][0], QK, 4 * P, A["mla_k_norm_2"][0], put(kT), rope=(64, 1, tab),
                          extra=rot[:, :, :], values=lambda c, j: vv[:, j, 4 * c * 64:4 * (c + 1) * 64].rearrange("p (h d) -> p h d", h=4))
        attend(nc, "m_at", C, [([(qT[:, h], kT[:, h])], [((lambda h: lambda k: vv[:, k, h * 64:(h + 1) * 64])(h), 64)], [S["mixT"][h * 64:(h + 1) * 64, :]]) for h in range(MH)],
               LT, LAT, QK ** -0.5)
    out_project_t(nc, "w_out", C, S["mixT"], A["w_out_2"][0], LT, S["x1"], S["x2"])


def cross_layer(nc, C, A, S):
    M, XH, XD = 256, 4, 256
    MT = M // P
    with ExitStack() as c1:
        sb = lambda name, shape: c1.enter_context(nc.sbuf_tensor(name, shape, F32))
        qT, kT, vv = sb("xqT", [P, 2 * XH, LAT]), sb("xkT", [P, 2 * XH, M]), sb("xv", [P, MT, D])
        with ExitStack() as c2:
            hT = c2.enter_context(nc.sbuf_tensor("h3T", [P, KD, LAT], F32))
            mT = c2.enter_context(nc.sbuf_tensor("memT", [P, KD, M], F32))
            norm_turn(nc, "n3", C, [(S["x2"][i * P:(i + 1) * P, :], 0, i * P) for i in range(LT)], [(A["norm_cross_2"][0], None, None)], hT)
            norm_turn(nc, "n4", C, [(A["mem_2"][0, i * P:(i + 1) * P, :], 0, i * P) for i in range(MT)], [(A["norm_mem_2"][0], None, None)], mT)
            by_tile = lambda t: lambda c, j, g: t[:, 4 * c:4 * c + 4, j * P:(j + 1) * P]
            project_heads(nc, "x_q", C, hT, [i * P for i in range(LT)], A["x_w_q_2"][0], XD, 2 * XD, A["x_q_norm_2"][0], by_tile(qT))
            project_heads(nc, "x_k", C, mT, [i * P for i in range(MT)], A["x_w_kv_2"][0][:, 0:D], XD, 2 * XD, A["x_k_norm_2"][0], by_tile(kT))
            project(nc, "x_v", mT, [i * P for i in range(MT)], A["x_w_kv_2"][0][:, D:2 * D], put=lambda j, a, b: vv[:, j, a:b])
        attend(nc, "x_at", C, [([(qT[:, 2 * h + u], kT[:, 2 * h + u]) for u in range(2)],
                                [((lambda h, u: lambda k: vv[:, k, h * XD + u * P:h * XD + (u + 1) * P])(h, u), P) for u in range(2)],
                                [S["xoT"][h * XD + u * P:h * XD + (u + 1) * P, :] for u in range(2)]) for h in range(XH)],
               LT, M, XD ** -0.5)
    out_project_t(nc, "x_out", C, S["xoT"], A["x_w_o_2"][0], LT, S["x2"], S["x3"])


EG, EE = 8, 8
NE = EG * EE
HID = 256
NBLK = 2 * LAT // P + NE
NONE = 5000


def route(nc, C, A, S, hT, wts):
    with Phase(nc, "route") as f:
        w = f.sb("w", [P, KD, EG + NE])
        bias = f.sb("bias", [P, EG + NE])
        lg = f.sb("lg", [P, LT, EG + NE])
        gm, gs, gd = f.sb("gm", [P, LT]), f.sb("gs", [P, LT]), f.sb("gd", [P, LT])
        g8, oh, e8, e8b = (f.sb(n, [P, LT, 8]) for n in ("g8", "oh", "e8", "e8b"))
        pr = f.sb("pr", [P, LT, EE, EG])
        m1, m2, i1, i2, ex = (f.sb(n, [P, LT]) for n in ("m1", "m2", "i1", "i2", "ex"))
        A1, A2, AA, AC, sl = (f.sb(n, [P, LT, NE]) for n in ("A1", "A2", "AA", "AC", "sl"))
        cnt, nb, pend, ps_, one = (f.sb(n, [P, NE]) for n in ("cnt", "nb", "pend", "pst", "one"))
        be, wi, wii = f.sb("be", [P, 1]), f.sb("wi", [P, P]), f.sb("wii", [P, P], U32)
        dst = f.sb("dst", [P, 2, LT])
        dsti = f.sb("dsti", [P, 2, LT], U32)
        info = f.sb("info", [P, LT, 2, 2], U32)
        none = f.sb("none", [P, NBLK * 2], U32)
        raw = f.ps("raw", [P, 2, 4, P])
        rank = f.ps("rank", [P, LT, NE])
        tot = f.ps("tot", [P, HALF])
        c_in, r_done, v_chain, a_chain, p_chain, cnt_done, init, done = (f.sem(n) for n in ("c_in", "r_done", "v_chain", "a_chain", "p_chain", "cnt_done", "init", "done"))
        iota8 = C["iota"][:, 0:8].rearrange("p (o e) -> p o e", o=1).to_broadcast([P, LT, 8])
        col = lambda x, n: x[:, :].rearrange("p (j o) -> p j o", o=1).to_broadcast([P, LT, n])
        N_ASSIGN, N_ALL = [0], [0]
        with nc.Block() as block:
            @block.vector
            def _(v):
                ch = Chain(v, v_chain)
                v.wait_ge(c_in, 64)
                v.wait_ge(r_done, 1)
                for b in range(2):
                    ch.done(v.tensor_tensor(lg[:, 4 * b:4 * b + 4], raw[:, b, :, 0:EG + NE], bias[:, :].rearrange("p (o n) -> p o n", o=1).to_broadcast([P, 4, EG + NE]), ALU.add))
                g = lg[:, :, 0:EG]

                def first_max(x, m, idx, eq):
                    ch.done(v.tensor_reduce(m[:, :], x, AX.X, ALU.max))
                    ch.done(v.tensor_tensor(eq, x, col(m, 8), ALU.is_equal))
                    ch.done(v.scalar_tensor_tensor(out=eq, in0=eq, scalar=-64.0, in1=iota8, op0=ALU.mult, op1=ALU.add))
                    ch.done(v.tensor_reduce(idx[:, :], eq, AX.X, ALU.min))
                    ch.done(v.tensor_scalar(idx[:, :], idx[:, :], 64.0, None, ALU.add))

                first_max(g, gm, gs, g8[:, :, :])
                ch.done(v.tensor_tensor(g8[:, :, :], g, col(gm, 8), ALU.subtract))
                at_g = ch.n
                ch.done(v.tensor_tensor(oh[:, :, :], iota8, col(gs, 8), ALU.is_equal))
                for j in range(LT):
                    e = v.tensor_tensor(pr[:, j], lg[:, j, EG:].rearrange("p (g e) -> p e g", g=EG), oh[:, j].rearrange("p (o g) -> p o g", o=1).to_broadcast([P, EE, EG]), ALU.mult)
                ch.done(e)
                ch.done(v.tensor_reduce(e8[:, :, :], pr[:, :, :, :], AX.X, ALU.add))
                first_max(e8[:, :, :], m1, i1, e8b[:, :, :])
                ch.done(v.tensor_tensor(e8b[:, :, :], iota8, col(i1, 8), ALU.is_equal))
                ch.done(v.scalar_tensor_tensor(out=e8[:, :, :], in0=e8b[:, :, :], scalar=-1e30, in1=e8[:, :, :], op0=ALU.mult, op1=ALU.add))
                first_max(e8[:, :, :], m2, i2, e8b[:, :, :])
                ch.done(v.tensor_tensor(ex[:, :], m2[:, :], m1[:, :], ALU.subtract))
                at_e = ch.n
                v.wait_ge(a_chain, 2)
                ch.done(v.tensor_reduce(gd[:, :], g8[:, :, :], AX.X, ALU.add))
                ch.done(v.tensor_scalar(m1[:, :], ex[:, :], 1.0, None, ALU.add))
                ch.done(v.tensor_tensor(m1[:, :], m1[:, :], gd[:, :], ALU.mult))
                ch.done(v.reciprocal(wts[:, :, 0], m1[:, :]))
                ch.done(v.tensor_tensor(wts[:, :, 1], wts[:, :, 0], ex[:, :], ALU.mult))
                ch.done(v.scalar_tensor_tensor(out=i1[:, :], in0=gs[:, :], scalar=float(EE), in1=i1[:, :], op0=ALU.mult, op1=ALU.add))
                ch.done(v.scalar_tensor_tensor(out=i2[:, :], in0=gs[:, :], scalar=float(EE), in1=i2[:, :], op0=ALU.mult, op1=ALU.add))
                i64 = C["iota"][:, 0:NE].rearrange("p (o e) -> p o e", o=1).to_broadcast([P, LT, NE])
                ch.done(v.tensor_tensor(A1[:, :, :], i64, col(i1, NE), ALU.is_equal))
                ch.done(v.tensor_tensor(A2[:, :, :], i64, col(i2, NE), ALU.is_equal))
                ch.done(v.tensor_tensor(AA[:, :, :], A1[:, :, :], A2[:, :, :], ALU.add))
                ch.done(v.memset(AC[:, 0], 0.0))
                for j in range(1, LT):
                    ch.done(v.tensor_tensor(AC[:, j], AC[:, j - 1], AA[:, j - 1], ALU.add))
                ch.done(v.tensor_tensor(sl[:, 0], AC[:, LT - 1], AA[:, LT - 1], ALU.add))
                at_c = ch.n
                v.wait_ge(cnt_done, 1)
                ch.done(v.tensor_copy(cnt[:, :], tot[:, 0:NE]))
                ch.done(v.tensor_scalar(nb[:, :], cnt[:, :], 0.0, None, ALU.is_gt))
                for j in range(1, LAT // P):
                    ch.done(v.scalar_tensor_tensor(out=nb[:, :], in0=cnt[:, :], scalar=float(P * j), in1=nb[:, :], op0=ALU.is_gt, op1=ALU.add))
                ch.done(v.memset(one[:, :], 1.0))
                ch.done(v.tensor_tensor_scan(pend[:, :], one[:, :], nb[:, :], 0.0, ALU.mult, ALU.add))
                ch.done(v.tensor_tensor(ps_[:, :], pend[:, :], nb[:, :], ALU.subtract))
                ch.done(v.tensor_scalar(ps_[:, :], ps_[:, :], float(P), None, ALU.mult))
                ch.done(v.tensor_tensor(sl[:, :, :], rank[:, :, :], ps_[:, :].rearrange("p (o e) -> p o e", o=1).to_broadcast([P, LT, NE]), ALU.add))
                for k, a in enumerate((A1, A2)):
                    ch.done(v.tensor_tensor(a[:, :, :], a[:, :, :], sl[:, :, :], ALU.mult))
                    ch.done(v.tensor_reduce(dst[:, k], a[:, :, :], AX.X, ALU.add))
                ch.done(v.tensor_copy(dsti[:, :, :], dst[:, :, :]))
                ch.done(v.tensor_scalar(one[:, :], pend[:, :], C["pidx"], None, ALU.is_le))
                ch.done(v.tensor_reduce(be[:, :], one[:, :], AX.X, ALU.add))
                ch.done(v.tensor_scalar(be[:, :], be[:, :], float(P), None, ALU.mult))
                ch.done(v.tensor_scalar(wi[:, :], C["iota"], be[:, 0:1], None, ALU.add))
                ch.done(v.tensor_copy(wii[:, :], wi[:, :]))
                N_ALL[0] = ch.n
                N_ASSIGN[0] = (at_g, at_e, at_c)

            at_g, at_e, at_c = N_ASSIGN[0]

            @block.scalar
            def _(act):
                ch = Chain(act, a_chain)
                act.wait_ge(v_chain, at_g)
                ch.done(act.activation(g8[:, :, :], g8[:, :, :], ACT.Exp))
                act.wait_ge(v_chain, at_e)
                ch.done(act.activation(ex[:, :], ex[:, :], ACT.Exp))

            @block.tensor
            def _(pe):
                pe.wait_ge(c_in, 64)
                for j in range(LT):
                    for k in range(KD):
                        mm = pe.matmul(raw[:, j // 4, j % 4, 0:EG + NE], hT[:, k, j * P:(j + 1) * P], w[:, k], start=(k == 0), stop=(k == KD - 1))
                mm.then_inc(r_done, 1)
                pe.wait_ge(v_chain, at_c)
                pe.matmul(rank[:, :, :], C["lt"], AA[:, :, :], start=True, stop=False)
                pe.matmul(rank[:, :, :], C["ones"], AC[:, :, :], start=False, stop=True)
                pe.matmul(tot[:, 0:NE], C["ones"], sl[:, 0], start=True, stop=True).then_inc(cnt_done, 1)

            @block.gpsimd
            def _(g):
                ch = Chain(g, p_chain)
                ch.done(g.memset(none[:, :], NONE))
                for j in range(LT):
                    for k in range(2):
                        g.iota(info[:, j, k, 0:1], [[0, 1]], base=j * P, channel_multiplier=1)
                        e = g.iota(info[:, j, k, 1:2], [[0, 1]], base=2 * j * P + k, channel_multiplier=2)
                ch.done(e)
                g.dma_start(S["idx"].rearrange("(p n) c -> p (n c)", p=P), none[:, :]).then_inc(init, 16)
                g.wait_ge(init, 16)
                g.wait_ge(v_chain, N_ALL[0])
                for j in range(LT):
                    for k in range(2):
                        g.indirect_dma_start(out=S["idx"], out_offset=bass.IndirectOffsetOnAxis(ap=dsti[:, k, j:j + 1], axis=0),
                                             in_=info[:, j, k, :], in_offset=None, bounds_check=NBLK * P - 1, oob_is_err=False).then_inc(done, 16)
                g.dma_start(S["wi"].rearrange("(b p) o -> b (p o)", p=P), wii[0:NBLK, :]).then_inc(done, 16)
                g.wait_ge(done, 16 * (2 * LT + 1))

            @block.sync
            def _(sp):
                sp.dma_start(w[:, :, 0:EG], A["moe_w_group_2"][0].rearrange("(k p) n -> p k n", p=P)).then_inc(c_in, 16)
                sp.dma_start(w[:, :, EG:], A["moe_w_expert_2"][0].rearrange("(k p) n -> p k n", p=P)).then_inc(c_in, 16)
                sp.dma_start(bias[:, 0:EG], row_bcast(A["moe_b_group_2"][0])).then_inc(c_in, 16)
                sp.dma_start(bias[:, EG:], row_bcast(A["moe_b_expert_2"][0])).then_inc(c_in, 16)


def experts(nc, C, A, S):
    TURNS = NBLK // 2
    HT = HID // P
    with Phase(nc, "moe") as f:
        nw = f.sb("nw", [P, KD])
        wg, wu, wd = f.sb("wg", [P, 2, KD, HID]), f.sb("wu", [P, 2, KD, HID]), f.sb("wd", [P, 2, HT, D])
        idx = [f.sb(f"idx{u}", [P, 2], U32) for u in range(2)]
        wi = [f.sb(f"wi{u}", [P, 1], U32) for u in range(2)]
        sidx = [f.sb(f"sidx{u}", [P, 1], U32) for u in range(2)]
        xg = [f.sb(f"xg{u}", [P, D]) for u in range(2)]
        xT = f.sb("xT", [P, 2, KD, P])
        th, sg = f.sb("th", [P, 2, HT * P]), f.sb("sg", [P, 2, HT * P])
        hh = f.sb("h", [P, 2, HT, P])
        y = [f.sb(f"y{u}", [P, D]) for u in range(2)]
        pt = f.ps("pt", [P, 2, 4, P])
        gu = f.ps("gu", [P, 2, 2, HT * P])
        acc = f.ps("acc", [P, 2, 2, HALF])
        c_in, w_in, idx_in, sidx_done, got = f.sem("c_in"), f.sem2("w_in"), f.sem2("idx_in"), f.sem("sidx_done"), f.sem2("got")
        turned, ev_a, ev_v, gu_mm, th_done, sg_done, h_done, d_mm, y_a, y_v, zero = (f.sem(n) for n in ("turned", "ev_a", "ev_v", "gu_mm", "th_done", "sg_done", "h_done", "d_mm", "y_a", "y_v", "zero"))
        put, passed, wi_in = f.sem2("put"), f.sem("passed"), f.sem2("wi_in")
        by_rows = lambda t: t[0].rearrange("e (p k) n -> (e p) (k n)", p=P)
        flat = lambda t: t.rearrange("p k n -> p (k n)")

        def turns(eng, body):
            body(0, True, False)
            with eng.Fori(1, TURNS - 1) as i:
                body(i, False, False)
            body(TURNS - 1, False, True)

        with nc.Block() as block:
            @block.sync
            def _(sp):
                sp.dma_start(nw[:, :], A["norm_ffn_2"][0].rearrange("(p k) -> p k", p=P)).then_inc(c_in, 16)

                def body(i, first, last):
                    for u in range(2):
                        b = 2 * i + u
                        if not first:
                            sp.wait_ge(got[u], 16 * i)
                            sp.sem_inc(passed, 1)
                            sp.wait_ge(sidx_done, b - 1)
                            sp.sem_inc(passed, 1)
                        sp.dma_start(idx[u][:, :], S["idx"][bass.ds(b * P, P), :]).then_inc(idx_in[u], 16)
                        if not first:
                            sp.wait_ge(w_in[u], 48 * i)
                            sp.sem_inc(passed, 1)
                        sp.dma_start(wi[u][:, :], S["wi"][bass.ds(b * P, P), :]).then_inc(wi_in[u], 16)

                turns(sp, body)

            @block.gpsimd
            def _(g):
                for u in range(2):
                    g.memset(xg[u][:, :], 0.0).then_inc(zero, 1)
                g.wait_ge(zero, 2)

                def gather(i, u):
                    g.wait_ge(idx_in[u], 16 * (i + 1))
                    g.sem_inc(passed, 1)
                    g.indirect_dma_start(out=xg[u][:, :], out_offset=None, in_=S["xn"], in_offset=bass.IndirectOffsetOnAxis(ap=idx[u][:, 0:1], axis=0),
                                         bounds_check=LAT - 1, oob_is_err=False).then_inc(got[u], 16)

                def weights(i, u, first):
                    b = 2 * i + u
                    g.wait_ge(wi_in[u], 16 * (i + 1))
                    for t, dst, used in (("gate", wg, gu_mm), ("up", wu, gu_mm), ("down", wd, d_mm)):
                        if not first and t != "up":
                            g.wait_ge(used, b - 1)
                        g.sem_inc(passed, 1)
                        g.indirect_dma_start(out=flat(dst[:, u]), out_offset=None, in_=by_rows(A[f"moe_w_{t}_2"]), in_offset=bass.IndirectOffsetOnAxis(ap=wi[u][:, :], axis=0),
                                             bounds_check=NE * P - 1, oob_is_err=False).then_inc(w_in[u], 16)

                def scatter(i, u):
                    b = 2 * i + u
                    g.wait_ge(y_a, b + 1)
                    g.wait_ge(y_v, b + 1)
                    g.sem_inc(passed, 1)
                    g.indirect_dma_start(out=S["Y"], out_offset=bass.IndirectOffsetOnAxis(ap=sidx[u][:, :], axis=0), in_=y[u][:, :], in_offset=None,
                                         bounds_check=2 * LAT - 1, oob_is_err=False).then_inc(put[u], 16)

                def body(i, first, last):
                    for u in range(2):
                        b = 2 * i + u
                        if not first:
                            g.wait_ge(turned, 2 * (b - 1))
                        gather(i, u)
                        weights(i, u, first)
                        if not first:
                            scatter(i - 1, u)
                    if last:
                        scatter(i, 0)
                        scatter(i, 1)

                turns(g, body)
                for u in range(2):
                    g.wait_ge(put[u], 16 * TURNS)

            @block.tensor
            def _(pe):
                def turn(i, u, first):
                    b = 2 * i + u
                    pe.wait_ge(got[u], 16 * (i + 1))
                    for q in range(2):
                        if not (first and u == 0):
                            pe.wait_ge(ev_a if q == 0 else ev_v, b)
                        for k in range(4):
                            mm = pe.transpose(pt[:, q, k], xg[u][:, :].rearrange("t (c k) -> t k c", k=KD)[:, 4 * q + k], C["ident"])
                        mm.then_inc(turned, 1)

                def body(i, first, last):
                    for u in range(2):
                        b = 2 * i + u
                        pe.wait_ge(w_in[u], 48 * (i + 1))
                        pe.wait_ge(ev_a, b + 1)
                        pe.wait_ge(ev_v, b + 1)
                        if not first:
                            pe.wait_ge(h_done, b - 1)
                        for w, m in enumerate((wg, wu)):
                            for n in range(HT):
                                for k in range(KD):
                                    mm = pe.matmul(gu[:, u, w, n * P:(n + 1) * P], m[:, u, k].rearrange("p (c n) -> p n c", n=HT)[:, n], xT[:, u, k], start=(k == 0), stop=(k == KD - 1))
                        mm.then_inc(gu_mm, 1)
                        if u == 0:
                            turn(i, 1, first)
                        elif not last:
                            turn(i + 1, 0, False)
                        pe.wait_ge(h_done, b + 1)
                        if not first:
                            pe.wait_ge(y_a, b - 1)
                            pe.wait_ge(y_v, b - 1)
                        for n in range(2):
                            for k in range(HT):
                                mm = pe.matmul(acc[:, u, n], hh[:, u, k], wd[:, u, k, n * HALF:(n + 1) * HALF], start=(k == 0), stop=(k == HT - 1))
                        mm.then_inc(d_mm, 1)

                turn(0, 0, True)
                turns(pe, body)

            @block.scalar
            def _(act):
                act.wait_ge(c_in, 16)

                def rows(i, u, first):
                    b = 2 * i + u
                    act.wait_ge(turned, 2 * b + 1)
                    if not first:
                        act.wait_ge(gu_mm, b - 1)
                    for k in range(4):
                        e = act.activation(xT[:, u, k], pt[:, 0, k], ACT.Copy, scale=nw[:, k:k + 1])
                    e.then_inc(ev_a, 1)

                def body(i, first, last):
                    for u in range(2):
                        b = 2 * i + u
                        act.wait_ge(gu_mm, b + 1)
                        if not first:
                            act.wait_ge(h_done, b - 1)
                        act.activation(th[:, u], gu[:, u, 0], ACT.Tanh, scale=0.5).then_inc(th_done, 1)
                        if u == 0:
                            rows(i, 1, first)
                        elif not last:
                            rows(i + 1, 0, False)
                        act.wait_ge(d_mm, b + 1)
                        if not first:
                            act.wait_ge(put[u], 16 * i)
                        act.copy(y[u][:, 0:HALF], acc[:, u, 0]).then_inc(y_a, 1)

                rows(0, 0, True)
                turns(act, body)

            @block.vector
            def _(v):
                v.wait_ge(c_in, 16)

                def rows(i, u, first):
                    b = 2 * i + u
                    v.wait_ge(turned, 2 * b + 2)
                    if not first:
                        v.wait_ge(gu_mm, b - 1)
                    for k in range(4, KD):
                        e = v.tensor_scalar(xT[:, u, k], pt[:, 1, k - 4], nw[:, k:k + 1], None, ALU.mult)
                    e.then_inc(ev_v, 1)

                def body(i, first, last):
                    for u in range(2):
                        b = 2 * i + u
                        v.wait_ge(idx_in[u], 16 * (i + 1))
                        if not first:
                            v.wait_ge(put[u], 16 * i)
                        v.tensor_copy(sidx[u][:, :], idx[u][:, 1:2]).then_inc(sidx_done, 1)
                        v.wait_ge(th_done, b + 1)
                        if not first:
                            v.wait_ge(d_mm, b - 1)
                        v.scalar_tensor_tensor(out=sg[:, u], in0=th[:, u], scalar=1.0, in1=gu[:, u, 0], op0=ALU.add, op1=ALU.mult).then_inc(sg_done, 1)
                        v.wait_ge(sg_done, b + 1)
                        v.scalar_tensor_tensor(out=hh[:, u].rearrange("p k t -> p (k t)"), in0=sg[:, u], scalar=0.5, in1=gu[:, u, 1], op0=ALU.mult, op1=ALU.mult).then_inc(h_done, 1)
                        if u == 0:
                            rows(i, 1, first)
                        elif not last:
                            rows(i + 1, 0, False)
                        v.wait_ge(d_mm, b + 1)
                        v.tensor_copy(y[u][:, HALF:D], acc[:, u, 1]).then_inc(y_v, 1)

                rows(0, 0, True)
                turns(v, body)


def combine(nc, C, A, S, wts, out):
    with Phase(nc, "comb") as f:
        Y, r = f.sb("Y", [P, 2, 2, D]), f.sb("r", [P, 2, D])
        a, o = f.sb("a", [P, 2, D]), f.sb("o", [P, 2, D])
        y_in, mid, done, stored = f.sem2("y_in"), f.sem("mid"), f.sem("done"), f.sem2("stored")
        with nc.Block() as block:
            @block.sync
            def _(sp):
                for i in range(LT):
                    if i >= 2:
                        sp.wait_ge(done, i - 1)
                    sp.dma_start(Y[:, i % 2], S["Y"][2 * i * P:2 * (i + 1) * P, :].rearrange("(p k) n -> p k n", k=2)).then_inc(y_in[i % 2], 16)
                    sp.dma_start(r[:, i % 2], S["x3"][i * P:(i + 1) * P, :]).then_inc(y_in[i % 2], 16)

            @block.vector
            def _(v):
                for i in range(LT):
                    v.wait_ge(y_in[i % 2], 32 * (i // 2 + 1))
                    v.scalar_tensor_tensor(out=a[:, i % 2], in0=Y[:, i % 2, 0], scalar=wts[:, i, 0:1], in1=r[:, i % 2], op0=ALU.mult, op1=ALU.add).then_inc(mid, 1)
                    v.wait_ge(mid, i + 1)
                    if i >= 2:
                        v.wait_ge(stored[i % 2], 16 * (i // 2))
                    v.scalar_tensor_tensor(out=o[:, i % 2], in0=Y[:, i % 2, 1], scalar=wts[:, i, 1:2], in1=a[:, i % 2], op0=ALU.mult, op1=ALU.add).then_inc(done, 1)

            @block.gpsimd
            def _(g):
                for i in range(LT):
                    g.wait_ge(done, i + 1)
                    g.dma_start(out[i * P:(i + 1) * P, :], o[:, i % 2]).then_inc(stored[i % 2], 16)
                for b in range(2):
                    g.wait_ge(stored[b], 16 * (LT // 2))


def moe_layer(nc, C, A, S, out):
    with ExitStack() as c1:
        wts = c1.enter_context(nc.sbuf_tensor("wts", [P, LT, 2], F32))
        with ExitStack() as c2:
            hT = c2.enter_context(nc.sbuf_tensor("h5T", [P, KD, LAT], F32))
            norm_turn(nc, "n5", C, [(S["x3"][i * P:(i + 1) * P, :], 0, i * P) for i in range(LT)], [(A["norm_ffn_2"][0], None, None)], hT, keep=S["xn"])
            route(nc, C, A, S, hT, wts)
        experts(nc, C, A, S)
        combine(nc, C, A, S, wts, out)


def first_layer(nc, C, A, S):
    m = lambda c, l, j: S["mod"][c, l, j * D:(j + 1) * D]
    rows = [A["ctx"][0, i * P:(i + 1) * P, :] if i < CT else A["x"][0, (i - CT) * P:(i - CT + 1) * P, :] for i in range(TT)]
    with nc.sbuf_tensor("h0T", [P, KD, T], F32) as hT:
        norm_turn(nc, "n0", C, [(rows[i], 0 if i < CT else 1, i * P) for i in range(TT)],
                  [(A["norm_w"][0], m(1, 0, 1), m(1, 0, 0)), (A["norm_w"][0], m(0, 0, 1), m(0, 0, 0))], hT)
        mamba_layer(nc, C, A, S, hT)
    out_project(nc, "m_out", C, [S["my"][i * P:(i + 1) * P, :] for i in range(TT)], A["m_out_w"][0],
                [(i, rows[i], m(1 if i < CT else 0, 0, 2)) for i in range(TT)], S["h1"], norm_w=A["m_norm_w"][0])


def second_layer(nc, C, A, S):
    m = lambda c, l, j: S["mod"][c, l, j * D:(j + 1) * D]
    with nc.sbuf_tensor("h1T", [P, KD, T], F32) as hT:
        norm_turn(nc, "n1", C, [(S["h1"][i * P:(i + 1) * P, :], 0 if i < CT else 1, i * P) for i in range(TT)],
                  [(A["norm_w"][1], m(1, 1, 1), m(1, 1, 0)), (A["norm_w"][1], m(0, 1, 1), m(0, 1, 0))], hT)
        attention_layer(nc, C, A, S, hT)


SCRATCH = {
    "mod": (2, 2, 3 * D), "my": (T, DI), "h1": (T, D), "ag": (LAT, D), "aoT": (D, LAT), "h2": (LAT, D),
    "x1": (LAT, D), "pa": (LAT, 352), "hfT": (1536, LAT), "hih": (LAT, D), "ho": (LAT, D // 2), "mixT": (D, LAT),
    "x2": (LAT, D), "xoT": (D, LAT), "x3": (LAT, D), "xn": (LAT, D), "Y": (2 * LAT, D),
}


def program(nc, A, out, offsets):
    S = {k: nc.dram_tensor("scratch_" + k, s, F32).ap() for k, s in SCRATCH.items()}
    S["idx"] = nc.dram_tensor("scratch_idx", (NBLK * P, 2), U32).ap()
    S["wi"] = nc.dram_tensor("scratch_wi", (NBLK * P, 1), U32).ap()
    with ExitStack() as ctx:
        C = load_constants(nc, ctx, A, offsets)
        modulation(nc, A, S)
        first_layer(nc, C, A, S)
        second_layer(nc, C, A, S)
        mixer_layer(nc, C, A, S)
        cross_layer(nc, C, A, S)
        moe_layer(nc, C, A, S, out[0])


_INS = ['x', 'c', 'ctx', 'c_ctx', 'norm_w', 'mod_w', 'mod_b', 'final_norm_w', 'm_in_w', 'm_conv_w', 'm_conv_b', 'm_a_log',
        'm_dt_bias', 'm_d', 'm_norm_w', 'm_out_w', 'a_in_w', 'a_q_norm', 'a_k_norm', 'a_out_w',
        'mem_2', 'positions_2', 'norm_mix_2', 'w_in_2', 'mla_q_a_norm_2', 'mla_w_q_up_2', 'mla_kv_a_norm_2',
        'mla_w_kv_up_2', 'mla_q_norm_2', 'mla_k_norm_2', 'hg_lb_logits_2', 'hg_o_norm_2', 'w_out_2',
        'norm_cross_2', 'norm_mem_2', 'x_w_q_2', 'x_w_kv_2', 'x_q_norm_2', 'x_k_norm_2', 'x_w_o_2', 'norm_ffn_2',
        'moe_w_group_2', 'moe_b_group_2', 'moe_w_expert_2', 'moe_b_expert_2', 'moe_w_gate_2', 'moe_w_up_2', 'moe_w_down_2']
_OUTS = [((1, LAT, D), 'float32')]


def kernel(**inputs):
    import numpy as _np
    import concourse.bacc as _bacc
    from concourse import mybir as _mybir
    from concourse.bass_utils import run_bass_kernel_spmd as _run

    nc = _bacc.Bacc("TRN2", target_bir_lowering=False, num_devices=1)
    constants, levels, offsets = shape_constants()
    given = {name: _np.ascontiguousarray(inputs[name]) for name in _INS}
    given["constants"], given["levels"] = constants, levels
    arrays, A = {}, {}
    for name, a in given.items():
        arrays[f"in_{name}_dram"] = a
        A[name] = nc.dram_tensor(f"in_{name}_dram", a.shape, _mybir.dt.from_np(a.dtype), kind="ExternalInput").ap()
    outs = [nc.dram_tensor(f"out_{i}_dram", s, _mybir.dt.from_np(_np.dtype(t)), kind="ExternalOutput").ap() for i, (s, t) in enumerate(_OUTS)]
    program(nc, A, outs[0], offsets)
    r = _run(nc, [arrays], core_ids=[0])
    return r.results[0]["out_0_dram"]
```
